# Optimizing a Trainium2 kernel written in Bass

```python
import math
import jax
import jax.numpy as jnp
from jax import lax
import numpy as np
import jax, jax.numpy as jnp

D_MODEL = 1024
BATCH = 1
SEQ = 1024
DEPTH = 1

GRID_W = 64
CTX_LEN = 256
D_SSD = D_MODEL
SSD_HEADDIM = 64
SSD_HEADS = D_SSD // SSD_HEADDIM
SSD_GROUPS = 4
SSD_HEADS_PER_GROUP = SSD_HEADS // SSD_GROUPS
SSD_STATE = 128
CONV_W = 5
CHUNK = 128
CONV_DIM = D_SSD + 2 * SSD_GROUPS * SSD_STATE
D_FOURIER = D_MODEL // 2
FOURIER_GROUPS = 4
FOURIER_CH = D_FOURIER // FOURIER_GROUPS
D_MIX = D_SSD + D_FOURIER
D_PROJ = D_SSD + CONV_DIM + 2 * SSD_HEADS + D_FOURIER
N_EXPERT_GROUPS = 4
EXPERTS_PER_GROUP = 8
N_EXPERTS = N_EXPERT_GROUPS * EXPERTS_PER_GROUP
TOP_K_INNER = 2
D_EXPERT = D_MODEL // 2
EXPERT_BLOCK = 128
EPS = 1e-6


def rmsnorm(u, w):
    uf = u.astype(jnp.float32)
    uf = uf * lax.rsqrt(jnp.mean(uf * uf, axis=-1, keepdims=True) + EPS)
    return uf.astype(u.dtype) * w

def modulate(u, shift, scale):
    return u * (1 + scale) + shift

def depthwise_conv(u, w):
    return lax.conv_general_dilated(u, w[:, None, :], window_strides=(1,), padding='SAME',
                                    dimension_numbers=('NWC', 'WIO', 'NWC'),
                                    feature_group_count=u.shape[-1])

def ssd_scan(xd, da, bm, cm, h0):
    out_dtype = xd.dtype
    b, l = xd.shape[0], xd.shape[1]
    nc = l // CHUNK
    g, r, p, n = SSD_GROUPS, SSD_HEADS_PER_GROUP, SSD_HEADDIM, SSD_STATE
    f32 = jnp.float32
    xd = xd.astype(f32).reshape(b, nc, CHUNK, g, r, p)
    da = da.astype(f32).reshape(b, nc, CHUNK, g, r)
    bm = bm.astype(f32).reshape(b, nc, CHUNK, g, n)
    cm = cm.astype(f32).reshape(b, nc, CHUNK, g, n)
    a_cs = jnp.cumsum(da, axis=2)
    a_lr = jnp.moveaxis(a_cs, 2, -1)
    lower = jnp.tril(jnp.ones((CHUNK, CHUNK), bool))
    seg = jnp.where(lower, a_lr[..., :, None] - a_lr[..., None, :], -jnp.inf)
    cb = jnp.einsum('bclgn,bcsgn->bcgls', cm, bm)
    y_diag = jnp.einsum('bcgrls,bcsgrp->bclgrp', cb[:, :, :, None] * jnp.exp(seg), xd)
    decay_to_end = jnp.exp(a_cs[:, :, -1:] - a_cs)
    chunk_states = jnp.einsum('bcqgn,bcqgrp->bcgrpn', bm, xd * decay_to_end[..., None])
    chunk_decay = jnp.exp(a_cs[:, :, -1])

    def carry_state(h, inp):
        dec, st = inp
        return h * dec[..., None, None] + st, h

    h_final, h_in = lax.scan(carry_state, h0.astype(f32),
                             (jnp.moveaxis(chunk_decay, 1, 0), jnp.moveaxis(chunk_states, 1, 0)))
    h_in = jnp.moveaxis(h_in, 0, 1)
    y_off = jnp.einsum('bcqgn,bcgrpn->bcqgrp', cm, h_in) * jnp.exp(a_cs)[..., None]
    y = (y_diag + y_off).reshape(b, l, SSD_HEADS, p)
    return y.astype(out_dtype), h_final

def ssd_mixer(z, xbc, dt_raw, h0_f, h0_b, conv_w, conv_b, dt_bias, a_log, d_skip, norm_w):
    b, l = xbc.shape[0], xbc.shape[1]
    xbc = jax.nn.silu(depthwise_conv(xbc, conv_w) + conv_b)
    xs, bm, cm = jnp.split(xbc, [D_SSD, D_SSD + SSD_GROUPS * SSD_STATE], axis=-1)
    xs = xs.reshape(b, l, SSD_HEADS, SSD_HEADDIM)
    bm = bm.reshape(b, l, SSD_GROUPS, SSD_STATE)
    cm = cm.reshape(b, l, SSD_GROUPS, SSD_STATE)
    dt = jax.nn.softplus(dt_raw.reshape(b, l, 2, SSD_HEADS) + dt_bias)
    da = dt * -jnp.exp(a_log)
    flip = lambda u: jnp.flip(u, axis=1)
    y_f, h_f = ssd_scan(xs * dt[:, :, 0, :, None], da[:, :, 0], bm, cm, h0_f)
    y_b, h_b = ssd_scan(flip(xs * dt[:, :, 1, :, None]), flip(da[:, :, 1]), flip(bm), flip(cm), h0_b)
    y = y_f + flip(y_b) + d_skip[:, None] * xs
    y = y.reshape(b, l, D_SSD) * jax.nn.silu(z)
    return rmsnorm(y, norm_w), h_f, h_b

def fourier_mixer(f, w_four):
    b, l = f.shape[0], f.shape[1]
    fg = f.reshape(b, l, FOURIER_GROUPS, FOURIER_CH).astype(jnp.float32)
    spec = jnp.fft.fft2(fg, axes=(1, 3), norm='ortho').real.astype(f.dtype)
    return jnp.einsum('blgc,gcd->blgd', spec, w_four).reshape(b, l, D_FOURIER)

def split_proj(proj):
    return jnp.split(proj, [D_SSD, D_SSD + CONV_DIM, D_SSD + CONV_DIM + 2 * SSD_HEADS], axis=-1)

def hier_moe(h, w_rg, b_rg, w_re, b_re, w_eg, w_eu, w_ed):
    bsz, l, d = h.shape
    t = h.reshape(bsz * l, d)
    n_tok = t.shape[0]
    f32 = jnp.float32
    p_grp = jax.nn.softmax((t @ w_rg + b_rg).astype(f32), axis=-1)
    p_top_grp, grp = lax.top_k(p_grp, 1)
    logit_exp = jnp.einsum('td,gde->tge', t, w_re) + b_re
    sel = jnp.broadcast_to(grp[:, :, None], (n_tok, 1, EXPERTS_PER_GROUP))
    logit_sel = jnp.take_along_axis(logit_exp, sel, axis=1)[:, 0]
    p_exp = jax.nn.softmax(logit_sel.astype(f32), axis=-1)
    p_top, j_top = lax.top_k(p_exp, TOP_K_INNER)
    gate = p_top_grp * p_top / jnp.sum(p_top, axis=-1, keepdims=True)
    eid = grp * EXPERTS_PER_GROUP + j_top
    n_assign = n_tok * TOP_K_INNER
    e_flat = eid.reshape(-1)
    g_flat = gate.reshape(-1)
    tok_flat = jnp.repeat(jnp.arange(n_tok, dtype=jnp.int32), TOP_K_INNER)
    order = jnp.argsort(e_flat)
    e_s, tok_s, g_s = e_flat[order], tok_flat[order], g_flat[order]
    counts = jnp.bincount(e_flat, length=N_EXPERTS)
    padded = (counts + EXPERT_BLOCK - 1) // EXPERT_BLOCK * EXPERT_BLOCK
    start = jnp.cumsum(counts) - counts
    end_pad = jnp.cumsum(padded)
    start_pad = end_pad - padded
    dest = start_pad[e_s] + jnp.arange(n_assign, dtype=jnp.int32) - start[e_s]
    n_blocks = -(-(n_assign + N_EXPERTS * (EXPERT_BLOCK - 1)) // EXPERT_BLOCK)
    n_rows = n_blocks * EXPERT_BLOCK
    row_tok = jnp.full((n_rows,), n_tok, jnp.int32).at[dest].set(tok_s)
    row_gate = jnp.zeros((n_rows,), f32).at[dest].set(g_s)
    blk_exp = jnp.minimum(jnp.searchsorted(end_pad, jnp.arange(n_blocks) * EXPERT_BLOCK, side='right'),
                          N_EXPERTS - 1)
    t_pad = jnp.concatenate([t, jnp.zeros((1, d), t.dtype)], axis=0)
    rows = t_pad[row_tok].reshape(n_blocks, EXPERT_BLOCK, d)

    def expert_block(args):
        xb, e = args
        return (jax.nn.silu(xb @ w_eg[e]) * (xb @ w_eu[e])) @ w_ed[e]

    y_rows = lax.map(expert_block, (rows, blk_exp)).reshape(n_rows, d)
    y = jax.ops.segment_sum(y_rows.astype(f32) * row_gate[:, None], row_tok,
                            num_segments=n_tok + 1)[:n_tok]
    return y.astype(h.dtype).reshape(bsz, l, d)

def first_inputs(seed: int = 0) -> dict:
    key = jax.random.key(seed)
    ks = jax.random.split(key, 26)
    f32 = jnp.float32

    def nrm(k, shape, scale):
        return jax.random.normal(k, shape, f32) * scale

    def gain(k, shape):
        return 1.0 + 0.05 * jax.random.normal(k, shape, f32)

    dt0 = jnp.exp(jax.random.uniform(ks[10], (DEPTH, 2, SSD_HEADS), f32,
                                     math.log(1e-3), math.log(1e-1)))
    dt_bias = dt0 + jnp.log(-jnp.expm1(-dt0))
    a_log = jnp.log(jax.random.uniform(ks[11], (DEPTH, 2, SSD_HEADS), f32, 1.0, 16.0))
    return {
        'x': nrm(ks[0], (BATCH, SEQ, D_MODEL), 1.0),
        'c': nrm(ks[1], (BATCH, D_MODEL), 1.0),
        'ctx': nrm(ks[2], (BATCH, CTX_LEN, D_MODEL), 1.0),
        'c_ctx': nrm(ks[3], (D_MODEL,), 1.0),
        'w_mod': nrm(ks[4], (DEPTH, D_MODEL, 6 * D_MODEL), D_MODEL ** -0.5),
        'b_mod': nrm(ks[5], (DEPTH, 6 * D_MODEL), 0.02),
        'norm1': gain(ks[6], (DEPTH, D_MODEL)),
        'w_in': nrm(ks[7], (DEPTH, D_MODEL, D_PROJ), D_MODEL ** -0.5),
        'conv_w': nrm(ks[8], (DEPTH, CONV_W, CONV_DIM), CONV_W ** -0.5),
        'conv_b': nrm(ks[9], (DEPTH, CONV_DIM), 0.02),
        'dt_bias': dt_bias,
        'a_log': a_log,
        'd_skip': gain(ks[12], (DEPTH, SSD_HEADS)),
        'ssd_norm': gain(ks[13], (DEPTH, D_SSD)),
        'w_four': nrm(ks[14], (DEPTH, FOURIER_GROUPS, FOURIER_CH, FOURIER_CH), FOURIER_CH ** -0.5),
        'w_out': nrm(ks[15], (DEPTH, D_MIX, D_MODEL), D_MIX ** -0.5),
        'norm2': gain(ks[16], (DEPTH, D_MODEL)),
        'w_rg': nrm(ks[17], (DEPTH, D_MODEL, N_EXPERT_GROUPS), D_MODEL ** -0.5),
        'b_rg': nrm(ks[18], (DEPTH, N_EXPERT_GROUPS), 0.01),
        'w_re': nrm(ks[19], (DEPTH, N_EXPERT_GROUPS, D_MODEL, EXPERTS_PER_GROUP), D_MODEL ** -0.5),
        'b_re': nrm(ks[20], (DEPTH, N_EXPERT_GROUPS, EXPERTS_PER_GROUP), 0.01),
        'w_eg': nrm(ks[21], (DEPTH, N_EXPERTS, D_MODEL, D_EXPERT), D_MODEL ** -0.5),
        'w_eu': nrm(ks[22], (DEPTH, N_EXPERTS, D_MODEL, D_EXPERT), D_MODEL ** -0.5),
        'w_ed': nrm(ks[23], (DEPTH, N_EXPERTS, D_EXPERT, D_MODEL), D_EXPERT ** -0.5),
        'final_norm': gain(ks[24], (D_MODEL,)),
    }

def first_block(x, c, ctx, c_ctx, w_mod, b_mod, norm1, w_in, conv_w, conv_b, dt_bias, a_log,
              d_skip, ssd_norm, w_four, w_out, norm2, w_rg, b_rg, w_re, b_re, w_eg, w_eu, w_ed,
              final_norm):
    n_lat = x.shape[1]
    rows = n_lat // GRID_W
    assert rows * GRID_W == n_lat
    bsz = x.shape[0]
    h_zero = jnp.zeros((bsz, SSD_GROUPS, SSD_HEADS_PER_GROUP, SSD_HEADDIM, SSD_STATE), jnp.float32)
    for layer in range(DEPTH):
        last = layer == DEPTH - 1
        mod_lat = jax.nn.silu(c) @ w_mod[layer] + b_mod[layer]
        mod_ctx = jax.nn.silu(c_ctx) @ w_mod[layer] + b_mod[layer]
        sh1, sc1, g1, sh2, sc2, g2 = jnp.split(mod_lat[:, None, :], 6, axis=-1)
        sh1c, sc1c, g1c, sh2c, sc2c, g2c = jnp.split(mod_ctx, 6, axis=-1)
        prj_c = modulate(rmsnorm(ctx, norm1[layer]), sh1c, sc1c) @ w_in[layer]
        prj_l = modulate(rmsnorm(x, norm1[layer]), sh1, sc1) @ w_in[layer]
        z_c, xbc_c, dt_c, f_c = split_proj(prj_c)
        z_l, xbc_l, dt_l, f_l = split_proj(prj_l)
        y_c, hf_c, hb_c = ssd_mixer(z_c, xbc_c, dt_c, h_zero, h_zero, conv_w[layer], conv_b[layer],
                                    dt_bias[layer], a_log[layer], d_skip[layer], ssd_norm[layer])
        y_l, _, _ = ssd_mixer(z_l, xbc_l, dt_l, hf_c, hb_c, conv_w[layer], conv_b[layer],
                              dt_bias[layer], a_log[layer], d_skip[layer], ssd_norm[layer])
        mix_l = jnp.concatenate([y_l, fourier_mixer(f_l, w_four[layer])], axis=-1) @ w_out[layer]
        x = x + g1 * mix_l
        if not last:
            mix_c = jnp.concatenate([y_c, fourier_mixer(f_c, w_four[layer])], axis=-1) @ w_out[layer]
            ctx = ctx + g1c * mix_c
            ctx = ctx + g2c * hier_moe(modulate(rmsnorm(ctx, norm2[layer]), sh2c, sc2c), w_rg[layer],
                                       b_rg[layer], w_re[layer], b_re[layer], w_eg[layer],
                                       w_eu[layer], w_ed[layer])
        x = x + g2 * hier_moe(modulate(rmsnorm(x, norm2[layer]), sh2, sc2), w_rg[layer], b_rg[layer],
                              w_re[layer], b_re[layer], w_eg[layer], w_eu[layer], w_ed[layer])
    return rmsnorm(x, final_norm)


SSM_WIDTH = D_MODEL // 2
SSM_GROUP_CH = 16
SSM_GROUPS = SSM_WIDTH // SSM_GROUP_CH
SSM_STATE = 64
SGU_WIDTH = D_MODEL // 2
SGU_HEADS = 8
SGU_HEAD_DIM = SGU_WIDTH // SGU_HEADS
SGU_CHUNK = 128
IN_WIDTH = SSM_WIDTH + 2 * SGU_WIDTH
N_GROUPS = 4
N_EXPERTS_2 = N_GROUPS * EXPERTS_PER_GROUP
TOP_K = 2
D_FF_EXPERT = D_MODEL // 2
RMS_EPS = 1e-6
LN_EPS = 1e-5


def rmsnorm_2(x, g):
    xf = x.astype(jnp.float32)
    y = xf * lax.rsqrt(jnp.mean(xf * xf, axis=-1, keepdims=True) + RMS_EPS)
    return (y * g.astype(jnp.float32)).astype(x.dtype)

def layernorm(x, g, b):
    xf = x.astype(jnp.float32)
    mu = jnp.mean(xf, axis=-1, keepdims=True)
    var = jnp.mean(jnp.square(xf - mu), axis=-1, keepdims=True)
    y = (xf - mu) * lax.rsqrt(var + LN_EPS) * g.astype(jnp.float32) + b.astype(jnp.float32)
    return y.astype(x.dtype)

def modulate_2(x, shift, scale):
    return x * (1.0 + scale[:, None, :]) + shift[:, None, :]

def s5_branch(u, a_re, a_im, b_re, b_im, c_re, c_im, d_skip, log_step, w_glu, b_glu):
    f32 = jnp.float32
    bq, sq, _ = u.shape
    uf = u.astype(f32).reshape(bq, sq, SSM_GROUPS, SSM_GROUP_CH)
    lam_re = jnp.minimum(a_re.astype(f32), -1e-4)
    lam_im = a_im.astype(f32)
    dt = jnp.exp(log_step.astype(f32))[:, None]
    mag = jnp.exp(lam_re * dt)
    ab_re = mag * jnp.cos(lam_im * dt)
    ab_im = mag * jnp.sin(lam_im * dt)
    den = lam_re * lam_re + lam_im * lam_im
    nr = ab_re - 1.0
    f_re = (nr * lam_re + ab_im * lam_im) / den
    f_im = (ab_im * lam_re - nr * lam_im) / den
    bu_re = jnp.einsum('bsgh,gnh->bsgn', uf, b_re.astype(f32))
    bu_im = jnp.einsum('bsgh,gnh->bsgn', uf, b_im.astype(f32))
    x_re = f_re * bu_re - f_im * bu_im
    x_im = f_re * bu_im + f_im * bu_re
    a_r = jnp.broadcast_to(ab_re[None, None], (1, sq, SSM_GROUPS, SSM_STATE))
    a_i = jnp.broadcast_to(ab_im[None, None], (1, sq, SSM_GROUPS, SSM_STATE))

    def combine(e1, e2):
        ar1, ai1, br1, bi1 = e1
        ar2, ai2, br2, bi2 = e2
        ar = ar2 * ar1 - ai2 * ai1
        ai = ar2 * ai1 + ai2 * ar1
        br = ar2 * br1 - ai2 * bi1 + br2
        bi = ar2 * bi1 + ai2 * br1 + bi2
        return (ar, ai, br, bi)

    _, _, h_re, h_im = lax.associative_scan(combine, (a_r, a_i, x_re, x_im), axis=1)
    y = (jnp.einsum('bsgn,ghn->bsgh', h_re, c_re.astype(f32))
         - jnp.einsum('bsgn,ghn->bsgh', h_im, c_im.astype(f32))
         + d_skip.astype(f32) * uf)
    y = jax.nn.gelu(y.reshape(bq, sq, SSM_WIDTH))
    y = y * jax.nn.sigmoid(y @ w_glu.astype(f32) + b_glu.astype(f32))
    return y.astype(u.dtype)

def sgu_branch(z_u, z_v, ln_g, ln_b, w_s, b_s):
    bq, sq, _ = z_u.shape
    u = jax.nn.gelu(z_u)
    v = layernorm(jax.nn.gelu(z_v), ln_g, ln_b)
    n_chunks = sq // SGU_CHUNK
    vh = v.reshape(bq, n_chunks, SGU_CHUNK, SGU_HEADS, SGU_HEAD_DIM)
    causal = jnp.tril(jnp.ones((SGU_CHUNK, SGU_CHUNK), w_s.dtype))
    ws = w_s * causal[None]
    mixed = jnp.einsum('hts,bcshd->bcthd', ws, vh) + b_s.T[None, None, :, :, None]
    return u * mixed.reshape(bq, sq, SGU_WIDTH)

def hierarchical_moe(xn, w_rg, b_rg, w_re, b_re, w1, w3, w2):
    f32 = jnp.float32
    bq, sq, dm = xn.shape
    n_tok = bq * sq
    xt = xn.reshape(n_tok, dm)
    lg = (xt @ w_rg + b_rg).astype(f32)
    pg = jax.nn.softmax(lg, axis=-1)
    grp = jnp.argmax(lg, axis=-1).astype(jnp.int32)
    pg_sel = jnp.take_along_axis(pg, grp[:, None], axis=1)[:, 0]
    le_all = (jnp.einsum('td,gde->tge', xt, w_re) + b_re[None]).astype(f32)
    le = jnp.take_along_axis(le_all, grp[:, None, None], axis=1)[:, 0]
    top_v, top_i = lax.top_k(le, TOP_K)
    pe = jax.nn.softmax(top_v, axis=-1)
    eid = grp[:, None] * EXPERTS_PER_GROUP + top_i.astype(jnp.int32)
    wgt = pg_sel[:, None] * pe

    n_asg = n_tok * TOP_K
    e_flat = eid.reshape(n_asg)
    w_flat = wgt.reshape(n_asg)
    tok_flat = jnp.repeat(jnp.arange(n_tok, dtype=jnp.int32), TOP_K)
    order = jnp.argsort(e_flat)
    e_s = e_flat[order]
    tok_s = tok_flat[order]
    w_s = w_flat[order]
    counts = jnp.bincount(e_flat, length=N_EXPERTS_2).astype(jnp.int32)
    padded = (counts + EXPERT_BLOCK - 1) // EXPERT_BLOCK * EXPERT_BLOCK
    starts = jnp.cumsum(counts) - counts
    ends_p = jnp.cumsum(padded)
    pstarts = ends_p - padded
    dest = pstarts[e_s] + (jnp.arange(n_asg, dtype=jnp.int32) - starts[e_s])
    n_buf = n_asg + N_EXPERTS_2 * EXPERT_BLOCK
    n_blocks = n_buf // EXPERT_BLOCK
    buf_tok = jnp.full((n_buf,), n_tok, jnp.int32).at[dest].set(tok_s)
    buf_w = jnp.zeros((n_buf,), f32).at[dest].set(w_s)
    block_start = jnp.arange(n_blocks, dtype=jnp.int32) * EXPERT_BLOCK
    block_e = jnp.clip(jnp.searchsorted(ends_p, block_start, side='right'), 0, N_EXPERTS_2 - 1)
    x_pad = jnp.concatenate([xt, jnp.zeros((1, dm), xt.dtype)], axis=0)
    xb = x_pad[buf_tok].reshape(n_blocks, EXPERT_BLOCK, dm)

    def expert_block(args):
        xblk, e = args
        hid = jax.nn.silu(xblk @ w1[e]) * (xblk @ w3[e])
        return hid @ w2[e]

    yb = lax.map(expert_block, (xb, block_e)).reshape(n_buf, dm)
    y = jnp.zeros((n_tok + 1, dm), yb.dtype).at[buf_tok].add(yb * buf_w[:, None].astype(yb.dtype))
    return y[:n_tok].reshape(bq, sq, dm)

def second_inputs(seed: int = 0) -> dict:
    key = jax.random.key(seed)
    ks = iter(jax.random.split(key, 40))
    f32 = jnp.float32
    L = DEPTH

    def nrm(shape, scale):
        return jax.random.normal(next(ks), shape, f32) * scale

    d_inv = D_MODEL ** -0.5
    x = nrm((BATCH, SEQ, D_MODEL), 1.0)
    c = nrm((BATCH, D_MODEL), 1.0)
    w_ada = nrm((L, D_MODEL, 6 * D_MODEL), 0.2 * d_inv)
    b_ada = nrm((L, 6 * D_MODEL), 0.01)
    norm1_g = 1.0 + nrm((L, D_MODEL), 0.01)
    w_in = nrm((L, D_MODEL, IN_WIDTH), d_inv)
    w_gate = nrm((L, D_MODEL, 2 * D_MODEL), d_inv)
    b_gate = nrm((L, 2 * D_MODEL), 0.01)
    ssm_a_re = -0.5 + nrm((L, SSM_GROUPS, SSM_STATE), 0.01)
    ssm_a_im = jnp.pi * jnp.arange(SSM_STATE, dtype=f32) + nrm((L, SSM_GROUPS, SSM_STATE), 0.01)
    ssm_b_re = nrm((L, SSM_GROUPS, SSM_STATE, SSM_GROUP_CH), (2 * SSM_GROUP_CH) ** -0.5)
    ssm_b_im = nrm((L, SSM_GROUPS, SSM_STATE, SSM_GROUP_CH), (2 * SSM_GROUP_CH) ** -0.5)
    ssm_c_re = nrm((L, SSM_GROUPS, SSM_GROUP_CH, SSM_STATE), 0.5)
    ssm_c_im = nrm((L, SSM_GROUPS, SSM_GROUP_CH, SSM_STATE), 0.5)
    ssm_d = nrm((L, SSM_GROUPS, SSM_GROUP_CH), 1.0)
    ssm_log_step = jax.random.uniform(next(ks), (L, SSM_GROUPS), f32, math.log(1e-3), math.log(1e-1))
    w_glu = nrm((L, SSM_WIDTH, SSM_WIDTH), SSM_WIDTH ** -0.5)
    b_glu = nrm((L, SSM_WIDTH), 0.01)
    sgu_ln_g = 1.0 + nrm((L, SGU_WIDTH), 0.01)
    sgu_ln_b = nrm((L, SGU_WIDTH), 0.01)
    sgu_w = nrm((L, SGU_HEADS, SGU_CHUNK, SGU_CHUNK), SGU_CHUNK ** -0.5)
    sgu_b = 1.0 + nrm((L, SGU_HEADS, SGU_CHUNK), 0.01)
    w_branch_a = nrm((L, SSM_WIDTH, D_MODEL), SSM_WIDTH ** -0.5)
    w_branch_b = nrm((L, SGU_WIDTH, D_MODEL), SGU_WIDTH ** -0.5)
    w_out = nrm((L, D_MODEL, D_MODEL), d_inv)
    norm2_g = 1.0 + nrm((L, D_MODEL), 0.01)
    w_router_group = nrm((L, D_MODEL, N_GROUPS), d_inv)
    b_router_group = nrm((L, N_GROUPS), 0.01)
    w_router_expert = nrm((L, N_GROUPS, D_MODEL, EXPERTS_PER_GROUP), d_inv)
    b_router_expert = nrm((L, N_GROUPS, EXPERTS_PER_GROUP), 0.01)
    w1 = nrm((L, N_EXPERTS_2, D_MODEL, D_FF_EXPERT), d_inv)
    w3 = nrm((L, N_EXPERTS_2, D_MODEL, D_FF_EXPERT), d_inv)
    w2 = nrm((L, N_EXPERTS_2, D_FF_EXPERT, D_MODEL), D_FF_EXPERT ** -0.5)
    norm_f_g = 1.0 + nrm((D_MODEL,), 0.01)
    return {"x": x, "c": c, "w_ada": w_ada, "b_ada": b_ada, "norm1_g": norm1_g,
            "w_in": w_in, "w_gate": w_gate, "b_gate": b_gate,
            "ssm_a_re": ssm_a_re, "ssm_a_im": ssm_a_im, "ssm_b_re": ssm_b_re, "ssm_b_im": ssm_b_im,
            "ssm_c_re": ssm_c_re, "ssm_c_im": ssm_c_im, "ssm_d": ssm_d, "ssm_log_step": ssm_log_step,
            "w_glu": w_glu, "b_glu": b_glu, "sgu_ln_g": sgu_ln_g, "sgu_ln_b": sgu_ln_b,
            "sgu_w": sgu_w, "sgu_b": sgu_b, "w_branch_a": w_branch_a, "w_branch_b": w_branch_b,
            "w_out": w_out, "norm2_g": norm2_g, "w_router_group": w_router_group,
            "b_router_group": b_router_group, "w_router_expert": w_router_expert,
            "b_router_expert": b_router_expert, "w1": w1, "w3": w3, "w2": w2, "norm_f_g": norm_f_g}

def second_block(x, c, w_ada, b_ada, norm1_g, w_in, w_gate, b_gate,
              ssm_a_re, ssm_a_im, ssm_b_re, ssm_b_im, ssm_c_re, ssm_c_im, ssm_d, ssm_log_step,
              w_glu, b_glu, sgu_ln_g, sgu_ln_b, sgu_w, sgu_b, w_branch_a, w_branch_b,
              w_out, norm2_g, w_router_group, b_router_group, w_router_expert,
              b_router_expert, w1, w3, w2, norm_f_g):
    h = x
    c_act = jax.nn.silu(c)
    for l in range(DEPTH):
        mod = c_act @ w_ada[l] + b_ada[l]
        sh1, sc1, gt1, sh2, sc2, gt2 = jnp.split(mod, 6, axis=-1)
        xn = modulate_2(rmsnorm_2(h, norm1_g[l]), sh1, sc1)
        proj = xn @ w_in[l]
        z_a = proj[..., :SSM_WIDTH]
        z_u = proj[..., SSM_WIDTH:SSM_WIDTH + SGU_WIDTH]
        z_v = proj[..., SSM_WIDTH + SGU_WIDTH:]
        y_a = s5_branch(z_a, ssm_a_re[l], ssm_a_im[l], ssm_b_re[l], ssm_b_im[l],
                        ssm_c_re[l], ssm_c_im[l], ssm_d[l], ssm_log_step[l], w_glu[l], b_glu[l])
        y_b = sgu_branch(z_u, z_v, sgu_ln_g[l], sgu_ln_b[l], sgu_w[l], sgu_b[l])
        gates = jax.nn.sigmoid(xn @ w_gate[l] + b_gate[l])
        g_a = gates[..., :D_MODEL]
        g_b = gates[..., D_MODEL:]
        merged = g_a * (y_a @ w_branch_a[l]) + g_b * (y_b @ w_branch_b[l])
        h = h + gt1[:, None, :] * (merged @ w_out[l])
        xn2 = modulate_2(rmsnorm_2(h, norm2_g[l]), sh2, sc2)
        y_m = hierarchical_moe(xn2, w_router_group[l], b_router_group[l], w_router_expert[l],
                               b_router_expert[l], w1[l], w3[l], w2[l])
        h = h + gt2[:, None, :] * y_m
    return rmsnorm_2(h, norm_f_g)


_first_inputs = second_inputs


def second_inputs(seed=0):
    import zlib

    import numpy as np

    out = dict(_first_inputs(seed))
    spreads = {}
    factors = {'b_ada': 8.0,
     'norm1_g': 8.0,
     'b_gate': 8.0,
     'ssm_a_re': 64.0,
     'ssm_a_im': 49.856,
     'ssm_b_re': 64.0,
     'ssm_b_im': 64.0,
     'ssm_c_re': 64.0,
     'ssm_c_im': 64.0,
     'ssm_d': 2.796,
     'ssm_log_step': 50.8,
     'w_glu': 7.06,
     'b_glu': 64.0,
     'sgu_ln_g': 25.841,
     'sgu_ln_b': 8.0,
     'sgu_b': 8.0,
     'norm2_g': 8.0,
     'b_router_group': 8.0,
     'b_router_expert': 8.0,
     'norm_f_g': 31.495}
    for name, (base, spread) in spreads.items():
        noise = np.random.default_rng([zlib.crc32(name.encode()), seed]).standard_normal(out[name].shape)
        drawn = base * np.exp(spread * noise) if base else spread * noise
        out[name] = __import__('jax').numpy.asarray(drawn.astype(out[name].dtype))
    for name, factor in factors.items():
        out[name] = (out[name] * factor).astype(out[name].dtype)
    return out


_narrow_inputs = second_inputs


def second_inputs(seed=0):
    out = dict(_narrow_inputs(seed))
    wider = {'b_glu': 12.0,
     'sgu_ln_g': 3.09,
     'sgu_ln_b': 12.0,
     'sgu_b': 3.13,
     'b_router_group': 4.84,
     'b_router_expert': 3.81,
     'norm_f_g': 6.1}
    for name, times in wider.items():
        mean = out[name].mean()
        out[name] = (mean + times * (out[name] - mean)).astype(out[name].dtype)
    return out


def setup_inputs(seed=0):
    out = dict(first_inputs(seed))
    for name, value in second_inputs(seed + 1).items():
        if name != "x":
            out[name + "_2"] = value
    return out


def reference(
    x, c, ctx, c_ctx, w_mod, b_mod, norm1, w_in, conv_w, conv_b, dt_bias, a_log, d_skip,
    ssd_norm, w_four, w_out, norm2, w_rg, b_rg, w_re, b_re, w_eg, w_eu, w_ed, final_norm, c_2,
    w_ada_2, b_ada_2, norm1_g_2, w_in_2, w_gate_2, b_gate_2, ssm_a_re_2, ssm_a_im_2, ssm_b_re_2,
    ssm_b_im_2, ssm_c_re_2, ssm_c_im_2, ssm_d_2, ssm_log_step_2, w_glu_2, b_glu_2, sgu_ln_g_2,
    sgu_ln_b_2, sgu_w_2, sgu_b_2, w_branch_a_2, w_branch_b_2, w_out_2, norm2_g_2,
    w_router_group_2, b_router_group_2, w_router_expert_2, b_router_expert_2, w1_2, w3_2, w2_2,
    norm_f_g_2,
):
    x = first_block(
        x, c, ctx, c_ctx, w_mod, b_mod, norm1, w_in, conv_w, conv_b, dt_bias, a_log, d_skip,
        ssd_norm, w_four, w_out, norm2, w_rg, b_rg, w_re, b_re, w_eg, w_eu, w_ed, final_norm,
    )
    return second_block(
        x, c_2, w_ada_2, b_ada_2, norm1_g_2, w_in_2, w_gate_2, b_gate_2, ssm_a_re_2, ssm_a_im_2,
        ssm_b_re_2, ssm_b_im_2, ssm_c_re_2, ssm_c_im_2, ssm_d_2, ssm_log_step_2, w_glu_2,
        b_glu_2, sgu_ln_g_2, sgu_ln_b_2, sgu_w_2, sgu_b_2, w_branch_a_2, w_branch_b_2, w_out_2,
        norm2_g_2, w_router_group_2, b_router_group_2, w_router_expert_2, b_router_expert_2,
        w1_2, w3_2, w2_2, norm_f_g_2,
    )


_drawn_inputs = setup_inputs


def setup_inputs(seed=0):
    import zlib

    import numpy as np

    out = dict(_drawn_inputs(seed))
    spreads = {}
    factors = {}
    for name, (base, spread) in spreads.items():
        noise = np.random.default_rng([zlib.crc32(name.encode()), seed]).standard_normal(out[name].shape)
        drawn = base * np.exp(spread * noise) if base else spread * noise
        out[name] = jnp.asarray(drawn.astype(out[name].dtype))
    for name, factor in factors.items():
        out[name] = (out[name] * factor).astype(out[name].dtype)
    return out
```

```python
from contextlib import ExitStack

import concourse.bass as bass
from concourse import mybir

P = 128
D = 1024
SEQ = 1024
T = SEQ // P
J = D // P
N_EXPERTS = 32
NBLK = 2 * SEQ // P + N_EXPERTS
EPS = 1e-6
NEG = -1e30
POOL_DMA_SEMAPHORES = 9

F32 = mybir.dt.float32
F32R = mybir.dt.float32r
I32 = mybir.dt.int32
U32 = mybir.dt.uint32
ALU = mybir.AluOpType
ACT = mybir.ActivationFunctionType
AX = mybir.AxisListType


def bc(ap, n, axis):
    wide = ap.unsqueeze(axis)
    shape = list(wide.shape)
    shape[axis] = n
    return wide.broadcast_to(shape)


def moe_phase(nc, tag, x_in, mod, norm_w, w_rg, b_rg, w_re, b_re, w_gate, w_up, w_down, final_w, x_out, pool_dma):
    xr_dram = nc.dram_tensor(f"{tag}_xr", (SEQ, D), F32, kind="Internal").ap()
    yrows = nc.dram_tensor(f"{tag}_yrows", ((NBLK + 2) * P, D), F32, kind="Internal").ap()
    slot_tok = nc.dram_tensor(f"{tag}_slot_tok", ((NBLK + 2) * P, 1), I32, kind="Internal").ap()
    blk_dram = nc.dram_tensor(f"{tag}_blk", (1, NBLK + 16), I32, kind="Internal").ap()
    x_t = x_in.rearrange("(t p) d -> t p d", p=P)
    out_t = x_out.rearrange("(t p) d -> t p d", p=P)
    xr_t = xr_dram.rearrange("(t p) d -> t p d", p=P)
    NE, NG = w_gate.shape[0], w_re.shape[0]
    EG = NE // NG
    NF = w_gate.shape[2]
    JF = NF // P

    s_zero, s_sc, s_idx, *rest = pool_dma
    s_xb, s_ga = rest[0:2], rest[2:6]
    with ExitStack() as ctx:
        def sb(name, shape, dt=F32):
            return ctx.enter_context(nc.sbuf_tensor(f"{tag}_{name}", shape, dt))

        def sem(name):
            return ctx.enter_context(nc.semaphore(f"{tag}_{name}"))

        X = sb("X", [P, T, D])
        ident = sb("ident", [P, P])
        gate1 = sb("gate1", [P, T])
        gate2 = sb("gate2", [P, T])
        pos1 = sb("pos1", [P, T], I32)
        pos2 = sb("pos2", [P, T], I32)
        ss = sb("ss", [P, T])
        rstd = sb("rstd", [P, T])
        junk = sb("junk", [P, D])

        with ExitStack() as c2:
            def sb2(name, shape, dt=F32):
                return c2.enter_context(nc.sbuf_tensor(f"{tag}_{name}", shape, dt))

            def ps2(name, shape, dt=F32):
                return c2.enter_context(nc.psum_tensor(f"{tag}_{name}", shape, dt))

            xs = sb2("xs", [P, T, D])
            xT = sb2("xT", [P, 2, J, P])
            wr = sb2("wr", [P, J, NG + NE])
            br = sb2("br", [P, NG + NE])
            nrow = sb2("nrow", [P, D])
            srow = sb2("srow", [P, D])
            shrow = sb2("shrow", [P, D])
            SU = sb2("SU", [P, P])
            ones = sb2("ones", [P, P])
            iota_e = sb2("iota_e", [P, NE])
            iota_b = sb2("iota_b", [1, NBLK])
            tokid = sb2("tokid", [P, T], I32)
            zero_i = sb2("zero_i", [P, NBLK + 2], I32)
            L = sb2("L", [P, T, 8 + NE])
            mg = sb2("mg", [P, T, 8])
            ig = sb2("ig", [P, T, 8], U32)
            igf = sb2("igf", [P, T, 8])
            pen = sb2("pen", [P, T, NG])
            LE = sb2("LE", [P, T, NE])
            me = sb2("me", [P, T, 8])
            ie = sb2("ie", [P, T, 8], U32)
            ief = sb2("ief", [P, T, 8])
            dg = sb2("dg", [P, T, NG])
            eg = sb2("eg", [P, T, NG])
            sg = sb2("sg", [P, T])
            de = sb2("de", [P, T])
            e2 = sb2("e2", [P, T])
            den = sb2("den", [P, T])
            M1 = sb2("M1", [P, T, NE])
            M2 = sb2("M2", [P, T, NE])
            M = sb2("M", [P, T, NE])
            Tc = sb2("Tc", [P, T, NE])
            cnt = sb2("cnt", [P, NE])
            nb = sb2("nb", [P, NE])
            onese = sb2("onese", [P, NE])
            bend = sb2("bend", [P, NE])
            bst = sb2("bst", [P, NE])
            slot = sb2("slot", [P, T, NE])
            pr = sb2("pr", [P, T, NE])
            posf = sb2("posf", [P, T])
            cb = sb2("cb", [1, NBLK, NE])
            bef = sb2("bef", [1, NBLK + 16])
            bei = sb2("bei", [1, NBLK + 16], I32)
            ps_t = ps2("ps_t", [P, 2, J, P])
            ps_l = ps2("ps_l", [P, T, 64])
            ps_r = ps2("ps_r", [P, T, NE])
            ps_c = ps2("ps_c", [P, T, NE])

            s_x = [sem(f"x{i}") for i in range(T)]
            s_par = sem("par")
            s_const = sem("const")
            s_sq = sem("sq")
            s_rstd = sem("rstd")
            s_sqrt = sem("sqrt")
            s_xm = sem("xm")
            s_xs = sem("xs")
            s_tr = sem("tr")
            s_xT = sem("xT")
            s_log = sem("log")
            s_d = sem("dchain")
            s_dg = sem("dg")
            s_eg = sem("eg")
            s_M = sem("M")
            s_rank = sem("rank")
            s_pos = sem("pos")
            s_blk = sem("blk")
            s_st = sem("st")

            with nc.Block() as block:
                @block.sync
                def _(sp):
                    for t in range(T):
                        sp.dma_start(X[:, t, :], x_t[t]).then_inc(s_x[t], 16)
                        if t == 0:
                            sp.dma_start(nrow[:, :], norm_w.partition_broadcast(P)).then_inc(s_par, 16)
                            sp.dma_start(srow[:, :], mod[4 * D:5 * D].partition_broadcast(P)).then_inc(s_par, 16)
                            sp.dma_start(shrow[:, :], mod[3 * D:4 * D].partition_broadcast(P)).then_inc(s_par, 16)
                            sp.dma_start(wr[:, :, 0:NG], w_rg.rearrange("(p j) g -> p j g", j=J)).then_inc(s_par, 16)
                            for g in range(NG):
                                sp.dma_start(wr[:, :, NG + g * EG:NG + (g + 1) * EG],
                                             w_re[g].rearrange("(p j) e -> p j e", j=J)).then_inc(s_par, 16)
                            sp.dma_start(br[:, 0:NG], b_rg.partition_broadcast(P)).then_inc(s_par, 16)
                            sp.dma_start(br[:, NG:NG + NE], b_re.rearrange("g e -> (g e)").partition_broadcast(P)).then_inc(s_par, 16)
                    for t in range(T):
                        sp.wait_ge(s_xs, t + 1)
                        sp.dma_start(xr_t[t], xs[:, t, :]).then_inc(s_st, 16)
                    sp.wait_ge(s_blk, 1)
                    sp.dma_start(blk_dram, bei[:, :]).then_inc(s_st, 16)
                    sp.wait_ge(s_st, 16 * (T + 1))

                @block.gpsimd
                def _(pool):
                    nc.gpsimd.iota(iota_e[:, :], [[1, NE]], base=0, channel_multiplier=0,
                                   allow_small_or_imprecise_dtypes=True).then_inc(s_const, 1)
                    nc.gpsimd.iota(iota_b[:, :], [[1, NBLK]], base=0, channel_multiplier=0,
                                   allow_small_or_imprecise_dtypes=True).then_inc(s_const, 1)
                    nc.gpsimd.iota(tokid[:, :], [[P, T]], base=0, channel_multiplier=1).then_inc(s_const, 1)
                    nc.gpsimd.memset(zero_i[:, :], 0).then_inc(s_const, 1)
                    nc.gpsimd.memset(ones[:, :], 1.0).then_inc(s_const, 1)
                    pool.wait_ge(s_const, 5)
                    nc.gpsimd.affine_select(out=SU[:, :], in_=ones[:, :], compare_op=ALU.is_gt, fill=0.0, base=0,
                                            pattern=[[1, P]], channel_multiplier=-1).then_inc(s_const, 1)
                    nc.gpsimd.affine_select(out=ident[:, :], in_=ones[:, :], compare_op=ALU.is_equal, fill=0.0,
                                            base=0, pattern=[[1, P]], channel_multiplier=-1).then_inc(s_const, 1)
                    pool.dma_start(slot_tok.rearrange("(p b) o -> p (b o)", p=P), zero_i[:, :]).then_inc(s_zero, 16)
                    pool.wait_ge(s_zero, 16)
                    for k, pos in enumerate((pos1, pos2)):
                        pool.wait_ge(s_pos, k + 1)
                        for t in range(T):
                            pool.indirect_dma_start(slot_tok, bass.IndirectOffsetOnAxis(ap=pos[:, t:t + 1], axis=0),
                                                    tokid[:, t:t + 1], None).then_inc(s_sc, 16)
                    pool.wait_ge(s_sc, 16 * 2 * T)

                @block.scalar
                def _(act):
                    for t in range(T):
                        act.wait_ge(s_x[t], 16)
                        if t > 0:
                            act.wait_ge(s_sq, t)
                        nc.scalar.activation(junk[:, :], X[:, t, :], ACT.Square,
                                             accum_out=ss[:, t:t + 1]).then_inc(s_sq, 1)
                    act.wait_ge(s_rstd, 1)
                    nc.scalar.activation(rstd[:, :], ss[:, :], ACT.Sqrt).then_inc(s_sqrt, 1)
                    for t in range(T):
                        act.wait_ge(s_tr, t + 1)
                        if t >= 2:
                            act.wait_ge(s_log, t - 1)
                        nc.scalar.activation(xT[:, t % 2, :, :], ps_t[:, t % 2, :, :], ACT.Copy).then_inc(s_xT, 1)
                    act.wait_ge(s_dg, 1)
                    nc.scalar.activation(eg[:, :, :], dg[:, :, :], ACT.Exp).then_inc(s_eg, 1)
                    nc.scalar.activation(e2[:, :], de[:, :], ACT.Exp).then_inc(s_eg, 1)

                @block.tensor
                def _(pe):
                    pe.wait_ge(s_const, 7)
                    pe.wait_ge(s_par, 16 * (6 + NG))
                    for t in range(T + 1):
                        if t < T:
                            pe.wait_ge(s_xs, t + 1)
                            if t >= 2:
                                pe.wait_ge(s_xT, t - 1)
                            for j in range(J):
                                last = nc.tensor.transpose(ps_t[:, t % 2, j, :], xs[:, t, j::J], ident[:, :])
                            last.then_inc(s_tr, 1)
                        if t >= 1:
                            pe.wait_ge(s_xT, t)
                            for j in range(J):
                                last = nc.tensor.matmul(ps_l[:, t - 1, 0:NG + NE], xT[:, (t - 1) % 2, j, :], wr[:, j, :],
                                                        start=(j == 0), stop=(j == J - 1))
                            last.then_inc(s_log, 1)
                    pe.wait_ge(s_M, 1)
                    nc.tensor.matmul(ps_r[:, :, :], SU[:, :], M[:, :, :], start=True, stop=True).then_inc(s_rank, 1)
                    nc.tensor.matmul(ps_c[:, :, :], ones[:, :], M[:, :, :], start=True, stop=True).then_inc(s_rank, 1)

                @block.vector
                def _(v):
                    n = [0]

                    def link(ins):
                        n[0] += 1
                        ins.then_inc(s_d, 1)
                        v.wait_ge(s_d, n[0])

                    v.wait_ge(s_par, 16 * (6 + NG))
                    link(nc.vector.scalar_tensor_tensor(out=srow[:, :], in0=srow[:, :], scalar=1.0, in1=nrow[:, :],
                                                        op0=ALU.add, op1=ALU.mult))
                    nc.vector.memset(L[:, :, NG:8], NEG)
                    link(nc.vector.memset(onese[:, :], 1.0))
                    v.wait_ge(s_sq, T)
                    nc.vector.tensor_scalar(ss[:, :], ss[:, :], 1.0 / D, EPS, ALU.mult, ALU.add).then_inc(s_rstd, 1)
                    v.wait_ge(s_sqrt, 1)
                    nc.vector.reciprocal(rstd[:, :], rstd[:, :]).then_inc(s_rstd, 1)
                    v.wait_ge(s_rstd, 2)
                    for t in range(T):
                        nc.vector.scalar_tensor_tensor(out=xs[:, t, :], in0=X[:, t, :], scalar=rstd[:, t:t + 1],
                                                       in1=srow[:, :], op0=ALU.mult, op1=ALU.mult).then_inc(s_xm, 1)
                        if t >= 1:
                            v.wait_ge(s_xm, t)
                            nc.vector.tensor_tensor(xs[:, t - 1, :], xs[:, t - 1, :], shrow[:, :], ALU.add).then_inc(s_xs, 1)
                    v.wait_ge(s_xm, T)
                    nc.vector.tensor_tensor(xs[:, T - 1, :], xs[:, T - 1, :], shrow[:, :], ALU.add).then_inc(s_xs, 1)
                    v.wait_ge(s_log, T)
                    nc.vector.tensor_tensor(L[:, :, 0:NG], ps_l[:, :, 0:NG], bc(br[:, 0:NG], T, 1), ALU.add)
                    link(nc.vector.tensor_tensor(L[:, :, 8:8 + NE], ps_l[:, :, NG:NG + NE],
                                                 bc(br[:, NG:NG + NE], T, 1), ALU.add))
                    for t in range(T):
                        last = nc.vector.max(mg[:, t, :], L[:, t, 0:8])
                    link(last)
                    for t in range(T):
                        last = nc.vector.max_index(ig[:, t, :], mg[:, t, :], L[:, t, 0:8])
                    link(last)
                    link(nc.vector.tensor_copy(igf[:, :, :], ig[:, :, :]))
                    link(nc.vector.tensor_tensor(pen[:, :, :], bc(iota_e[:, 0:NG], T, 1), bc(igf[:, :, 0], NG, 2), ALU.is_equal))
                    link(nc.vector.tensor_scalar(pen[:, :, :], pen[:, :, :], -1.0, -NEG, ALU.add, ALU.mult))
                    link(nc.vector.tensor_tensor(LE[:, :, :].rearrange("p t (g e) -> p t g e", g=NG),
                                                 L[:, :, 8:8 + NE].rearrange("p t (g e) -> p t g e", g=NG),
                                                 bc(pen[:, :, :], EG, 3), ALU.add))
                    for t in range(T):
                        last = nc.vector.max(me[:, t, :], LE[:, t, :])
                    link(last)
                    for t in range(T):
                        last = nc.vector.max_index(ie[:, t, :], me[:, t, :], LE[:, t, :])
                    link(last)
                    link(nc.vector.tensor_copy(ief[:, :, :], ie[:, :, :]))
                    nc.vector.tensor_tensor(dg[:, :, :], L[:, :, 0:NG], bc(mg[:, :, 0], NG, 2), ALU.subtract)
                    nc.vector.tensor_tensor(de[:, :], me[:, :, 1], me[:, :, 0], ALU.subtract).then_inc(s_dg, 1)
                    nc.vector.tensor_tensor(M1[:, :, :], bc(iota_e[:, :], T, 1), bc(ief[:, :, 0], NE, 2), ALU.is_equal)
                    link(nc.vector.tensor_tensor(M2[:, :, :], bc(iota_e[:, :], T, 1), bc(ief[:, :, 1], NE, 2), ALU.is_equal))
                    nc.vector.tensor_tensor(M[:, :, :], M1[:, :, :], M2[:, :, :], ALU.add).then_inc(s_M, 1)
                    v.wait_ge(s_eg, 2)
                    link(nc.vector.tensor_reduce(sg[:, :], eg[:, :, :], AX.X, ALU.add))
                    link(nc.vector.scalar_tensor_tensor(out=den[:, :], in0=e2[:, :], scalar=1.0, in1=sg[:, :],
                                                        op0=ALU.add, op1=ALU.mult))
                    link(nc.vector.reciprocal(gate1[:, :], den[:, :]))
                    link(nc.vector.tensor_tensor(gate2[:, :], gate1[:, :], e2[:, :], ALU.mult))
                    v.wait_ge(s_rank, 2)
                    link(nc.vector.memset(Tc[:, 0, :], 0.0))
                    for t in range(1, T):
                        link(nc.vector.tensor_tensor(Tc[:, t, :], Tc[:, t - 1, :], ps_c[:, t - 1, :], ALU.add))
                    link(nc.vector.tensor_tensor(cnt[:, :], Tc[:, T - 1, :], ps_c[:, T - 1, :], ALU.add))
                    link(nc.vector.tensor_scalar(nb[:, :], cnt[:, :], 0.0, None, ALU.is_gt))
                    for k in range(1, SEQ // P):
                        link(nc.vector.scalar_tensor_tensor(out=nb[:, :], in0=cnt[:, :], scalar=float(P * k), in1=nb[:, :],
                                                            op0=ALU.is_gt, op1=ALU.add))
                    link(nc.vector.tensor_tensor_scan(bend[:, :], onese[:, :], nb[:, :], 0.0, ALU.mult, ALU.add))
                    link(nc.vector.tensor_tensor(bst[:, :], bend[:, :], nb[:, :], ALU.subtract))
                    link(nc.vector.scalar_tensor_tensor(out=slot[:, :, :], in0=bc(bst[:, :], T, 1), scalar=float(P),
                                                        in1=Tc[:, :, :], op0=ALU.mult, op1=ALU.add))
                    link(nc.vector.tensor_tensor(slot[:, :, :], ps_r[:, :, :], slot[:, :, :], ALU.add))
                    for Mk, pos in ((M1, pos1), (M2, pos2)):
                        link(nc.vector.tensor_tensor(pr[:, :, :], Mk[:, :, :], slot[:, :, :], ALU.mult))
                        link(nc.vector.tensor_reduce(posf[:, :], pr[:, :, :], AX.X, ALU.add))
                        ins = nc.vector.tensor_copy(pos[:, :], posf[:, :])
                        ins.then_inc(s_pos, 1)
                        v.wait_ge(s_pos, 1 if pos is pos1 else 2)
                    link(nc.vector.tensor_tensor(cb[:, :, :], bc(bend[0:1, :], NBLK, 1), bc(iota_b[:, :], NE, 2), ALU.is_le))
                    link(nc.vector.tensor_reduce(bef[:, 0:NBLK], cb[:, :, :], AX.X, ALU.add))
                    link(nc.vector.tensor_scalar(bef[:, 0:NBLK], bef[:, 0:NBLK], float(NE - 1), None, ALU.min))
                    link(nc.vector.tensor_scalar(cb[:, 0, 0:NBLK // 2], iota_b[:, 0:NBLK:2], bend[0:1, NE - 1:NE], None, ALU.is_lt))
                    link(nc.vector.memset(bef[:, NBLK:NBLK + 16], 0.0))
                    link(nc.vector.tensor_reduce(bef[:, NBLK:NBLK + 1], cb[:, 0, 0:NBLK // 2], AX.X, ALU.add))
                    nc.vector.tensor_copy(bei[:, :], bef[:, :]).then_inc(s_blk, 1)

        with ExitStack() as c2:
            def sb2(name, shape, dt=F32):
                return c2.enter_context(nc.sbuf_tensor(f"{tag}_{name}", shape, dt))

            def ps2(name, shape, dt=F32):
                return c2.enter_context(nc.psum_tensor(f"{tag}_{name}", shape, dt))

            WF = J * NF // 2
            assert 2 * WF == JF * D
            raw = [sb2(f"raw{p}", [P, WF]) for p in range(6)]
            wh = [sb2(f"wh{k}", [P, WF], F32R) for k in range(4)]
            wl = [sb2(f"wl{k}", [P, WF], F32R) for k in range(4)]
            idx = [sb2(f"idx{r}", [P, 1], I32) for r in range(2)]
            xb = [sb2(f"xb{r}", [P, D]) for r in range(2)]
            xh = [sb2(f"xh{r}", [P, J, P], F32R) for r in range(2)]
            xl = [sb2(f"xl{r}", [P, J, P], F32R) for r in range(2)]
            sil = sb2("sil", [P, NF])
            hid = sb2("hid", [P, NF])
            hh = sb2("hh", [P, JF, P], F32R)
            hl = sb2("hl", [P, JF, P], F32R)
            yb = [sb2(f"yb{r}", [P, D]) for r in range(2)]
            zrow = sb2("zrow", [P, D])
            ps_x = ps2("ps_x", [P, J, P])
            ps_g = ps2("ps_g", [P, NF])
            ps_u = ps2("ps_u", [P, NF])
            ps_h = ps2("ps_h", [P, JF, P])
            ps_y = ps2("ps_y", [P, D])

            s_raw = [sem(f"raw{p}") for p in range(6)]
            s_hi, s_lo, s_used = sem("hi"), sem("lo"), sem("used")
            s_xtr, s_xh, s_xl = sem("xtr"), sem("xh"), sem("xl")
            s_sil, s_hid = sem("sil"), sem("hid")
            s_htr, s_hh, s_hl = sem("htr"), sem("hh"), sem("hl")
            s_yb = sem("yb")
            s_ys = [sem(f"ys{r}") for r in range(2)]
            s_one = sem("one")
            s_zr, s_zs = sem("zr"), sem("zs")

            w_dram = (w_gate.rearrange("e (p j) f -> e p (j f)", j=J), w_up.rearrange("e (p j) f -> e p (j f)", j=J),
                      w_down.rearrange("e (p j) f -> e p (j f)", j=JF))
            tok_b = slot_tok.rearrange("(b p) o -> b p o", p=P)
            y_b = yrows.rearrange("(b p) d -> b p d", p=P)

            def pairs(eng):
                return eng.value_load(blk_dram[0:1, NBLK:NBLK + 1], min_val=1, max_val=NBLK // 2)

            with nc.Block() as block:
                @block.sync
                def _(sp):
                    n2 = pairs(sp)
                    sp.sem_inc(s_lo, 6)
                    with sp.Fori(0, n2) as i:
                        for r in range(2):
                            e = sp.value_load(blk_dram[0:1, bass.ds(2 * i + r, 1)], min_val=0, max_val=NE - 1)
                            for p in range(6):
                                sp.wait_ge(s_lo, 12 * i + 6 * r + p + 1)
                                sp.dma_start(raw[p][:, :], w_dram[p // 2][e][:, p % 2 * WF:(p % 2 + 1) * WF]).then_inc(s_raw[p], 16)
                        sp.sem_inc(s_zs, 32)
                    for p in range(4):
                        sp.wait_ge(s_lo, 12 * n2 + p + 1)
                        sp.sem_inc(s_raw[p], 16)
                    sp.wait_ge(s_zr, 1)
                    with sp.Fori(n2, NBLK // 2 + 1) as i:
                        for r in range(2):
                            sp.dma_start(y_b[2 * i + r], zrow[:, :]).then_inc(s_zs, 16)
                    sp.wait_ge(s_zs, 32 * (NBLK // 2 + 1))

                @block.gpsimd
                def _(pool):
                    n2 = pairs(pool)

                    def gather(b, r):
                        pool.wait_ge(s_xtr, b + 1)
                        pool.sem_inc(s_one, 1)
                        pool.dma_start(idx[r][:, :], tok_b[b]).then_inc(s_idx, 16)
                        pool.wait_ge(s_idx, 16 * b + 16)
                        pool.sem_inc(s_one, 1)
                        pool.indirect_dma_start(xb[r][:, :], None, xr_dram,
                                                bass.IndirectOffsetOnAxis(ap=idx[r][:, :], axis=0)).then_inc(s_xb[r], 16)

                    with pool.Fori(0, n2) as i:
                        for r in range(2):
                            gather(2 * i + r, r)
                    gather(pool.snap(2 * n2), 0)
                    pool.wait_ge(s_xb[0], 16 * n2 + 16)
                    pool.sem_inc(s_one, 1)

                @block.tensor
                def _(pe):
                    n2 = pairs(pe)
                    pe.sem_inc(s_xtr, 2)
                    pe.sem_inc(s_used, 4)
                    pe.sem_inc(s_htr, 1)

                    def rows_T(b, r, turn):
                        pe.wait_ge(s_xb[r], 16 * turn + 16)
                        pe.wait_ge(s_xl, b + 1)
                        for j in range(J):
                            last = nc.tensor.transpose(ps_x[:, j, :], xb[r][:, j::J], ident[:, :])
                        last.then_inc(s_xtr, 1)

                    def product(out, a_h, a_l, q, k, half, n_j, width):
                        w_h = wh[k][:, :].rearrange("p (j f) -> p j f", f=width)
                        w_l = wl[k][:, :].rearrange("p (j f) -> p j f", f=width)
                        pe.wait_ge(s_lo, q + 7)
                        for c in range(0, width, 512):
                            o = out[:, c:c + 512]
                            for i in range(n_j // 2):
                                j = half * n_j // 2 + i
                                nc.tensor.matmul(o, a_h[:, j, :], w_h[:, i, c:c + 512], start=(j == 0), stop=False)
                                nc.tensor.matmul(o, a_h[:, j, :], w_l[:, i, c:c + 512], start=False, stop=False)
                                last = nc.tensor.matmul(o, a_l[:, j, :], w_h[:, i, c:c + 512], start=False, stop=(j == n_j - 1))
                        last.then_inc(s_used, 1)

                    rows_T(0, 0, 0)
                    with pe.Fori(0, n2) as i:
                        for r in range(2):
                            b = 2 * i + r
                            q = 12 * i + 6 * r
                            pe.wait_ge(s_xl, b + 2)
                            pe.wait_ge(s_sil, b + 1)
                            for h in range(2):
                                product(ps_g, xh[r], xl[r], q + h, (2 * r + h) % 4, h, J, NF)
                            pe.wait_ge(s_hid, b + 1)
                            for h in range(2):
                                product(ps_u, xh[r], xl[r], q + 2 + h, (2 * r + 2 + h) % 4, h, J, NF)
                            rows_T(b + 1, 1 - r, i + r)
                            pe.wait_ge(s_hid, b + 2)
                            pe.wait_ge(s_hl, b + 1)
                            for j in range(JF):
                                last = nc.tensor.transpose(ps_h[:, j, :], hid[:, j::JF], ident[:, :])
                            last.then_inc(s_htr, 1)
                            pe.wait_ge(s_hl, b + 2)
                            pe.wait_ge(s_yb, b + 1)
                            for h in range(2):
                                product(ps_y, hh, hl, q + 4 + h, (2 * r + 4 + h) % 4, h, JF, D)

                @block.vector
                def _(v):
                    n2 = pairs(v)
                    for s in (s_xl, s_hid, s_hl):
                        v.sem_inc(s, 1)
                    nc.vector.memset(zrow[:, :], 0.0).then_inc(s_zr, 1)

                    def rows_low(b, r):
                        v.wait_ge(s_xh, b + 1)
                        nc.vector.tensor_tensor(xl[r][:, :, :], ps_x[:, :, :], xh[r][:, :, :].bitcast(F32),
                                                ALU.subtract).then_inc(s_xl, 1)

                    def low(q, p, k):
                        v.wait_ge(s_hi, q + 1)
                        nc.vector.tensor_tensor(wl[k][:, :], raw[p][:, :], wh[k][:, :].bitcast(F32), ALU.subtract).then_inc(s_lo, 1)

                    rows_low(0, 0)
                    for p in range(4):
                        low(p, p, p)
                    with v.Fori(0, n2) as i:
                        for r in range(2):
                            b = 2 * i + r
                            q = 12 * i + 6 * r
                            for p in (4, 5):
                                low(q + p, p, (2 * r + p) % 4)
                            v.wait_ge(s_sil, b + 2)
                            v.wait_ge(s_used, q + 8)
                            v.wait_ge(s_htr, b + 1)
                            nc.vector.tensor_tensor(hid[:, :], ps_u[:, :], sil[:, :], ALU.mult).then_inc(s_hid, 1)
                            rows_low(b + 1, 1 - r)
                            v.wait_ge(s_hh, b + 1)
                            nc.vector.tensor_tensor(hl[:, :, :], ps_h[:, :, :], hh[:, :, :].bitcast(F32), ALU.subtract).then_inc(s_hl, 1)
                            for p in range(4):
                                low(q + 6 + p, p, (2 * r + 6 + p) % 4)

                @block.scalar
                def _(act):
                    n2 = pairs(act)
                    for s in (s_sil, s_yb):
                        act.sem_inc(s, 1)
                    act.sem_inc(s_ys[0], 16)
                    act.sem_inc(s_ys[1], 16)

                    def high(q, p, k, turn):
                        act.wait_ge(s_raw[p], 16 * turn + 16)
                        act.wait_ge(s_used, q + 1)
                        nc.scalar.activation(wh[k][:, :], raw[p][:, :], ACT.Copy).then_inc(s_hi, 1)

                    def rows_high(b, r):
                        act.wait_ge(s_xtr, b + 3)
                        nc.scalar.activation(xh[r][:, :, :], ps_x[:, :, :], ACT.Copy).then_inc(s_xh, 1)

                    rows_high(0, 0)
                    for p in range(4):
                        high(p, p, p, 0)
                    with act.Fori(0, n2) as i:
                        for r in range(2):
                            b = 2 * i + r
                            q = 12 * i + 6 * r
                            high(q + 4, 4, (2 * r + 4) % 4, b)
                            act.wait_ge(s_used, q + 6)
                            act.wait_ge(s_hid, b + 1)
                            nc.scalar.activation(sil[:, :], ps_g[:, :], ACT.Silu).then_inc(s_sil, 1)
                            high(q + 5, 5, (2 * r + 5) % 4, b)
                            high(q + 6, 0, (2 * r + 6) % 4, b + 1)
                            rows_high(b + 1, 1 - r)
                            act.wait_ge(s_htr, b + 2)
                            nc.scalar.activation(hh[:, :, :], ps_h[:, :, :], ACT.Copy).then_inc(s_hh, 1)
                            for p in (1, 2, 3):
                                high(q + 6 + p, p, (2 * r + 6 + p) % 4, b + 1)
                            act.wait_ge(s_used, q + 10)
                            act.wait_ge(s_ys[r], 16 * i + 16)
                            nc.scalar.activation(yb[r][:, :], ps_y[:, :], ACT.Copy).then_inc(s_yb, 1)
                            act.wait_ge(s_yb, b + 2)
                            act.dma_start(y_b[b], yb[r][:, :]).then_inc(s_ys[r], 16)
                    act.wait_ge(s_ys[0], 16 * n2 + 16)
                    act.wait_ge(s_ys[1], 16 * n2 + 16)
                    act.sem_inc(s_one, 1)

        with ExitStack() as c2:
            def sb2(name, shape, dt=F32):
                return c2.enter_context(nc.sbuf_tensor(f"{tag}_{name}", shape, dt))

            NB = 4
            ya = sb2("ya", [P, NB, D])
            yc = sb2("yc", [P, NB, D])
            g2row = sb2("g2row", [P, D])
            frow = sb2("frow", [P, D])
            s_row = sem("row")
            s_cm = sem("cm")
            s_q = sem("q")
            s_k = sem("k")
            s_f = sem("f")
            s_out = sem("out")
            s_v = sem("v2")
            with nc.Block() as block:
                @block.gpsimd
                def _(pool):
                    for t in range(T):
                        if t >= NB:
                            pool.wait_ge(s_cm, t - NB + 1)
                        pool.indirect_dma_start(ya[:, t % NB, :], None, yrows,
                                                bass.IndirectOffsetOnAxis(ap=pos1[:, t:t + 1], axis=0)).then_inc(s_ga[t % NB], 16)
                        pool.indirect_dma_start(yc[:, t % NB, :], None, yrows,
                                                bass.IndirectOffsetOnAxis(ap=pos2[:, t:t + 1], axis=0)).then_inc(s_ga[t % NB], 16)

                @block.vector
                def _(v):
                    n = [0]

                    def link(ins):
                        n[0] += 1
                        ins.then_inc(s_v, 1)
                        v.wait_ge(s_v, n[0])

                    v.wait_ge(s_row, 32)
                    for t in range(T):
                        a = ya[:, t % NB, :]
                        v.wait_ge(s_ga[t % NB], 32 * (t // NB + 1))
                        link(nc.vector.tensor_scalar(a, a, gate1[:, t:t + 1], None, ALU.mult))
                        link(nc.vector.scalar_tensor_tensor(out=a, in0=yc[:, t % NB, :], scalar=gate2[:, t:t + 1], in1=a,
                                                            op0=ALU.mult, op1=ALU.add))
                        link(nc.vector.tensor_tensor(a, a, g2row[:, :], ALU.mult))
                        nc.vector.tensor_tensor(X[:, t, :], X[:, t, :], a, ALU.add).then_inc(s_cm, 1)
                    v.wait_ge(s_q, T)
                    nc.vector.tensor_scalar(ss[:, :], ss[:, :], 1.0 / D, EPS, ALU.mult, ALU.add).then_inc(s_k, 1)
                    v.wait_ge(s_q, T + 1)
                    link(nc.vector.reciprocal(rstd[:, :], rstd[:, :]))
                    for t in range(T):
                        nc.vector.scalar_tensor_tensor(out=X[:, t, :], in0=X[:, t, :], scalar=rstd[:, t:t + 1],
                                                       in1=frow[:, :], op0=ALU.mult, op1=ALU.mult).then_inc(s_f, 1)

                @block.scalar
                def _(act):
                    for t in range(T):
                        act.wait_ge(s_cm, t + 1)
                        if t > 0:
                            act.wait_ge(s_q, t)
                        nc.scalar.activation(junk[:, :], X[:, t, :], ACT.Square, accum_out=ss[:, t:t + 1]).then_inc(s_q, 1)
                    act.wait_ge(s_k, 1)
                    nc.scalar.activation(rstd[:, :], ss[:, :], ACT.Sqrt).then_inc(s_q, 1)

                @block.sync
                def _(sp):
                    sp.dma_start(g2row[:, :], mod[5 * D:6 * D].partition_broadcast(P)).then_inc(s_row, 16)
                    sp.dma_start(frow[:, :], final_w.partition_broadcast(P)).then_inc(s_row, 16)
                    for t in range(T):
                        sp.wait_ge(s_f, t + 1)
                        sp.dma_start(out_t[t], X[:, t, :]).then_inc(s_out, 16)
                    sp.wait_ge(s_out, 16 * T)


class Chain:

    def __init__(self, engine, semaphore):
        self.engine, self.semaphore, self.n = engine, semaphore, 0

    def __call__(self, ins):
        self.n += 1
        ins.then_inc(self.semaphore, 1)
        self.engine.wait_ge(self.semaphore, self.n)


def mod_phase(nc, jobs):
    N = 6 * D // 512
    R = 4
    tiles = [(k, n) for k in range(len(jobs)) for n in range(N)]
    with ExitStack() as ctx:
        cs = [ctx.enter_context(nc.sbuf_tensor(f"mod_c{k}", [P, len(job[0]), J], F32)) for k, job in enumerate(jobs)]
        sg = [ctx.enter_context(nc.sbuf_tensor(f"mod_s{k}", [P, len(job[0]), J], F32)) for k, job in enumerate(jobs)]
        row = [ctx.enter_context(nc.sbuf_tensor(f"mod_r{k}", [len(job[0]), N, 512], F32)) for k, job in enumerate(jobs)]
        ring = ctx.enter_context(nc.sbuf_tensor("mod_ring", [P, R, J, 512], F32))
        acc = ctx.enter_context(nc.psum_tensor("mod_acc", [P, 4, 512], F32))
        s_w = [ctx.enter_context(nc.semaphore(f"mod_w{r}")) for r in range(R)]
        s_c = ctx.enter_context(nc.semaphore("mod_c"))
        s_b = ctx.enter_context(nc.semaphore("mod_b"))
        s_silu = ctx.enter_context(nc.semaphore("mod_silu"))
        s_mm = ctx.enter_context(nc.semaphore("mod_mm"))
        s_row = ctx.enter_context(nc.semaphore("mod_row"))
        s_out = ctx.enter_context(nc.semaphore("mod_out"))
        n_c = sum(len(job[0]) for job in jobs)
        with nc.Block() as block:
            @block.sync
            def _(sp):
                for i, (k, n) in enumerate(tiles):
                    if i >= R:
                        sp.wait_ge(s_mm, i - R + 1)
                    w = jobs[k][1]
                    sp.dma_start(ring[:, i % R, :, :], w[:, n * 512:(n + 1) * 512].rearrange("(p j) n -> p j n", j=J)
                                 ).then_inc(s_w[i % R], 16)

            @block.scalar
            def _(act):
                for k, (rows, w, b, out) in enumerate(jobs):
                    for r, src in enumerate(rows):
                        act.dma_start(cs[k][:, r, :], src.rearrange("(p j) -> p j", j=J)).then_inc(s_c, 16)
                for k, (rows, w, b, out) in enumerate(jobs):
                    act.dma_start(row[k][:, :, :].rearrange("r n c -> r (n c)"), b.partition_broadcast(len(rows))).then_inc(s_b, 16)
                act.wait_ge(s_c, 16 * n_c)
                for k in range(len(jobs)):
                    nc.scalar.activation(sg[k][:, :, :], cs[k][:, :, :], ACT.Silu).then_inc(s_silu, 1)
                for k, (rows, w, b, out) in enumerate(jobs):
                    act.wait_ge(s_row, N * (k + 1))
                    act.dma_start(out, row[k][:, :, :].rearrange("r n c -> r (n c)")).then_inc(s_out, 16)
                act.wait_ge(s_out, 16 * len(jobs))

            @block.tensor
            def _(pe):
                pe.wait_ge(s_silu, len(jobs))
                for i, (k, n) in enumerate(tiles):
                    pe.wait_ge(s_w[i % R], 16 * (i // R + 1))
                    if i >= 4:
                        pe.wait_ge(s_row, i - 3)
                    for j in range(J):
                        last = nc.tensor.matmul(acc[0:len(jobs[k][0]), i % 4, :], sg[k][:, :, j], ring[:, i % R, j, :],
                                                start=(j == 0), stop=(j == J - 1))
                    last.then_inc(s_mm, 1)

            @block.vector
            def _(v):
                v.wait_ge(s_b, 16 * len(jobs))
                for i, (k, n) in enumerate(tiles):
                    v.wait_ge(s_mm, i + 1)
                    nc.vector.tensor_tensor(row[k][:, n, :], acc[0:len(jobs[k][0]), i % 4, :], row[k][:, n, :],
                                            ALU.add).then_inc(s_row, 1)


def norm_transpose(nc, tag, src, groups, ident, dst, in_sbuf=False):
    n = sum(g[0] for g in groups)
    of = [k for k, g in enumerate(groups) for _ in range(g[0])]
    with ExitStack() as ctx:
        def sb(name, shape):
            return ctx.enter_context(nc.sbuf_tensor(f"{tag}_{name}", shape, F32))

        def sem(name):
            return ctx.enter_context(nc.semaphore(f"{tag}_{name}"))

        NX = 1 if in_sbuf else 4
        xin = sb("xin", [P, NX, D])
        xs = sb("xs", [P, 2, D])
        junk = sb("junk", [P, D])
        ss = sb("ss", [P, n])
        rstd = sb("rstd", [P, n])
        col = sb("col", [P, len(groups), 3, J])
        pt = ctx.enter_context(nc.psum_tensor(f"{tag}_pt", [P, 2, J, P], F32))
        s_x = [sem(f"x{r}") for r in range(NX)]
        s_par, s_col, s_sq, s_var, s_sd, s_rstd, s_xs, s_tr, s_ev = (
            sem(k) for k in ("par", "col", "sq", "var", "sd", "rstd", "xs", "tr", "ev"))
        n_par = sum(1 + (g[2] is not None) + (g[3] is not None) for g in groups)
        with nc.Block() as block:
            @block.sync
            def _(sp):
                def params():
                    for k, (_, *cols) in enumerate(groups):
                        for c, v in enumerate(cols):
                            if v is not None:
                                sp.dma_start(col[:, k, c, :], v.rearrange("(p j) -> p j", j=J)).then_inc(s_par, 16)

                if in_sbuf:
                    params()
                else:
                    for t in range(n):
                        if t >= NX:
                            sp.wait_ge(s_xs, t - NX + 1)
                        sp.dma_start(xin[:, t % NX, :], src(t)).then_inc(s_x[t % NX], 16)
                        if t == 0:
                            params()

            def rows(t):
                return src(t) if in_sbuf else xin[:, t % NX, :]

            @block.scalar
            def _(act):
                for t in range(n + 1):
                    if t < n:
                        if not in_sbuf:
                            act.wait_ge(s_x[t % NX], 16 * (t // NX + 1))
                        if t > 0:
                            act.wait_ge(s_sq, t)
                        nc.scalar.activation(junk[:, :], rows(t), ACT.Square, accum_out=ss[:, t:t + 1]).then_inc(s_sq, 1)
                    if t > 0:
                        u = t - 1
                        act.wait_ge(s_rstd, u + 1)
                        if u >= 2:
                            act.wait_ge(s_tr, u - 1)
                        nc.scalar.activation(xs[:, u % 2, :], rows(u), ACT.Copy, scale=rstd[:, u:u + 1]).then_inc(s_xs, 1)
                    if t < n:
                        act.wait_ge(s_var, t + 1)
                        nc.scalar.activation(rstd[:, t:t + 1], ss[:, t:t + 1], ACT.Sqrt).then_inc(s_sd, 1)

            @block.tensor
            def _(pe):
                for t in range(n):
                    pe.wait_ge(s_xs, t + 1)
                    if t >= 2:
                        pe.wait_ge(s_ev, t - 1)
                    for j in range(J):
                        last = nc.tensor.transpose(pt[:, t % 2, j, :], xs[:, t % 2, j::J], ident[:, :])
                    last.then_inc(s_tr, 1)

            @block.vector
            def _(v):
                link = Chain(v, s_col)
                v.wait_ge(s_par, 16 * n_par)
                for k, g in enumerate(groups):
                    if g[2] is not None:
                        link(nc.vector.scalar_tensor_tensor(out=col[:, k, 0, :], in0=col[:, k, 1, :], scalar=1.0,
                                                            in1=col[:, k, 0, :], op0=ALU.add, op1=ALU.mult))
                for t in range(n + 1):
                    if t < n:
                        v.wait_ge(s_sq, t + 1)
                        nc.vector.tensor_scalar(ss[:, t:t + 1], ss[:, t:t + 1], 1.0 / D, EPS, ALU.mult, ALU.add).then_inc(s_var, 1)
                        v.wait_ge(s_sd, t + 1)
                        nc.vector.reciprocal(rstd[:, t:t + 1], rstd[:, t:t + 1]).then_inc(s_rstd, 1)
                    if t > 0:
                        u = t - 1
                        k = of[u]
                        v.wait_ge(s_tr, u + 1)
                        for j in range(J):
                            o, i = dst[:, j, u * P:(u + 1) * P], pt[:, u % 2, j, :]
                            if groups[k][3] is None:
                                last = nc.vector.tensor_scalar(o, i, col[:, k, 0, j:j + 1], None, ALU.mult)
                            else:
                                last = nc.vector.tensor_scalar(o, i, col[:, k, 0, j:j + 1], col[:, k, 2, j:j + 1],
                                                               ALU.mult, ALU.add)
                        last.then_inc(s_ev, 1)


def make_masks(nc, tag, masks):
    with ExitStack() as ctx:
        ones = ctx.enter_context(nc.sbuf_tensor(f"{tag}_one", [P, P], F32))
        s_one = ctx.enter_context(nc.semaphore(f"{tag}_s_one"))
        s_mask = ctx.enter_context(nc.semaphore(f"{tag}_s_mask"))
        with nc.Block() as block:
            @block.gpsimd
            def _(pool):
                nc.gpsimd.memset(ones[:, :], 1.0).then_inc(s_one, 1)
                pool.wait_ge(s_one, 1)
                for tile, op, sign in masks:
                    nc.gpsimd.affine_select(out=tile[:, :], in_=ones[:, :], compare_op=op, fill=0.0, base=0,
                                            pattern=[[sign, P]], channel_multiplier=-sign).then_inc(s_mask, 1)
                pool.wait_ge(s_mask, len(masks))


def project_rows(nc, tag, xT, w_tiles, func, out, lhs=None):
    lhs = lhs or (lambda j, t: xT[:, j, t * P:(t + 1) * P])
    R, RO, RP = 2, 4, 4
    with ExitStack() as ctx:
        ring = ctx.enter_context(nc.sbuf_tensor(f"{tag}_ring", [P, R, J, 512], F32))
        ob = ctx.enter_context(nc.sbuf_tensor(f"{tag}_ob", [P, RO, 512], F32))
        acc = ctx.enter_context(nc.psum_tensor(f"{tag}_acc", [P, RP, 512], F32))
        s_w = [ctx.enter_context(nc.semaphore(f"{tag}_w{r}")) for r in range(R)]
        s_o = [ctx.enter_context(nc.semaphore(f"{tag}_o{r}")) for r in range(RO)]
        s_mm = ctx.enter_context(nc.semaphore(f"{tag}_mm"))
        s_ev = ctx.enter_context(nc.semaphore(f"{tag}_ev"))
        steps = [(n, t) for n in range(len(w_tiles)) for t in range(T)]
        with nc.Block() as block:
            @block.sync
            def _(sp):
                for n, w in enumerate(w_tiles):
                    if n >= R:
                        sp.wait_ge(s_mm, T * (n - R + 1))
                    sp.dma_start(ring[:, n % R, :, :], w).then_inc(s_w[n % R], 16)
                for i, (n, t) in enumerate(steps):
                    sp.wait_ge(s_ev, i + 1)
                    sp.dma_start(out(n, t), ob[:, i % RO, :]).then_inc(s_o[i % RO], 16)
                for r in range(RO):
                    sp.wait_ge(s_o[r], 16 * len(steps[r::RO]))

            @block.tensor
            def _(pe):
                for i, (n, t) in enumerate(steps):
                    if t == 0:
                        pe.wait_ge(s_w[n % R], 16 * (n // R + 1))
                    if i >= RP:
                        pe.wait_ge(s_ev, i - RP + 1)
                    for j in range(J):
                        last = nc.tensor.matmul(acc[:, i % RP, :], lhs(j, t), ring[:, n % R, j, :],
                                                start=(j == 0), stop=(j == J - 1))
                    last.then_inc(s_mm, 1)

            @block.scalar
            def _(act):
                for i in range(len(steps)):
                    act.wait_ge(s_mm, i + 1)
                    if i >= RO:
                        act.wait_ge(s_o[i % RO], 16 * (i // RO))
                    nc.scalar.activation(ob[:, i % RO, :], acc[:, i % RP, :], func).then_inc(s_ev, 1)


def project_channels(nc, tag, xT, n_j, w_tiles, func, bias, dst):
    R, RP = 2, 4
    with ExitStack() as ctx:
        ring = ctx.enter_context(nc.sbuf_tensor(f"{tag}_ring", [P, R, n_j, 512], F32))
        acc = ctx.enter_context(nc.psum_tensor(f"{tag}_acc", [P, RP, 512], F32))
        s_w = [ctx.enter_context(nc.semaphore(f"{tag}_w{r}")) for r in range(R)]
        s_mm = ctx.enter_context(nc.semaphore(f"{tag}_mm"))
        s_ev = ctx.enter_context(nc.semaphore(f"{tag}_ev"))
        steps = [(n, c, h) for n in range(len(w_tiles)) for c in range(4) for h in range(2)]
        with nc.Block() as block:
            @block.sync
            def _(sp):
                for n, w in enumerate(w_tiles):
                    if n >= R:
                        sp.wait_ge(s_mm, 8 * (n - R + 1))
                    sp.dma_start(ring[:, n % R, :, :], w).then_inc(s_w[n % R], 16)

            @block.tensor
            def _(pe):
                for i, (n, c, h) in enumerate(steps):
                    if c == 0 and h == 0:
                        pe.wait_ge(s_w[n % R], 16 * (n // R + 1))
                    if i >= RP:
                        pe.wait_ge(s_ev, i - RP + 1)
                    for j in range(n_j):
                        last = nc.tensor.matmul(acc[:, i % RP, :], ring[:, n % R, j, c * P:(c + 1) * P],
                                                xT[:, j, h * 512:(h + 1) * 512], start=(j == 0), stop=(j == n_j - 1))
                    last.then_inc(s_mm, 1)

            @block.scalar
            def _(act):
                for i, (n, c, h) in enumerate(steps):
                    act.wait_ge(s_mm, i + 1)
                    m = 4 * n + c
                    if bias is None:
                        ins = nc.scalar.activation(dst(m, h), acc[:, i % RP, :], func)
                    else:
                        ins = nc.scalar.activation(dst(m, h), acc[:, i % RP, :], func, bias=bias[:, m:m + 1])
                    ins.then_inc(s_ev, 1)


def transpose_rows(nc, tag, src, n_rows, ident, dst):
    with ExitStack() as ctx:
        rows = ctx.enter_context(nc.sbuf_tensor(f"{tag}_rows", [n_rows, P], F32))
        pt = ctx.enter_context(nc.psum_tensor(f"{tag}_pt", [P, n_rows], F32))
        s_in = ctx.enter_context(nc.semaphore(f"{tag}_in"))
        s_t = ctx.enter_context(nc.semaphore(f"{tag}_t"))
        s_e = ctx.enter_context(nc.semaphore(f"{tag}_e"))
        with nc.Block() as block:
            @block.sync
            def _(sp):
                at = 0
                for s in src:
                    sp.dma_start(rows[at:at + s.shape[0], :], s).then_inc(s_in, 16)
                    at += s.shape[0]

            @block.tensor
            def _(pe):
                pe.wait_ge(s_in, 16 * len(src))
                nc.tensor.transpose(pt[:, :], rows[:, :], ident[0:n_rows, 0:n_rows]).then_inc(s_t, 1)

            @block.vector
            def _(v):
                v.wait_ge(s_t, 1)
                nc.vector.tensor_copy(dst, pt[:, :]).then_inc(s_e, 1)


H, G, HD, NS, CW = 16, 4, 64, 128, 5
HG = H // G
NC = 256 // P
TT = T + NC
C0 = SEQ + 4
OUTW = C0 + NC * P
PADW = OUTW + CW - 1


def ssd_inputs(nc, xnT, w_v, cwb, dt_bias, a_log, ident, masks, xs_tok, b_tok, bT, cT, dt, ecum, eend, etot, da):
    NM = (D + 2 * G * NS) // P
    with ExitStack() as ctx:
        def sb(name, shape, dt_=F32):
            return ctx.enter_context(nc.sbuf_tensor(f"si_{name}", shape, dt_))

        def ps(name, shape):
            return ctx.enter_context(nc.psum_tensor(f"si_{name}", shape, F32))

        def sem(name):
            return ctx.enter_context(nc.semaphore(f"si_{name}"))

        R = 2
        ring = sb("ring", [P, R, J, 512])
        xpad = sb("xpad", [P, 2, PADW])
        cacc = sb("cacc", [P, OUTW])
        xc = sb("xc", [P, 2, OUTW])
        acc = ps("acc", [P, 5, 512])
        pt = ps("pt", [P, 3, 4, P])
        s_w = [sem(f"w{r}") for r in range(R)]
        s_pad, s_mm, s_ev, s_cv, s_ch, s_xc, s_tr, s_te = (sem(k) for k in ("pad", "mm", "ev", "cv", "ch", "xc", "tr", "te"))
        halves = ((0, 512), (512, 512), (SEQ, NC * P))
        tgroups = ((0, 4), (4, 4), (8, NC))
        n_t = 12
        with nc.Block() as block:
            @block.sync
            def _(sp):
                for n in range(NM // 4):
                    if n >= R:
                        sp.wait_ge(s_mm, 3 * 4 * (n - R + 1))
                    sp.dma_start(ring[:, n % R, :, :], w_v[:, :, D + n * 512:D + (n + 1) * 512]).then_inc(s_w[n % R], 16)

            @block.tensor
            def _(pe):
                def turn(m):
                    for g, (t0, nt) in enumerate(tgroups):
                        i = 3 * m + g
                        pe.wait_ge(s_xc, m + 1)
                        if i >= 3:
                            pe.wait_ge(s_te, i - 2)
                        for k in range(nt):
                            at = (t0 + k) * P if t0 < T else C0 + k * P
                            last = nc.tensor.transpose(pt[:, i % 3, k, :], xc[:, m % 2, at:at + P], ident[:, :])
                        last.then_inc(s_tr, 1)

                for m in range(NM + 1):
                    if m < NM:
                        if m % 4 == 0:
                            pe.wait_ge(s_w[(m // 4) % R], 16 * (m // 4 // R + 1))
                        for g, (at, n) in enumerate(halves):
                            i = 3 * m + g
                            if i >= 5:
                                pe.wait_ge(s_ev, i - 4)
                            for j in range(J):
                                last = nc.tensor.matmul(acc[:, i % 5, 0:n], ring[:, (m // 4) % R, j, (m % 4) * P:(m % 4 + 1) * P],
                                                        xnT[:, j, at:at + n], start=(j == 0), stop=(j == J - 1))
                            last.then_inc(s_mm, 1)
                    if 1 <= m <= n_t:
                        turn(m - 1)

            @block.scalar
            def _(act):
                def fill(m):
                    if m >= 2:
                        act.wait_ge(s_cv, m - 1)
                    else:
                        act.wait_ge(s_pad, 1)
                    for g, (at, n) in enumerate(halves):
                        act.wait_ge(s_mm, 3 * m + g + 1)
                        o = 2 + at if at < SEQ else C0 + 2
                        nc.scalar.activation(xpad[:, m % 2, o:o + n], acc[:, (3 * m + g) % 5, 0:n], ACT.Copy).then_inc(s_ev, 1)

                for m in range(NM + 1):
                    if m < NM:
                        fill(m)
                    if m >= 1:
                        u = m - 1
                        act.wait_ge(s_cv, u + 1)
                        if 2 <= u < n_t:
                            act.wait_ge(s_tr, 3 * (u - 1))
                        bias = cwb[:, CW * NM + u:CW * NM + u + 1]
                        if u < n_t:
                            ins = nc.scalar.activation(xc[:, u % 2, :], cacc[:, :], ACT.Silu, bias=bias)
                            ins.then_inc(s_xc, 1)
                        if 8 <= u < 12:
                            nc.scalar.activation(bT[:, u - 8, :], cacc[:, 0:SEQ], ACT.Silu, bias=bias).then_inc(s_ch, 1)
                        if u >= 12:
                            nc.scalar.activation(cT[:, u - 12, :], cacc[:, 0:SEQ], ACT.Silu, bias=bias).then_inc(s_xc, 1)

            @block.vector
            def _(v):
                s_link = sem("link")
                link = Chain(v, s_link)
                link(nc.vector.memset(xpad[:, :, 0:2], 0.0))
                link(nc.vector.memset(xpad[:, :, SEQ + 2:C0 + 2], 0.0))
                nc.vector.memset(xpad[:, :, PADW - 2:PADW], 0.0).then_inc(s_pad, 1)

                def conv(m):
                    v.wait_ge(s_ev, 3 * m + 3)
                    if m >= 1:
                        v.wait_ge(s_xc, m)
                    if 9 <= m < 13:
                        v.wait_ge(s_ch, m - 8)
                    for k in range(CW):
                        w = cwb[:, k * NM + m:k * NM + m + 1]
                        x_k = xpad[:, m % 2, k:k + OUTW]
                        if k == 0:
                            ins = nc.vector.tensor_scalar(cacc[:, :], x_k, w, None, ALU.mult)
                        else:
                            ins = nc.vector.scalar_tensor_tensor(out=cacc[:, :], in0=x_k, scalar=w, in1=cacc[:, :],
                                                                 op0=ALU.mult, op1=ALU.add)
                        if k < CW - 1:
                            link(ins)
                        else:
                            ins.then_inc(s_cv, 1)

                def place(m):
                    for g, (t0, nt) in enumerate(tgroups):
                        v.wait_ge(s_tr, 3 * m + g + 1)
                        dst = xs_tok[:, t0:t0 + nt, m * P:(m + 1) * P] if m < 8 else b_tok[:, t0:t0 + nt, (m - 8) * P:(m - 7) * P]
                        nc.vector.tensor_copy(dst, pt[:, (3 * m + g) % 3, 0:nt, :]).then_inc(s_te, 1)

                for m in range(NM + 1):
                    if m < NM:
                        conv(m)
                    if 1 <= m <= n_t:
                        place(m - 1)

    LE_, GT, GE, LT, ONE = masks
    with ExitStack() as ctx:
        def sb(name, shape, dt_=F32):
            return ctx.enter_context(nc.sbuf_tensor(f"sd_{name}", shape, dt_))

        def sem(name):
            return ctx.enter_context(nc.semaphore(f"sd_{name}"))

        wdt = sb("wdt", [P, J, 2 * H])
        bias = sb("bias", [P, 2 * H])
        alog = sb("alog", [P, 2 * H])
        raw, mag, u, w, c1, lg = (sb(n, [P, TT, 2 * H]) for n in ("raw", "mag", "u", "w", "c1", "lg"))
        pd = ctx.enter_context(nc.psum_tensor("sd_pd", [P, TT, 2 * H], F32))
        pc, pe_, po = (ctx.enter_context(nc.psum_tensor(f"sd_{n}", [P, 2, TT, H], F32)) for n in ("pc", "pe", "po"))
        s_in, s_mm, s_l, s_a, s_b, s_e = (sem(k) for k in ("in", "mm", "l", "a", "b", "e"))
        DT0 = D + D + 2 * G * NS
        with nc.Block() as block:
            @block.sync
            def _(sp):
                sp.dma_start(wdt[:, :, :], w_v[:, :, DT0:DT0 + 2 * H]).then_inc(s_in, 16)
                sp.dma_start(bias[:, :], dt_bias.rearrange("d h -> (d h)").partition_broadcast(P)).then_inc(s_in, 16)
                sp.dma_start(alog[:, :], a_log.rearrange("d h -> (d h)").partition_broadcast(P)).then_inc(s_in, 16)

            @block.tensor
            def _(pe):
                pe.wait_ge(s_in, 48)
                for t in range(TT):
                    for j in range(J):
                        last = nc.tensor.matmul(pd[:, t, :], xnT[:, j, t * P:(t + 1) * P], wdt[:, j, :],
                                                start=(j == 0), stop=(j == J - 1))
                last.then_inc(s_mm, 1)
                pe.wait_ge(s_a, 1)
                for q, (mc, me) in enumerate(((LE_, GT), (GE, LT))):
                    r = da[:, :, q * H:(q + 1) * H]
                    nc.tensor.matmul(pc[:, q, :, :], mc[:, :], r, start=True, stop=True)
                    nc.tensor.matmul(pe_[:, q, :, :], me[:, :], r, start=True, stop=True)
                    nc.tensor.matmul(po[:, q, :, :], ONE[:, :], r, start=True, stop=True).then_inc(s_mm, 1)

            @block.vector
            def _(v):
                link = Chain(v, s_l)
                v.wait_ge(s_mm, 1)
                link(nc.vector.tensor_tensor(raw[:, :, :], pd[:, :, :], bc(bias[:, :], TT, 1), ALU.add))
                link(nc.vector.tensor_scalar(mag[:, :, :], raw[:, :, :], -1.0, None, ALU.mult))
                nc.vector.tensor_tensor(mag[:, :, :], mag[:, :, :], raw[:, :, :], ALU.min).then_inc(s_b, 1)
                v.wait_ge(s_e, 1)
                link(nc.vector.tensor_scalar(w[:, :, :], u[:, :, :], 1.0, None, ALU.add))
                nc.vector.tensor_scalar(c1[:, :, :], w[:, :, :], -1.0, None, ALU.add).then_inc(s_b, 1)
                v.wait_ge(s_b, 2)
                link(nc.vector.tensor_tensor(c1[:, :, :], u[:, :, :], c1[:, :, :], ALU.subtract))
                link(nc.vector.reciprocal(w[:, :, :], w[:, :, :]))
                link(nc.vector.tensor_tensor(c1[:, :, :], c1[:, :, :], w[:, :, :], ALU.mult))
                v.wait_ge(s_e, 3)
                link(nc.vector.tensor_tensor(lg[:, :, :], lg[:, :, :], c1[:, :, :], ALU.add))
                link(nc.vector.scalar_tensor_tensor(out=dt[:, :, :], in0=raw[:, :, :], scalar=0.0, in1=lg[:, :, :],
                                                    op0=ALU.max, op1=ALU.add))
                nc.vector.scalar_tensor_tensor(out=da[:, :, :], in0=dt[:, :, :], scalar=-1.0, in1=bc(alog[:, :], TT, 1),
                                               op0=ALU.mult, op1=ALU.mult).then_inc(s_a, 1)
                v.wait_ge(s_e, 6)
                for q in range(2):
                    link(nc.vector.tensor_tensor(eend[:, :, q * H:(q + 1) * H], eend[:, :, q * H:(q + 1) * H],
                                                 dt[:, :, q * H:(q + 1) * H], ALU.mult))

            @block.scalar
            def _(act):
                act.wait_ge(s_b, 1)
                nc.scalar.activation(u[:, :, :], mag[:, :, :], ACT.Exp).then_inc(s_e, 1)
                nc.scalar.activation(alog[:, :], alog[:, :], ACT.Exp).then_inc(s_e, 1)
                act.wait_ge(s_b, 2)
                nc.scalar.activation(lg[:, :, :], u[:, :, :], ACT.Ln, bias=1.0).then_inc(s_e, 1)
                act.wait_ge(s_mm, 3)
                for src, dst in ((pc, ecum), (pe_, eend), (po, etot)):
                    nc.scalar.activation(dst[:, :, :].rearrange("p t (q h) -> p q t h", q=2), src[:, :, :, :],
                                         ACT.Exp).then_inc(s_e, 1)


def ssd_scan(nc, masks, xs_tok, b_tok, bT, cT, dt, da, ecum, eend, etot, d_skip, y):
    LE_, GT, GE, LT, ONE = masks
    jobs = []
    for a, b in zip(list(range(T, TT)) + list(range(T)), list(reversed(range(T, TT))) + list(reversed(range(T)))):
        jobs += [(0, a), (1, b)]
    lat = [i for i, (q, c) in enumerate(jobs) if c < T]
    nth = {i: k for k, i in enumerate(lat)}
    with ExitStack() as ctx:
        def sb(name, shape, dt_=F32):
            return ctx.enter_context(nc.sbuf_tensor(f"ss_{name}", shape, dt_))

        def ps(name, shape):
            return ctx.enter_context(nc.psum_tensor(f"ss_{name}", shape, F32))

        def sem(name):
            return ctx.enter_context(nc.semaphore(f"ss_{name}"))

        hst = sb("hst", [P, 2, H, HD])
        tri = sb("tri", [P, 2, H, P])
        ex = sb("ex", [P, 2, HG, P])
        cbm = sb("cbm", [P, G, P])
        gm = sb("gm", [P, H, P])
        xd = sb("xd", [P, 2, H, HD])
        xe = sb("xe", [P, 2, H, HD])
        yo = sb("yo", [P, H, HD])
        dsk = sb("dsk", [P, H])
        p_seg = ps("seg", [P, 2, HG, P])
        p_cb = ps("cb", [P, G, P])
        p_d = ps("d", [P, H, HD])
        p_o = ps("o", [P, H, HD])
        s_in, s_tri, s_xd, s_seg, s_ex, s_cb, s_gm, s_d, s_o, s_st, s_v, s_yo, s_h, s_y = (
            sem(k) for k in ("in", "tri", "xd", "seg", "ex", "cb", "gm", "d", "o", "st", "v", "yo", "h", "y"))
        with nc.Block() as block:
            @block.sync
            def _(sp):
                sp.dma_start(dsk[:, :], d_skip.partition_broadcast(P)).then_inc(s_in, 16)

            @block.gpsimd
            def _(pool):
                for i, (q, c) in enumerate(jobs):
                    r = i % 2
                    if i >= 2:
                        pool.wait_ge(s_st, i - 1)
                    xv = xs_tok[:, c, :].rearrange("p (h d) -> p h d", h=H)
                    nc.gpsimd.tensor_tensor(xe[:, r, :, :], xv, bc(eend[:, c, q * H:(q + 1) * H], HD, 2), ALU.mult).then_inc(s_xd, 1)
                    if i in nth:
                        nc.gpsimd.tensor_tensor(xd[:, r, :, :], xv, bc(dt[:, c, q * H:(q + 1) * H], HD, 2), ALU.mult).then_inc(s_xd, 1)
                        m = LE_ if q == 0 else GE
                        nc.gpsimd.tensor_tensor(tri[:, r, :, :], bc(m[:, :], H, 1), bc(da[:, c, q * H:(q + 1) * H], P, 2),
                                                ALU.mult).then_inc(s_tri, 1)

            def xd_count(i):
                return sum(1 + (k in nth) for k in range(i + 1))

            @block.tensor
            def _(pe):
                for i, (q, c) in enumerate(jobs):
                    r = i % 2
                    tok = slice(c * P, (c + 1) * P)
                    if i in nth:
                        k = nth[i]
                        if k >= 1:
                            pe.wait_ge(s_gm, 4 * k)
                        for g in range(G):
                            last = nc.tensor.matmul(p_cb[:, g, :], bT[:, g, tok], cT[:, g, tok], start=True, stop=True)
                        last.then_inc(s_cb, 1)
                        pe.wait_ge(s_tri, k + 1)
                        for g in range(G):
                            n = 4 * k + g
                            if n >= 2:
                                pe.wait_ge(s_ex, n - 1)
                            nc.tensor.matmul(p_seg[:, n % 2, :, :], (GT if q == 0 else LT)[:, :], tri[:, r, 4 * g:4 * g + 4, :],
                                             start=True, stop=True).then_inc(s_seg, 1)
                        pe.wait_ge(s_h, 2 + i)
                        for g in range(G):
                            last = nc.tensor.matmul(p_o[:, 4 * g:4 * g + 4, :], cT[:, g, tok], hst[:, q, 4 * g:4 * g + 4, :],
                                                    start=True, stop=True)
                        last.then_inc(s_o, 1)
                        pe.wait_ge(s_xd, xd_count(i))
                        pe.wait_ge(s_gm, 4 * k + 4)
                        if k >= 1:
                            pe.wait_ge(s_y, k)
                        for h in range(H):
                            last = nc.tensor.matmul(p_d[:, h, :], gm[:, h, :], xd[:, r, h, :], start=True, stop=True)
                        last.then_inc(s_d, 1)
                        pe.wait_ge(s_yo, k + 1)
                    else:
                        pe.wait_ge(s_xd, xd_count(i))
                        pe.wait_ge(s_h, 2 + i)
                    for g in range(G):
                        last = nc.tensor.matmul(p_o[:, 4 * g:4 * g + 4, :], b_tok[:, c, g * NS:(g + 1) * NS],
                                                xe[:, r, 4 * g:4 * g + 4, :], start=True, stop=True)
                    last.then_inc(s_st, 1)

            @block.scalar
            def _(act):
                for k, i in enumerate(lat):
                    for g in range(G):
                        n = 4 * k + g
                        act.wait_ge(s_seg, n + 1)
                        if n >= 2:
                            act.wait_ge(s_gm, n - 1)
                        nc.scalar.activation(ex[:, n % 2, :, :], p_seg[:, n % 2, :, :], ACT.Exp).then_inc(s_ex, 1)

            @block.vector
            def _(v):
                link = Chain(v, s_v)
                nc.vector.memset(hst[:, 0, :, :], 0.0).then_inc(s_h, 1)
                nc.vector.memset(hst[:, 1, :, :], 0.0).then_inc(s_h, 1)
                v.wait_ge(s_in, 16)
                for c in range(T):
                    last = nc.vector.tensor_tensor(y[:, c, :].rearrange("p (h d) -> p h d", h=H),
                                                   xs_tok[:, c, :].rearrange("p (h d) -> p h d", h=H),
                                                   bc(dsk[:, :], HD, 2), ALU.mult)
                link(last)
                v.wait_ge(s_h, 2)
                for i, (q, c) in enumerate(jobs):
                    hs = slice(q * H, (q + 1) * H)
                    yc = y[:, c, :].rearrange("p (h d) -> p h d", h=H) if c < T else None
                    if i in nth:
                        k = nth[i]
                        v.wait_ge(s_cb, k + 1)
                        m = LE_ if q == 0 else GE
                        if k >= 1:
                            v.wait_ge(s_d, k)
                        link(nc.vector.tensor_tensor(cbm[:, :, :], p_cb[:, :, :], bc(m[:, :], G, 1), ALU.mult))
                        for g in range(G):
                            n = 4 * k + g
                            v.wait_ge(s_ex, n + 1)
                            nc.vector.tensor_tensor(gm[:, 4 * g:4 * g + 4, :], ex[:, n % 2, :, :], bc(cbm[:, g, :], HG, 1),
                                                    ALU.mult).then_inc(s_gm, 1)
                        v.wait_ge(s_o, k + 1)
                        nc.vector.tensor_tensor(yo[:, :, :], p_o[:, :, :], bc(ecum[:, c, hs], HD, 2), ALU.mult).then_inc(s_yo, 1)
                        v.wait_ge(s_yo, k + 1)
                        link(nc.vector.tensor_tensor(yc, yc, yo[:, :, :], ALU.add))
                        v.wait_ge(s_d, k + 1)
                        nc.vector.tensor_tensor(yc, p_d[:, :, :], yc, ALU.add).then_inc(s_y, 1)
                    link(nc.vector.tensor_tensor(hst[:, q, :, :], hst[:, q, :, :], bc(etot[:, c, hs], HD, 2), ALU.mult))
                    v.wait_ge(s_st, i + 1)
                    nc.vector.tensor_tensor(hst[:, q, :, :], p_o[:, :, :], hst[:, q, :, :], ALU.add).then_inc(s_h, 1)
                    v.wait_ge(s_h, 3 + i)


def gate_rows(nc, tag, y, z_rows, out_rows):
    with ExitStack() as ctx:
        zb = ctx.enter_context(nc.sbuf_tensor(f"{tag}_zb", [P, 4, D], F32))
        s_z = [ctx.enter_context(nc.semaphore(f"{tag}_z{r}")) for r in range(4)]
        s_m = ctx.enter_context(nc.semaphore(f"{tag}_m"))
        s_o = ctx.enter_context(nc.semaphore(f"{tag}_o"))
        with nc.Block() as block:
            @block.sync
            def _(sp):
                for t in range(T):
                    if t >= 4:
                        sp.wait_ge(s_m, t - 3)
                    sp.dma_start(zb[:, t % 4, :], z_rows(t)).then_inc(s_z[t % 4], 16)

            @block.vector
            def _(v):
                for t in range(T):
                    v.wait_ge(s_z[t % 4], 16 * (t // 4 + 1))
                    nc.vector.tensor_tensor(y[:, t, :], y[:, t, :], zb[:, t % 4, :], ALU.mult).then_inc(s_m, 1)

            @block.scalar
            def _(act):
                for t in range(T):
                    act.wait_ge(s_m, t + 1)
                    act.dma_start(out_rows(t), y[:, t, :]).then_inc(s_o, 16)
                act.wait_ge(s_o, 16 * T)


def fourier(nc, f_dram, fT, w_four, dft, rot):
    C = 512
    with ExitStack() as ctx:
        def sb(name, shape):
            return ctx.enter_context(nc.sbuf_tensor(f"fo_{name}", shape, F32))

        def ps(name, shape):
            return ctx.enter_context(nc.psum_tensor(f"fo_{name}", shape, F32))

        def sem(name):
            return ctx.enter_context(nc.semaphore(f"fo_{name}"))

        tab = sb("tab", [P, 2, P])
        rt = sb("rt", [P, 2, T, P])
        wf = sb("wf", [P, G, P])
        cw = sb("cw", [P, G, 2, P])
        ab = sb("ab", [P, 2, T, C])
        bb = sb("bb", [P, 2, T, C])
        p_w = ps("w", [P, G, 2, P])
        p_u = ps("u", [P, 2, G, 2, P])
        p_f = ps("f", [P, 2, G, P])
        s_in, s_f, s_w, s_cw, s_u, s_ev, s_v, s_g, s_o, s_oe = (sem(k) for k in ("in", "f", "w", "cw", "u", "ev", "v", "g", "o", "oe"))
        with nc.Block() as block:
            @block.sync
            def _(sp):
                sp.dma_start(tab[:, :, :], dft).then_inc(s_in, 16)
                sp.dma_start(wf[:, :, :], w_four.rearrange("g c d -> c g d")).then_inc(s_in, 16)
                sp.dma_start(rt[:, :, :, :], rot).then_inc(s_in, 16)
                sp.dma_start(fT[:, :, :], f_dram).then_inc(s_f, 16)

            @block.tensor
            def _(pe):
                pe.wait_ge(s_in, 48)
                for g in range(G):
                    for a in range(2):
                        last = nc.tensor.matmul(p_w[:, g, a, :], tab[:, a, :], wf[:, g, :], start=True, stop=True)
                last.then_inc(s_w, 1)
                pe.wait_ge(s_cw, 1)
                pe.wait_ge(s_f, 16)
                for t in range(T):
                    if t >= 2:
                        pe.wait_ge(s_ev, 2 * (t - 1))
                    for g in range(G):
                        last = nc.tensor.matmul(p_u[:, t % 2, g, :, :], fT[:, g, t * P:(t + 1) * P], cw[:, g, :, :],
                                                start=True, stop=True)
                    last.then_inc(s_u, 1)
                pe.wait_ge(s_g, 1)
                for k2 in range(T):
                    if k2 >= 2:
                        pe.wait_ge(s_oe, k2 - 1)
                    for g in range(G):
                        for a in range(2):
                            last = nc.tensor.matmul(p_f[:, k2 % 2, g, :], ab[:, a, k2, g * P:(g + 1) * P], rt[:, a, k2, :],
                                                    start=(a == 0), stop=(a == 1))
                    last.then_inc(s_o, 1)

            @block.scalar
            def _(act):
                for t in range(T):
                    act.wait_ge(s_u, t + 1)
                    nc.scalar.activation(ab[:, 0, t, :].rearrange("p (g c) -> p g c", g=G), p_u[:, t % 2, :, 0, :], ACT.Copy).then_inc(s_ev, 1)
                    nc.scalar.activation(ab[:, 1, t, :].rearrange("p (g c) -> p g c", g=G), p_u[:, t % 2, :, 1, :], ACT.Copy,
                                         scale=-1.0).then_inc(s_ev, 1)
                for k2 in range(T):
                    act.wait_ge(s_o, k2 + 1)
                    nc.scalar.activation(fT[:, :, k2::T], p_f[:, k2 % 2, :, :], ACT.Copy).then_inc(s_oe, 1)

            @block.vector
            def _(v):
                link = Chain(v, s_v)
                v.wait_ge(s_w, 1)
                nc.vector.tensor_copy(cw[:, :, :, :], p_w[:, :, :, :]).then_inc(s_cw, 1)
                v.wait_ge(s_ev, 2 * T)
                re, im = 0, 1
                RT = 0.5 ** 0.5

                def tt(o, a, b, op):
                    return nc.vector.tensor_tensor(o, a, b, op)

                for c in (re, im):
                    tt(bb[:, c, 0:4, :], ab[:, c, 0:4, :], ab[:, c, 4:8, :], ALU.add)
                    last = tt(bb[:, c, 4:8, :], ab[:, c, 0:4, :], ab[:, c, 4:8, :], ALU.subtract)
                link(last)
                for t in (5, 7):
                    tt(ab[:, re, t, :], bb[:, re, t, :], bb[:, im, t, :], ALU.add)
                    last = tt(ab[:, im, t, :], bb[:, im, t, :], bb[:, re, t, :], ALU.subtract)
                link(last)
                nc.vector.tensor_scalar(bb[:, re, 5, :], ab[:, re, 5, :], RT, None, ALU.mult)
                nc.vector.tensor_scalar(bb[:, im, 5, :], ab[:, im, 5, :], RT, None, ALU.mult)
                nc.vector.tensor_scalar(bb[:, re, 7, :], ab[:, im, 7, :], RT, None, ALU.mult)
                link(nc.vector.tensor_scalar(bb[:, im, 7, :], ab[:, re, 7, :], -RT, None, ALU.mult))
                nc.vector.tensor_copy(ab[:, re, 6, :], bb[:, im, 6, :])
                link(nc.vector.tensor_scalar(ab[:, im, 6, :], bb[:, re, 6, :], -1.0, None, ALU.mult))
                nc.vector.tensor_copy(bb[:, re, 6, :], ab[:, re, 6, :])
                link(nc.vector.tensor_copy(bb[:, im, 6, :], ab[:, im, 6, :]))
                s = bb[:, :, :, :].rearrange("p c (a b) n -> p c a b n", a=2)
                d = ab[:, :, :, :].rearrange("p c (a b) n -> p c a b n", a=2)
                for c in (re, im):
                    for a in range(2):
                        tt(d[:, c, a, 0:2, :], s[:, c, a, 0:2, :], s[:, c, a, 2:4, :], ALU.add)
                        last = tt(d[:, c, a, 2:4, :], s[:, c, a, 0:2, :], s[:, c, a, 2:4, :], ALU.subtract)
                link(last)
                for a in range(2):
                    for c, o, op in ((re, im, (ALU.add, ALU.subtract)), (im, re, (ALU.subtract, ALU.add))):
                        tt(bb[:, c, a, :], d[:, c, a, 0, :], d[:, c, a, 1, :], ALU.add)
                        tt(bb[:, c, 4 + a, :], d[:, c, a, 0, :], d[:, c, a, 1, :], ALU.subtract)
                        tt(bb[:, c, 2 + a, :], d[:, c, a, 2, :], d[:, o, a, 3, :], op[0])
                        last = tt(bb[:, c, 6 + a, :], d[:, c, a, 2, :], d[:, o, a, 3, :], op[1])
                link(last)
                nc.vector.tensor_copy(ab[:, re, :, :], bb[:, re, :, :])
                nc.vector.tensor_scalar(ab[:, im, :, :], bb[:, im, :, :], -1.0, None, ALU.mult).then_inc(s_g, 1)


def mix_out(nc, tag, parts, w_parts, x_rows, gate, out_rows):
    counts = [p.shape[1] for p in parts]
    K = sum(counts)
    with ExitStack() as ctx:
        wt = ctx.enter_context(nc.sbuf_tensor(f"{tag}_w", [P, K, D], F32))
        grow = ctx.enter_context(nc.sbuf_tensor(f"{tag}_grow", [P, D], F32))
        xb = ctx.enter_context(nc.sbuf_tensor(f"{tag}_xb", [P, 3, D], F32))
        tmp = ctx.enter_context(nc.sbuf_tensor(f"{tag}_tmp", [P, 2, D], F32))
        acc = ctx.enter_context(nc.psum_tensor(f"{tag}_acc", [P, 2, D], F32))
        s_w = ctx.enter_context(nc.semaphore(f"{tag}_sw"))
        s_g = ctx.enter_context(nc.semaphore(f"{tag}_sg"))
        s_x = [ctx.enter_context(nc.semaphore(f"{tag}_sx{r}")) for r in range(3)]
        s_mm = ctx.enter_context(nc.semaphore(f"{tag}_mm"))
        s_t = ctx.enter_context(nc.semaphore(f"{tag}_st"))
        s_y = ctx.enter_context(nc.semaphore(f"{tag}_sy"))
        s_o = [ctx.enter_context(nc.semaphore(f"{tag}_so{r}")) for r in range(3)]
        tiles = [(p, k) for p, n in zip(parts, counts) for k in range(n)]
        with nc.Block() as block:
            @block.sync
            def _(sp):
                at = 0
                for n, w in zip(counts, w_parts):
                    sp.dma_start(wt[:, at:at + n, :], w).then_inc(s_w, 16)
                    at += n
                sp.dma_start(grow[:, :], gate.partition_broadcast(P)).then_inc(s_g, 16)
                for t in range(T):
                    if t >= 3:
                        sp.wait_ge(s_o[t % 3], 16 * (t // 3))
                    sp.dma_start(xb[:, t % 3, :], x_rows(t)).then_inc(s_x[t % 3], 16)

            @block.tensor
            def _(pe):
                pe.wait_ge(s_w, 16 * len(parts))
                for t in range(T):
                    if t >= 2:
                        pe.wait_ge(s_t, t - 1)
                    for c in range(2):
                        for i, (part, k) in enumerate(tiles):
                            last = nc.tensor.matmul(acc[:, t % 2, c * 512:(c + 1) * 512], part[:, k, t * P:(t + 1) * P],
                                                    wt[:, i, c * 512:(c + 1) * 512], start=(i == 0), stop=(i == K - 1))
                    last.then_inc(s_mm, 1)

            @block.vector
            def _(v):
                v.wait_ge(s_g, 16)
                for t in range(T):
                    v.wait_ge(s_mm, t + 1)
                    nc.vector.tensor_tensor(tmp[:, t % 2, :], acc[:, t % 2, :], grow[:, :], ALU.mult).then_inc(s_t, 1)
                    v.wait_ge(s_t, t + 1)
                    v.wait_ge(s_x[t % 3], 16 * (t // 3 + 1))
                    nc.vector.tensor_tensor(xb[:, t % 3, :], xb[:, t % 3, :], tmp[:, t % 2, :], ALU.add).then_inc(s_y, 1)

            @block.scalar
            def _(act):
                for t in range(T):
                    act.wait_ge(s_y, t + 1)
                    act.dma_start(out_rows(t), xb[:, t % 3, :]).then_inc(s_o[t % 3], 16)
                for r in range(3):
                    act.wait_ge(s_o[r], 16 * len(range(r, T, 3)))


def mixer1_phase(nc, x, ctx_in, mod, norm1, w_in, conv_w, conv_b, dt_bias, a_log, d_skip, ssd_norm, w_four, w_out,
                 dft, rot, x1_out):
    x_t, c_t, out_t = (a.rearrange("(t p) d -> t p d", p=P) for a in (x, ctx_in, x1_out))
    w_v = w_in.rearrange("(p j) n -> p j n", j=J)
    F0 = D + D + 2 * G * NS + 2 * H
    z_dram = nc.dram_tensor("x1_zd", (SEQ, D), F32, kind="Internal").ap().rearrange("(t p) d -> t p d", p=P)
    y_dram = nc.dram_tensor("x1_yd", (SEQ, D), F32, kind="Internal").ap().rearrange("(t p) d -> t p d", p=P)
    f_dram = nc.dram_tensor("x1_fd", (P, G, SEQ), F32, kind="Internal").ap()

    with ExitStack() as top:
        ident = top.enter_context(nc.sbuf_tensor("x1_ident", [P, P], F32))
        with ExitStack() as mid:
            def sb(name, shape):
                return mid.enter_context(nc.sbuf_tensor(f"x1_{name}", shape, F32))

            masks = tuple(sb(n, [P, P]) for n in ("mLE", "mGT", "mGE", "mLT", "mONE"))
            make_masks(nc, "x1m", [(ident, ALU.is_equal, 1), (masks[0], ALU.is_ge, 1), (masks[1], ALU.is_gt, -1),
                                   (masks[2], ALU.is_ge, -1), (masks[3], ALU.is_gt, 1), (masks[4], ALU.is_ge, 0)])
            xs_tok, b_tok = sb("xs_tok", [P, TT, D]), sb("b_tok", [P, TT, G * NS])
            bT, cT = sb("bT", [P, G, SEQ]), sb("cT", [P, G, SEQ])
            dt, da, ecum, eend, etot = (sb(n, [P, TT, 2 * H]) for n in ("dt", "da", "ecum", "eend", "etot"))
            cwb = sb("cwb", [P, (CW + 1) * 16])
            with ExitStack() as c2:
                xnT = c2.enter_context(nc.sbuf_tensor("x1_xnT", [P, J, TT * P], F32))
                norm_transpose(nc, "x1n", lambda t: x_t[t] if t < T else c_t[t - T],
                               [(T, norm1, mod[0, D:2 * D], mod[0, 0:D]), (NC, norm1, mod[1, D:2 * D], mod[1, 0:D])],
                               ident, xnT)
                transpose_rows(nc, "x1c", [conv_w.rearrange("k (m p) -> (k m) p", p=P), conv_b.rearrange("(m p) -> m p", p=P)],
                               (CW + 1) * 16, ident, cwb[:, :])
                project_rows(nc, "x1z", xnT, [w_v[:, :, 0:512], w_v[:, :, 512:1024]], ACT.Silu,
                             lambda n, t: z_dram[t][:, n * 512:(n + 1) * 512])
                with ExitStack() as c3:
                    fb = c3.enter_context(nc.sbuf_tensor("x1_fb", [P, G, SEQ], F32))
                    project_channels(nc, "x1f", xnT, J, [w_v[:, :, F0:F0 + 512]], ACT.Copy, None,
                                     lambda m, h: fb[:, m, h * 512:(h + 1) * 512])
                    store(nc, "x1fs", fb[:, :, :], f_dram)
                ssd_inputs(nc, xnT, w_v, cwb, dt_bias, a_log, ident, masks, xs_tok, b_tok, bT, cT, dt, ecum, eend, etot, da)
            y = sb("y", [P, T, D])
            ssd_scan(nc, masks, xs_tok, b_tok, bT, cT, dt, da, ecum, eend, etot, d_skip, y)
            gate_rows(nc, "x1g", y, lambda t: z_dram[t], lambda t: y_dram[t])
        yT = top.enter_context(nc.sbuf_tensor("x1_yT", [P, J, SEQ], F32))
        fT = top.enter_context(nc.sbuf_tensor("x1_fT", [P, G, SEQ], F32))
        norm_transpose(nc, "x1y", lambda t: y_dram[t], [(T, ssd_norm, None, None)], ident, yT)
        fourier(nc, f_dram, fT, w_four, dft, rot)
        mix_out(nc, "x1o", [yT, fT], [w_out[0:D, :].rearrange("(p j) n -> p j n", j=J),
                                      w_out[D:D + G * P, :].rearrange("(g p) n -> p g n", p=P)],
                lambda t: x_t[t], mod[0, 2 * D:3 * D], lambda t: out_t[t])


def store(nc, tag, src, dst):
    with nc.semaphore(f"{tag}_s") as s_st:
        with nc.Block() as block:
            @block.sync
            def _(sp):
                sp.dma_start(dst, src).then_inc(s_st, 16)
                sp.wait_ge(s_st, 16)


def dft_tables():
    import numpy as np
    c = np.arange(P)
    a = 2 * np.pi * np.outer(c, c) / P
    scale = 1.0 / np.sqrt(SEQ * P)
    dft = np.stack([np.cos(a), np.sin(a)], 1) * scale
    k = (np.arange(T)[:, None] + T * np.arange(P)[None, :])
    b = 2 * np.pi * np.mod(c[:, None, None] * k, SEQ) / SEQ
    rot = np.stack([np.cos(b), -np.sin(b)], 1)
    return dft.astype(np.float32), rot.astype(np.float32)


SG, SN, SC = 32, 64, 16
NQ = SG // 2
TC = P // SC
W2 = SG * SC
M2 = W2 // P
SH, SHD = 8, 64
LN_EPS = 1e-5
TWO_PI = 6.283185307179586
CW1 = 6.28125
CW2 = 0.0019350051879882812
CW3 = TWO_PI - CW1 - CW2
ROUND = 1.5 * 2.0 ** 23
PI_IN = 3.1415925


def s5_coefficients(nc, a_re, a_im, b_re, b_im, c_re, c_im, log_step, ident, pw, phase8, rho8, wre, wim, cre, cim,
                    spare):
    with ExitStack() as ctx:
        def sb(name, shape):
            return ctx.enter_context(nc.sbuf_tensor(f"sc_{name}", shape, F32))

        def sem(name):
            return ctx.enter_context(nc.semaphore(f"sc_{name}"))

        rows = sb("rows", [NQ, 3, P])
        ls = sb("ls", [NQ, 2])
        w1, w2 = (spare[:, 2 * k:2 * k + 2, :].rearrange("p a (b c d) -> p (a b) c d", c=TC, d=SC) for k in range(2))
        crow = spare[0:SC, 4:8, :].rearrange("p (k a) (b c) -> p k (a b) c", k=2, c=P)
        bb = sb("bb", [P, 2, NQ, SC])
        fb = sb("fb", [P, 2, NQ, SC])
        par = sb("par", [P, 3, NQ])
        names = ("lr", "dtv", "m", "th", "k", "r", "ra", "sn", "cs", "den", "nr", "t1", "t2", "fr", "fi")
        v_ = {n: sb(n, [P, NQ]) for n in names}
        rev = sb("rev", [P, 2, TC, NQ])
        p_p = ctx.enter_context(nc.psum_tensor("sc_p", [P, 3, NQ], F32))
        p_c = [ctx.enter_context(nc.psum_tensor(f"sc_c{k}", [P, NQ, SC], F32)) for k in range(2)]
        s_in, s_c, s_b, s_ls, s_t, s_v, s_a, s_x = (sem(k) for k in ("in", "c", "b", "ls", "t", "v", "a", "x"))
        with nc.Block() as block:
            @block.sync
            def _(sp):
                sp.dma_start(ls[:, :], log_step.rearrange("(q r) -> q r", r=2)).then_inc(s_in, 16)
                sp.dma_start(rows[:, 0, :], a_re.rearrange("(q r) n -> q (r n)", r=2)).then_inc(s_in, 16)
                sp.dma_start(rows[:, 1, :], a_im.rearrange("(q r) n -> q (r n)", r=2)).then_inc(s_in, 16)
                for k, b in enumerate((b_re, b_im)):
                    for r in range(2):
                        sp.dma_start(bb[r * SN:(r + 1) * SN, k, :, :], b.rearrange("(q r) n h -> r n q h", r=2)[r]).then_inc(s_b, 16)

                for k, c in enumerate((c_re, c_im)):
                    for r in range(2):
                        sp.dma_start(crow[:, k, :, r * SN:(r + 1) * SN], c.rearrange("(q r) h n -> r h q n", r=2)[r]).then_inc(s_c, 16)

            @block.tensor
            def _(pe):
                pe.wait_ge(s_ls, 1)
                for k in range(3):
                    last = nc.tensor.transpose(p_p[:, k, :], rows[:, k, :], ident[0:NQ, 0:NQ])
                last.then_inc(s_t, 1)
                pe.wait_ge(s_c, 64)
                for k in range(2):
                    for q in range(NQ):
                        last = nc.tensor.transpose(p_c[k][:, q, :], crow[:, k, q, :], ident[0:SC, 0:SC])
                last.then_inc(s_t, 1)

            @block.scalar
            def _(act):
                act.wait_ge(s_x, 1)
                nc.scalar.activation(v_["dtv"][:, :], par[:, 2, :], ACT.Exp).then_inc(s_a, 1)
                act.wait_ge(s_x, 2)
                nc.scalar.activation(v_["m"][:, :], v_["m"][:, :], ACT.Exp).then_inc(s_a, 1)
                act.wait_ge(s_x, 3)
                nc.scalar.activation(v_["sn"][:, :], v_["r"][:, :], ACT.Sin).then_inc(s_a, 1)
                nc.scalar.activation(v_["cs"][:, :], v_["ra"][:, :], ACT.Sin).then_inc(s_a, 1)

            @block.vector
            def _(v):
                link = Chain(v, s_v)

                def tt(o, a, b, op):
                    link(nc.vector.tensor_tensor(o, a, b, op))

                def ts(o, a, c1, op1, c2=None, op2=None):
                    link(nc.vector.tensor_scalar(o, a, c1, c2, op1, op2) if op2 else nc.vector.tensor_scalar(o, a, c1, None, op1))

                def stt(o, a, c, b, op0, op1):
                    link(nc.vector.scalar_tensor_tensor(out=o, in0=a, scalar=c, in1=b, op0=op0, op1=op1))

                def g(n):
                    return v_[n][:, :]

                v.wait_ge(s_in, 48)
                nc.vector.tensor_copy(rows[:, 2, :].rearrange("q (r n) -> q r n", r=2), bc(ls[:, :], SN, 2)).then_inc(s_ls, 1)
                for t_ in (wre, wim):
                    link(nc.vector.memset(t_[:, :, TC:, :], 0.0))
                for t_ in (cre, cim):
                    link(nc.vector.memset(t_[:, :, :, :], 0.0))
                v.wait_ge(s_t, 1)
                nc.vector.tensor_copy(par[:, :, :], p_p[:, :, :]).then_inc(s_x, 1)
                v.wait_ge(s_x, 1)
                ts(g("lr"), par[:, 0, :], -1e-4, ALU.min)
                li = par[:, 1, :]
                v.wait_ge(s_a, 1)
                nc.vector.tensor_tensor(g("m"), g("lr"), g("dtv"), ALU.mult).then_inc(s_x, 1)
                tt(g("th"), li, g("dtv"), ALU.mult)
                ts(g("k"), g("th"), 1.0 / TWO_PI, ALU.mult)
                ts(g("k"), g("k"), ROUND, ALU.add)
                ts(g("k"), g("k"), -ROUND, ALU.add)
                stt(g("r"), g("k"), -CW1, g("th"), ALU.mult, ALU.add)
                stt(g("r"), g("k"), -CW2, g("r"), ALU.mult, ALU.add)
                stt(g("r"), g("k"), -CW3, g("r"), ALU.mult, ALU.add)
                ts(g("r"), g("r"), PI_IN, ALU.min, -PI_IN, ALU.max)
                stt(g("ra"), g("r"), -1.0, g("r"), ALU.mult, ALU.max)
                nc.vector.tensor_scalar(g("ra"), g("ra"), -1.0, 0.5 * 3.141592653589793, ALU.mult, ALU.add).then_inc(s_x, 1)
                v.wait_ge(s_a, 4)
                P_re, P_im = pw[0], pw[1]
                link(nc.vector.memset(P_re[:, 0, :], 1.0))
                link(nc.vector.memset(P_im[:, 0, :], 0.0))
                tt(P_re[:, 1, :], g("m"), g("cs"), ALU.mult)
                tt(P_im[:, 1, :], g("m"), g("sn"), ALU.mult)

                def cmul(o_re, o_im, ar, ai, br, bi, t1, t2, t3):
                    tt(t1, ar, br, ALU.mult)
                    tt(t2, ai, bi, ALU.mult)
                    tt(t3, ar, bi, ALU.mult)
                    tt(t1, t1, t2, ALU.subtract)
                    tt(t2, ai, br, ALU.mult)
                    link(nc.vector.tensor_copy(o_re, t1))
                    tt(o_im, t3, t2, ALU.add)

                for d in range(2, TC + 1):
                    cmul(P_re[:, d, :], P_im[:, d, :], P_re[:, d - 1, :], P_im[:, d - 1, :], P_re[:, 1, :], P_im[:, 1, :],
                         g("t1"), g("t2"), g("k"))
                link(nc.vector.tensor_copy(phase8[0], g("cs")))
                link(nc.vector.tensor_copy(phase8[1], g("sn")))
                link(nc.vector.tensor_copy(rho8, g("m")))
                for _ in range(3):
                    cmul(phase8[0], phase8[1], phase8[0], phase8[1], phase8[0], phase8[1], g("t1"), g("t2"), g("k"))
                    tt(rho8, rho8, rho8, ALU.mult)
                tt(g("den"), g("lr"), g("lr"), ALU.mult)
                tt(g("t1"), li, li, ALU.mult)
                tt(g("den"), g("den"), g("t1"), ALU.add)
                link(nc.vector.reciprocal(g("den"), g("den")))
                ts(g("nr"), P_re[:, 1, :], -1.0, ALU.add)
                tt(g("t1"), g("nr"), g("lr"), ALU.mult)
                tt(g("t2"), P_im[:, 1, :], li, ALU.mult)
                tt(g("fr"), g("t1"), g("t2"), ALU.add)
                tt(g("fr"), g("fr"), g("den"), ALU.mult)
                tt(g("t1"), P_im[:, 1, :], g("lr"), ALU.mult)
                tt(g("t2"), g("nr"), li, ALU.mult)
                tt(g("fi"), g("t1"), g("t2"), ALU.subtract)
                tt(g("fi"), g("fi"), g("den"), ALU.mult)
                v.wait_ge(s_b, 64)
                fr, fi = bc(g("fr"), SC, 2), bc(g("fi"), SC, 2)
                cmul(fb[:, 0, :, :], fb[:, 1, :, :], fr, fi, bb[:, 0, :, :], bb[:, 1, :, :],
                     w1[:, :, 0, :], w2[:, :, 0, :], w1[:, :, 1, :])
                for j in range(TC):
                    for k in range(2):
                        link(nc.vector.tensor_copy(rev[:, k, j, :], pw[k][:, TC - 1 - j, :]))
                ar, ai = (bc(rev[:, k, :, :].rearrange("p d q -> p q d"), SC, 3) for k in range(2))
                br, bi = (bc(fb[:, k, :, :], TC, 2) for k in range(2))
                tt(w1[:, :, :, :], ar, br, ALU.mult)
                tt(w2[:, :, :, :], ai, bi, ALU.mult)
                tt(wre[:, :, 0:TC, :], w1[:, :, :, :], w2[:, :, :, :], ALU.subtract)
                tt(w1[:, :, :, :], ar, bi, ALU.mult)
                tt(w2[:, :, :, :], ai, br, ALU.mult)
                tt(wim[:, :, 0:TC, :], w1[:, :, :, :], w2[:, :, :, :], ALU.add)
                v.wait_ge(s_t, 2)
                for r in range(2):
                    h = slice(r * SN, (r + 1) * SN)
                    link(nc.vector.tensor_copy(cre[h, :, r, :], p_c[0][h, :, :]))
                    link(nc.vector.tensor_scalar(cim[h, :, r, :], p_c[1][h, :, :], -1.0, None, ALU.mult))


def s5_states(nc, za, ident, pw, phase8, rho8, wre, wim, cre, cim, uT, mT, hre, him, z_re, z_im, t1, t2, t3):
    with ExitStack() as ctx:
        bt = ctx.enter_context(nc.sbuf_tensor("sx_bt", [P, 2, 2, P], F32))
        ub = ctx.enter_context(nc.sbuf_tensor("sx_ub", [P, 2, 4, TC, SC], F32))
        p_u = ctx.enter_context(nc.psum_tensor("sx_u", [P, 2, 4, P], F32))
        p_m = ctx.enter_context(nc.psum_tensor("sx_m", [P, 2, 512], F32))
        p_b = ctx.enter_context(nc.psum_tensor("sx_b", [P, 2, 512], F32))
        p_z = ctx.enter_context(nc.psum_tensor("sx_z", [P, 2, 512], F32))
        s_u, s_ue, s_m, s_me, s_b, s_be, s_z, s_ze, s_v = (
            ctx.enter_context(nc.semaphore(f"sx_{k}")) for k in ("u", "ue", "m", "me", "b", "be", "z", "ze", "v"))
        s_ub = ctx.enter_context(nc.semaphore("sx_ub"))
        C = P
        with nc.Block() as block:
            @block.gpsimd
            def _(pool):
                for i in range(SG // 4):
                    if i >= 2:
                        pool.wait_ge(s_u, i - 1)
                    nc.gpsimd.tensor_copy(ub[:, i % 2, :, :, :], za[:, :, 4 * i * SC:4 * (i + 1) * SC].rearrange(
                        "p t (g h) -> p g t h", g=4)).then_inc(s_ub, 1)

            @block.tensor
            def _(pe):
                for i in range(SG // 4):
                    if i >= 2:
                        pe.wait_ge(s_ue, i - 1)
                    for k in range(4):
                        if k == 0:
                            pe.wait_ge(s_ub, i + 1)
                        last = nc.tensor.transpose(p_u[:, i % 2, k, :], ub[:, i % 2, k, :, :], ident[:, :])
                    last.then_inc(s_u, 1)
                pe.wait_ge(s_ue, SG // 4)
                for q in range(NQ + 1):
                    if q < NQ:
                        if q >= 2:
                            pe.wait_ge(s_be, q - 1)
                        nc.tensor.transpose(p_b[:, q % 2, 0:P], wre[:, q, 0:TC, :], ident[:, :])
                        nc.tensor.transpose(p_b[:, q % 2, P:2 * P], wim[:, q, 0:TC, :], ident[:, :]).then_inc(s_b, 1)
                        if q >= 2:
                            pe.wait_ge(s_me, q - 1)
                        for t in range(TC):
                            o = p_m[:, q % 2, t * 2 * SC:(t + 1) * 2 * SC]
                            nc.tensor.matmul(o, wre[:, q, TC - 1 - t:2 * TC - 1 - t, :], cre[:, q, :, :], start=True, stop=False)
                            last = nc.tensor.matmul(o, wim[:, q, TC - 1 - t:2 * TC - 1 - t, :], cim[:, q, :, :], start=False, stop=True)
                        last.then_inc(s_m, 1)
                    if q >= 1:
                        u = q - 1
                        pe.wait_ge(s_be, u + 1)
                        if u >= 2:
                            pe.wait_ge(s_ze, u - 1)
                        for k in range(2):
                            for r in range(2):
                                last = nc.tensor.matmul(p_z[r * SN:(r + 1) * SN, u % 2, k * C:(k + 1) * C],
                                                        bt[:, u % 2, k, r * SN:(r + 1) * SN], uT[:, 2 * u + r, :],
                                                        start=True, stop=True)
                        last.then_inc(s_z, 1)

            @block.scalar
            def _(act):
                for i in range(SG // 4):
                    act.wait_ge(s_u, i + 1)
                    nc.scalar.activation(uT[:, 4 * i:4 * i + 4, :], p_u[:, i % 2, :, :], ACT.Copy).then_inc(s_ue, 1)
                for q in range(NQ + 1):
                    if q < NQ:
                        act.wait_ge(s_b, q + 1)
                        if q >= 2:
                            act.wait_ge(s_z, q - 1)
                        nc.scalar.activation(bt[:, q % 2, :, :].rearrange("p k n -> p (k n)"), p_b[:, q % 2, 0:2 * P], ACT.Copy).then_inc(s_be, 1)
                        act.wait_ge(s_m, q + 1)
                        nc.scalar.activation(mT[:, 2 * q:2 * q + 2, :, :].rearrange("p r t h -> p t r h"),
                                             p_m[:, q % 2, 0:2 * P].rearrange("p (t r h) -> p t r h", t=TC, r=2),
                                             ACT.Copy).then_inc(s_me, 1)
                    if q >= 1:
                        u = q - 1
                        act.wait_ge(s_z, u + 1)
                        nc.scalar.activation(z_re[:, u, :], p_z[:, u % 2, 0:C], ACT.Copy)
                        nc.scalar.activation(z_im[:, u, :], p_z[:, u % 2, C:2 * C], ACT.Copy).then_inc(s_ze, 1)

            @block.vector
            def _(v):
                link = Chain(v, s_v)

                def tt(o, a, b, op):
                    link(nc.vector.tensor_tensor(o, a, b, op))

                cs, sn = hre, him
                link(nc.vector.memset(cs[:, :, 0:1], 1.0))
                link(nc.vector.memset(sn[:, :, 0:1], 0.0))
                link(nc.vector.tensor_copy(cs[:, :, 1], phase8[0]))
                link(nc.vector.tensor_copy(sn[:, :, 1], phase8[1]))
                n = 1
                while n < C // 2:
                    c_, s_ = cs[:, :, n], sn[:, :, n]
                    tt(t1[:, :, 0], c_, c_, ALU.mult)
                    tt(t2[:, :, 0], s_, s_, ALU.mult)
                    tt(t3[:, :, 0], c_, s_, ALU.mult)
                    tt(cs[:, :, 2 * n], t1[:, :, 0], t2[:, :, 0], ALU.subtract)
                    link(nc.vector.tensor_scalar(sn[:, :, 2 * n], t3[:, :, 0], 2.0, None, ALU.mult))
                    m = 2 * n
                    a_c, a_s = bc(cs[:, :, m], m - 1, 2), bc(sn[:, :, m], m - 1, 2)
                    b_c, b_s = cs[:, :, 1:m], sn[:, :, 1:m]
                    tt(t1[:, :, 1:m], a_c, b_c, ALU.mult)
                    tt(t2[:, :, 1:m], a_s, b_s, ALU.mult)
                    tt(cs[:, :, m + 1:2 * m], t1[:, :, 1:m], t2[:, :, 1:m], ALU.subtract)
                    tt(t1[:, :, 1:m], a_c, b_s, ALU.mult)
                    tt(t2[:, :, 1:m], a_s, b_c, ALU.mult)
                    tt(sn[:, :, m + 1:2 * m], t1[:, :, 1:m], t2[:, :, 1:m], ALU.add)
                    n = m
                v.wait_ge(s_ze, NQ)
                tt(t1, z_re, cs, ALU.mult)
                tt(t2, z_im, sn, ALU.mult)
                tt(t1, t1, t2, ALU.add)
                tt(t2, z_im, cs, ALU.mult)
                tt(t3, z_re, sn, ALU.mult)
                tt(t2, t2, t3, ALU.subtract)
                link(nc.vector.tensor_copy(t3, bc(rho8, C, 2)))
                link(nc.vector.memset(t3[:, :, 0:1], 0.0))

                def flat(a):
                    return a.rearrange("p q c -> p (q c)")

                link(nc.vector.tensor_tensor_scan(flat(z_re), flat(t3), flat(t1), 0.0, ALU.mult, ALU.add))
                link(nc.vector.tensor_tensor_scan(flat(z_im), flat(t3), flat(t2), 0.0, ALU.mult, ALU.add))
                tt(t1, z_re, cs, ALU.mult)
                tt(t2, z_im, sn, ALU.mult)
                tt(t3, z_re, sn, ALU.mult)
                tt(z_im, z_im, cs, ALU.mult)
                link(nc.vector.memset(hre[:, :, 0:1], 0.0))
                link(nc.vector.memset(him[:, :, 0:1], 0.0))
                tt(hre[:, :, 1:], t1[:, :, 0:C - 1], t2[:, :, 0:C - 1], ALU.subtract)
                tt(him[:, :, 1:], t3[:, :, 0:C - 1], z_im[:, :, 0:C - 1], ALU.add)


def s5_outputs(nc, za, ident, d_skip, pw, cre, cim, uT, mT, hre, him, yT):
    with ExitStack() as ctx:
        dsk = ctx.enter_context(nc.sbuf_tensor("so_dsk", [P, W2], F32))
        ot = ctx.enter_context(nc.sbuf_tensor("so_ot", [P, 2, 2, 2, TC, SC], F32))
        t1 = ctx.enter_context(nc.sbuf_tensor("so_t1", [P, 2, TC, SC], F32))
        t2 = ctx.enter_context(nc.sbuf_tensor("so_t2", [P, 2, TC, SC], F32))
        p_y = ctx.enter_context(nc.psum_tensor("so_y", [P, 2, 512], F32))
        p_t = ctx.enter_context(nc.psum_tensor("so_t", [P, 2, M2, P], F32))
        s_in, s_v, s_ot, s_y, s_ye, s_g, s_t, s_te = (
            ctx.enter_context(nc.semaphore(f"so_{k}")) for k in ("in", "v", "ot", "y", "ye", "g", "t", "te"))
        with nc.Block() as block:
            @block.sync
            def _(sp):
                sp.dma_start(dsk[:, :], d_skip.rearrange("g h -> (g h)").partition_broadcast(P)).then_inc(s_in, 16)

            @block.tensor
            def _(pe):
                for q in range(NQ):
                    pe.wait_ge(s_ot, q + 1)
                    if q >= 2:
                        pe.wait_ge(s_ye, q - 1)
                    o = p_y[:, q % 2, 0:2 * P]
                    nc.tensor.matmul(o, hre[:, q, :], ot[:, q % 2, 0, :, :, :], start=True, stop=False, skip_group_check=True)
                    nc.tensor.matmul(o, him[:, q, :], ot[:, q % 2, 1, :, :, :], start=False, stop=False, skip_group_check=True)
                    for r in range(2):
                        last = nc.tensor.matmul(p_y[:, q % 2, r * P:(r + 1) * P], uT[:, 2 * q + r, :], mT[:, 2 * q + r, :, :],
                                                start=False, stop=(r == 1), skip_group_check=True)
                    last.then_inc(s_y, 1)
                for t in range(TC):
                    pe.wait_ge(s_g, t + 1)
                    if t >= 2:
                        pe.wait_ge(s_te, t - 1)
                    for m in range(M2):
                        last = nc.tensor.transpose(p_t[:, t % 2, m, :], za[:, t, m * P:(m + 1) * P], ident[:, :])
                    last.then_inc(s_t, 1)

            @block.vector
            def _(v):
                link = Chain(v, s_v)
                v.wait_ge(s_in, 16)
                link(nc.vector.tensor_tensor(za[:, :, :], za[:, :, :], bc(dsk[:, :], TC, 1), ALU.mult))

                def coefficients(q):
                    if q >= 2:
                        v.wait_ge(s_y, q - 1)
                    ar, ai = (bc(bc(pw[k][:, 1:, q], 2, 1), SC, 3) for k in range(2))
                    cr, ci = (bc(c[:, q, :, :], TC, 2) for c in (cre, cim))
                    o = ot[:, q % 2]
                    link(nc.vector.tensor_tensor(t1[:, :, :, :], ar, cr, ALU.mult))
                    link(nc.vector.tensor_tensor(t2[:, :, :, :], ai, ci, ALU.mult))
                    link(nc.vector.tensor_tensor(o[:, 0], t1[:, :, :, :], t2[:, :, :, :], ALU.add))
                    link(nc.vector.tensor_tensor(t1[:, :, :, :], ar, ci, ALU.mult))
                    link(nc.vector.tensor_tensor(t2[:, :, :, :], ai, cr, ALU.mult))
                    nc.vector.tensor_tensor(o[:, 1], t1[:, :, :, :], t2[:, :, :, :], ALU.subtract).then_inc(s_ot, 1)
                    v.wait_ge(s_ot, q + 1)

                for q in range(NQ + 1):
                    if q < NQ:
                        coefficients(q)
                    if q >= 1:
                        u = q - 1
                        v.wait_ge(s_y, u + 1)
                        z = za[:, :, u * 2 * SC:(u + 1) * 2 * SC].rearrange("p t (r h) -> p r t h", r=2)
                        nc.vector.tensor_tensor(z, p_y[:, u % 2, 0:2 * P].rearrange("p (r t h) -> p r t h", r=2, t=TC), z,
                                                ALU.add).then_inc(s_ye, 1)
                for t in range(TC):
                    v.wait_ge(s_t, t + 1)
                    nc.vector.tensor_copy(yT[:, :, t * P:(t + 1) * P], p_t[:, t % 2, :, :]).then_inc(s_te, 1)

            @block.scalar
            def _(act):
                act.wait_ge(s_ye, NQ)
                for t in range(TC):
                    nc.scalar.activation(za[:, t, :], za[:, t, :], ACT.Gelu_apprx_tanh).then_inc(s_g, 1)


def glu_close(nc, yT, sg, yaT):
    with nc.semaphore("gc_s") as s_m:
        with nc.Block() as block:
            @block.vector
            def _(v):
                for m in range(M2):
                    nc.vector.tensor_tensor(yaT[:, m, :].rearrange("p (c t) -> p t c", t=TC),
                                            yT[:, m, :].rearrange("p (t c) -> p t c", t=TC),
                                            sg[:, m, :].rearrange("p (t c) -> p t c", t=TC), ALU.mult).then_inc(s_m, 1)
                v.wait_ge(s_m, M2)


def spatial_gating(nc, u_rows, v_rows, ln_g, ln_b, w_s, b_s, ident, tril, ybT):
    with ExitStack() as ctx:
        def sb(name, shape):
            return ctx.enter_context(nc.sbuf_tensor(f"sg_{name}", shape, F32))

        def sem(name):
            return ctx.enter_context(nc.semaphore(f"sg_{name}"))

        u, vv = sb("u", [P, T, W2]), sb("v", [P, T, W2])
        lg, lb = sb("lg", [P, W2]), sb("lb", [P, W2])
        ws, wsT = sb("ws", [P, SH, P]), sb("wsT", [P, SH, P])
        br, bs = sb("br", [SH, P]), sb("bs", [P, SH])
        st, ag = sb("st", [P, T, 6]), sb("ag", [P, T, 2])
        sd = sb("sd", [P, T])
        p_w = ctx.enter_context(nc.psum_tensor("sg_w", [P, SH, P], F32))
        p_b = ctx.enter_context(nc.psum_tensor("sg_b", [P, 512], F32))
        p_x = ctx.enter_context(nc.psum_tensor("sg_x", [P, 2, T, SHD], F32))
        p_t = ctx.enter_context(nc.psum_tensor("sg_t", [P, 2, M2, P], F32))
        s_u, s_w, s_b, s_l = sem("iu"), sem("iw"), sem("ib"), sem("il")
        s_vt = [sem(f"v{t}") for t in range(T)]
        s_v, s_wm, s_wt, s_ag, s_sd, s_ln, s_x, s_y, s_t, s_te, s_wc = (
            sem(k) for k in ("v", "wm", "wt", "ag", "sd", "ln", "x", "y", "t", "te", "wc"))
        with nc.Block() as block:
            @block.sync
            def _(sp):
                sp.dma_start(ws[:, :, :], w_s.rearrange("h t s -> t h s")).then_inc(s_w, 16)
                sp.dma_start(br[:, :], b_s).then_inc(s_b, 16)
                sp.dma_start(lg[:, :], ln_g.partition_broadcast(P)).then_inc(s_l, 16)
                sp.dma_start(lb[:, :], ln_b.partition_broadcast(P)).then_inc(s_l, 16)
                for t in range(T):
                    sp.dma_start(vv[:, t, :], v_rows(t)).then_inc(s_vt[t], 16)
                for t in range(T):
                    sp.dma_start(u[:, t, :], u_rows(t)).then_inc(s_u, 16)

            @block.tensor
            def _(pe):
                pe.wait_ge(s_b, 16)
                nc.tensor.transpose(p_b[:, 0:SH], br[:, :], ident[0:SH, 0:SH]).then_inc(s_wt, 1)
                pe.wait_ge(s_wm, 1)
                for h in range(SH):
                    last = nc.tensor.transpose(p_w[:, h, :], ws[:, h, :], ident[:, :])
                last.then_inc(s_wt, 1)
                pe.wait_ge(s_wc, 2)
                pe.wait_ge(s_ln, T)
                for h in range(SH):
                    if h >= 2:
                        pe.wait_ge(s_y, h - 1)
                    nc.tensor.matmul(p_x[:, h % 2, :, :], wsT[:, h, :], vv[:, :, h * SHD:(h + 1) * SHD],
                                     start=True, stop=True).then_inc(s_x, 1)
                pe.wait_ge(s_y, SH)
                for t in range(T):
                    if t >= 2:
                        pe.wait_ge(s_te, t - 1)
                    for m in range(M2):
                        last = nc.tensor.transpose(p_t[:, t % 2, m, :], u[:, t, m * P:(m + 1) * P], ident[:, :])
                    last.then_inc(s_t, 1)

            @block.scalar
            def _(act):
                act.wait_ge(s_ag, 1)
                nc.scalar.activation(sd[:, :], sd[:, :], ACT.Sqrt).then_inc(s_sd, 1)
                for t in range(T):
                    act.wait_ge(s_t, t + 1)
                    nc.scalar.activation(ybT[:, :, t * P:(t + 1) * P], p_t[:, t % 2, :, :], ACT.Copy).then_inc(s_te, 1)

            @block.vector
            def _(v):
                link = Chain(v, s_v)
                v.wait_ge(s_w, 16)
                nc.vector.tensor_tensor(ws[:, :, :], ws[:, :, :], bc(tril[:, :], SH, 1), ALU.mult).then_inc(s_wm, 1)
                for t in range(T):
                    v.wait_ge(s_vt[t], 16)
                    link(nc.vector.bn_stats(st[:, t, :], vv[:, t, :]))
                    last = nc.vector.bn_aggr(ag[:, t, :], st[:, t, :])
                link(last)
                nc.vector.tensor_scalar(sd[:, :], ag[:, :, 1], LN_EPS, None, ALU.add).then_inc(s_ag, 1)
                v.wait_ge(s_wt, 2)
                nc.vector.tensor_copy(bs[:, :], p_b[:, 0:SH]).then_inc(s_wc, 1)
                nc.vector.tensor_copy(wsT[:, :, :], p_w[:, :, :]).then_inc(s_wc, 1)
                v.wait_ge(s_sd, 1)
                link(nc.vector.reciprocal(sd[:, :], sd[:, :]))
                v.wait_ge(s_l, 32)
                for t in range(T):
                    link(nc.vector.tensor_scalar(vv[:, t, :], vv[:, t, :], ag[:, t, 0:1], sd[:, t:t + 1], ALU.subtract, ALU.mult))
                    link(nc.vector.tensor_tensor(vv[:, t, :], vv[:, t, :], lg[:, :], ALU.mult))
                    nc.vector.tensor_tensor(vv[:, t, :], vv[:, t, :], lb[:, :], ALU.add).then_inc(s_ln, 1)
                v.wait_ge(s_u, 16 * T)
                v.wait_ge(s_wc, 2)
                for h in range(SH):
                    v.wait_ge(s_x, h + 1)
                    z = u[:, :, h * SHD:(h + 1) * SHD]
                    nc.vector.scalar_tensor_tensor(out=z, in0=p_x[:, h % 2, :, :], scalar=bs[:, h:h + 1], in1=z,
                                                   op0=ALU.add, op1=ALU.mult).then_inc(s_y, 1)


def merge(nc, xnT, yaT, ybT, w_gate, b_gate, w_a, w_b, mT):
    with ExitStack() as ctx:
        wg = ctx.enter_context(nc.sbuf_tensor("mg_wg", [P, 2, 2, J, 512], F32))
        wb = ctx.enter_context(nc.sbuf_tensor("mg_wb", [P, 2, 2, M2, 512], F32))
        gs = ctx.enter_context(nc.sbuf_tensor("mg_gs", [P, 2, 2, 512], F32))
        acc = ctx.enter_context(nc.psum_tensor("mg_acc", [P, 2, 4, 512], F32))
        s_w = [ctx.enter_context(nc.semaphore(f"mg_w{n}")) for n in range(2)]
        s_mm, s_g, s_v, s_o = (ctx.enter_context(nc.semaphore(f"mg_{k}")) for k in ("mm", "g", "v", "o"))
        steps = [(m, h) for m in range(D // P) for h in range(2)]
        with nc.Block() as block:
            @block.sync
            def _(sp):
                for n in range(2):
                    for k in range(2):
                        at = k * D + n * 512
                        sp.dma_start(wg[:, n, k, :, :], w_gate[:, at:at + 512].rearrange("(p j) n -> p j n", j=J)).then_inc(s_w[n], 16)
                    for k, w in enumerate((w_a, w_b)):
                        sp.dma_start(wb[:, n, k, :, :], w[:, n * 512:(n + 1) * 512].rearrange("(m p) n -> p m n", p=P)).then_inc(s_w[n], 16)

            @block.tensor
            def _(pe):
                for i, (m, h) in enumerate(steps):
                    n, c = m // 4, slice((m % 4) * P, (m % 4 + 1) * P)
                    tok = slice(h * 512, (h + 1) * 512)
                    if i % 8 == 0:
                        pe.wait_ge(s_w[n], 64)
                    if i >= 2:
                        pe.wait_ge(s_o, i - 1)
                    for k in range(2):
                        for j in range(J):
                            last = nc.tensor.matmul(acc[:, i % 2, k, :], wg[:, n, k, j, c], xnT[:, j, tok], start=(j == 0), stop=(j == J - 1))
                    last.then_inc(s_mm, 1)
                    for k, y in enumerate((yaT, ybT)):
                        for j in range(M2):
                            last = nc.tensor.matmul(acc[:, i % 2, 2 + k, :], wb[:, n, k, j, c], y[:, j, tok], start=(j == 0), stop=(j == M2 - 1))
                    last.then_inc(s_mm, 1)

            @block.scalar
            def _(act):
                for i, (m, h) in enumerate(steps):
                    act.wait_ge(s_mm, 2 * i + 1)
                    if i >= 2:
                        act.wait_ge(s_o, i - 1)
                    for k in range(2):
                        b = k * (D // P) + m
                        nc.scalar.activation(gs[:, i % 2, k, :], acc[:, i % 2, k, :], ACT.Sigmoid, bias=b_gate[:, b:b + 1]).then_inc(s_g, 1)

            @block.vector
            def _(v):
                link = Chain(v, s_v)
                for i, (m, h) in enumerate(steps):
                    v.wait_ge(s_mm, 2 * i + 2)
                    v.wait_ge(s_g, 2 * i + 2)
                    for k in range(2):
                        last = nc.vector.tensor_tensor(gs[:, i % 2, k, :], acc[:, i % 2, 2 + k, :], gs[:, i % 2, k, :], ALU.mult)
                    link(last)
                    nc.vector.tensor_tensor(mT[:, m, h * 512:(h + 1) * 512], gs[:, i % 2, 0, :], gs[:, i % 2, 1, :],
                                            ALU.add).then_inc(s_o, 1)


def load(nc, tag, dst, src):
    with nc.semaphore(f"{tag}_s") as s_ld:
        with nc.Block() as block:
            @block.sync
            def _(sp):
                sp.dma_start(dst, src).then_inc(s_ld, 16)
                sp.wait_ge(s_ld, 16)


def mixer2_phase(nc, h_in, mod, norm1, w_in, w_gate, b_gate, a_re, a_im, b_re, b_im, c_re, c_im, s_d, log_step,
                 w_glu, b_glu, ln_g, ln_b, sgu_w, sgu_b, w_a, w_b, w_out, h_out):
    h_t, out_t = (a.rearrange("(t p) d -> t p d", p=P) for a in (h_in, h_out))
    w_v = w_in.rearrange("(p j) n -> p j n", j=J)
    u_dram = nc.dram_tensor("x2_u", (SEQ, W2), F32, kind="Internal").ap().rearrange("(t p) d -> t p d", p=P)
    v_dram = nc.dram_tensor("x2_v", (SEQ, W2), F32, kind="Internal").ap().rearrange("(t p) d -> t p d", p=P)
    za_dram = nc.dram_tensor("x2_za", (P, TC, W2), F32, kind="Internal").ap()

    with ExitStack() as top:
        def sb(name, shape, to=top):
            return to.enter_context(nc.sbuf_tensor(f"x2_{name}", shape, F32))

        ident, tril = sb("ident", [P, P]), sb("tril", [P, P])
        make_masks(nc, "x2m", [(ident, ALU.is_equal, 1), (tril, ALU.is_ge, -1)])
        bcol = sb("bcol", [P, 2 * D // P + M2])
        transpose_rows(nc, "x2c", [b_gate.rearrange("(m p) -> m p", p=P), b_glu.rearrange("(m p) -> m p", p=P)],
                       2 * D // P + M2, ident, bcol[:, :])
        mT = sb("mT", [P, D // P, SEQ])
        with ExitStack() as mid:
            xnT = sb("xnT", [P, J, SEQ], mid)
            norm_transpose(nc, "x2n", lambda t: h_t[t], [(T, norm1, mod[D:2 * D], mod[0:D])], ident, xnT)
            project_rows(nc, "x2v", xnT, [w_v[:, :, W2:2 * W2], w_v[:, :, 2 * W2:3 * W2]], ACT.Gelu_apprx_tanh,
                         lambda n, t: (u_dram, v_dram)[n][t])
            project_rows(nc, "x2a", None, [w_v[:, :, 0:W2]], ACT.Copy, lambda n, t: za_dram[:, t, :],
                         lhs=lambda j, t: xnT[:, j, t::TC])
            yaT, ybT = sb("yaT", [P, M2, SEQ], mid), sb("ybT", [P, M2, SEQ], mid)
            spatial_gating(nc, lambda t: u_dram[t], lambda t: v_dram[t], ln_g, ln_b, sgu_w, sgu_b, ident, tril, ybT)
            with ExitStack() as s5:
                pw = [sb(f"pw{k}", [P, TC + 1, NQ], s5) for k in range(2)]
                ph = sb("ph", [P, 3, NQ], s5)
                phase8, rho8 = (ph[:, 0, :], ph[:, 1, :]), ph[:, 2, :]
                cre, cim = (sb(f"c{k}", [P, NQ, 2, SC], s5) for k in ("re", "im"))
                uT, msT = sb("uT", [P, SG, P], s5), sb("msT", [P, SG, TC, SC], s5)
                hre, him = (sb(f"h{k}", [P, NQ, P], s5) for k in ("re", "im"))
                with ExitStack() as st:
                    wre, wim = (sb(f"w{k}", [P, NQ, 2 * TC - 1, SC], st) for k in ("re", "im"))
                    s5_coefficients(nc, a_re, a_im, b_re, b_im, c_re, c_im, log_step, ident, pw, phase8, rho8, wre, wim, cre, cim, mT)
                    bufs = [mT[:, 2 * k:2 * k + 2, :].rearrange("p a (b c) -> p (a b) c", c=P) for k in range(3)]
                    z_re = mT[:, 6:8, :].rearrange("p a (b c) -> p (a b) c", c=P)
                    z_im = yaT[:, 0:2, :].rearrange("p a (b c) -> p (a b) c", c=P)
                    za1 = sb("za1", [P, TC, W2], st)
                    load(nc, "x2l1", za1[:, :, :], za_dram)
                    s5_states(nc, za1, ident, pw, phase8, rho8, wre, wim, cre, cim, uT, msT, hre[:, :, :], him[:, :, :],
                              z_re, z_im, *bufs)
                with ExitStack() as st:
                    za2, yT = sb("za2", [P, TC, W2], st), sb("yT", [P, M2, SEQ], st)
                    load(nc, "x2l2", za2[:, :, :], za_dram)
                    s5_outputs(nc, za2, ident, s_d, pw, cre, cim, uT, msT, hre, him, yT)
                    sg = mT[:, 0:M2, :]
                    project_channels(nc, "x2g", yT, M2, [w_glu.rearrange("(m p) n -> p m n", p=P)], ACT.Sigmoid,
                                     bcol[:, 2 * D // P:], lambda m, h: sg[:, m, h * 512:(h + 1) * 512])
                    glu_close(nc, yT, sg, yaT)
            merge(nc, xnT, yaT, ybT, w_gate, bcol, w_a, w_b, mT)
        mix_out(nc, "x2o", [mT], [w_out.rearrange("(m p) n -> p m n", p=P)], lambda t: h_t[t], mod[2 * D:3 * D],
                lambda t: out_t[t])


def free_semaphores(nc):
    used = list(nc.released_uncleared_semaphores)
    with nc.Block() as block:
        @block.gpsimd
        def _(pool):
            pool.sem_clear(range(min(used), max(used) + 1))


def two_blocks(nc, i, out):
    with ExitStack() as ctx:
        pool_dma = [ctx.enter_context(nc.semaphore(f"pool_dma{k}")) for k in range(2 * POOL_DMA_SEMAPHORES)]
        run_blocks(nc, i, out, pool_dma)


def run_blocks(nc, i, out, pool_dma):
    mod1 = nc.dram_tensor("mod1", (2, 6 * D), F32, kind="Internal").ap()
    mod2 = nc.dram_tensor("mod2", (1, 6 * D), F32, kind="Internal").ap()
    stage = [nc.dram_tensor(f"stage{k}", (SEQ, D), F32, kind="Internal").ap() for k in range(3)]
    mod_phase(nc, [([i["c"][0], i["c_ctx"]], i["w_mod"][0], i["b_mod"][0], mod1),
                   ([i["c_2"][0]], i["w_ada_2"][0], i["b_ada_2"][0], mod2)])
    mixer1_phase(nc, i["x"][0], i["ctx"][0], mod1, *(i[n][0] for n in (
        "norm1", "w_in", "conv_w", "conv_b", "dt_bias", "a_log", "d_skip", "ssd_norm", "w_four", "w_out")),
        i["dft"], i["rot"], stage[0])
    free_semaphores(nc)
    moe_phase(nc, "m1", stage[0], mod1[0], *(i[n][0] for n in (
        "norm2", "w_rg", "b_rg", "w_re", "b_re", "w_eg", "w_eu", "w_ed")), i["final_norm"], stage[1], pool_dma[:POOL_DMA_SEMAPHORES])
    free_semaphores(nc)
    mixer2_phase(nc, stage[1], mod2[0], *(i[n + "_2"][0] for n in (
        "norm1_g", "w_in", "w_gate", "b_gate", "ssm_a_re", "ssm_a_im", "ssm_b_re", "ssm_b_im", "ssm_c_re", "ssm_c_im",
        "ssm_d", "ssm_log_step", "w_glu", "b_glu", "sgu_ln_g", "sgu_ln_b", "sgu_w", "sgu_b", "w_branch_a", "w_branch_b",
        "w_out")), stage[2])
    free_semaphores(nc)
    moe_phase(nc, "m2", stage[2], mod2[0], *(i[n + "_2"][0] for n in (
        "norm2_g", "w_router_group", "b_router_group", "w_router_expert", "b_router_expert", "w1", "w3", "w2")),
        i["norm_f_g_2"], out[0], pool_dma[POOL_DMA_SEMAPHORES:])


def kernel(**inputs):
    import numpy as _np
    import concourse.bacc as _bacc
    from concourse import mybir as _mybir
    from concourse.bass_utils import run_bass_kernel_spmd as _run

    nc = _bacc.Bacc("TRN2", target_bir_lowering=False, num_devices=1)
    arrays, args = {}, {}
    dft, rot = dft_tables()
    for name, a in list(inputs.items()) + [("dft", dft), ("rot", rot)]:
        a = _np.ascontiguousarray(a)
        arrays[f"in_{name}_dram"] = a
        args[name] = nc.dram_tensor(f"in_{name}_dram", a.shape, _mybir.dt.from_np(a.dtype), kind="ExternalInput").ap()
    out = nc.dram_tensor("out_0_dram", (1, SEQ, D), F32, kind="ExternalOutput").ap()
    two_blocks(nc, args, out)
    r = _run(nc, [arrays], core_ids=[0])
    return r.results[0]["out_0_dram"]
```

```python
from contextlib import ExitStack

import concourse.bass as bass
from concourse import mybir

P = 128
D = 1024
SEQ = 1024
T = SEQ // P
J = D // P
N_EXPERTS = 32
NBLK = 2 * SEQ // P + N_EXPERTS
EPS = 1e-6
NEG = -1e30
POOL_DMA_SEMAPHORES = 9

F32 = mybir.dt.float32
F32R = mybir.dt.float32r
I32 = mybir.dt.int32
U32 = mybir.dt.uint32
ALU = mybir.AluOpType
ACT = mybir.ActivationFunctionType
AX = mybir.AxisListType


def bc(ap, n, axis):
    wide = ap.unsqueeze(axis)
    shape = list(wide.shape)
    shape[axis] = n
    return wide.broadcast_to(shape)


def moe_phase(nc, tag, x_in, mod, norm_w, w_rg, b_rg, w_re, b_re, w_gate, w_up, w_down, final_w, x_out, pool_dma):
    xr_dram = nc.dram_tensor(f"{tag}_xr", (SEQ, D), F32, kind="Internal").ap()
    yrows = nc.dram_tensor(f"{tag}_yrows", ((NBLK + 2) * P, D), F32, kind="Internal").ap()
    slot_tok = nc.dram_tensor(f"{tag}_slot_tok", ((NBLK + 2) * P, 1), I32, kind="Internal").ap()
    blk_dram = nc.dram_tensor(f"{tag}_blk", (1, NBLK + 16), I32, kind="Internal").ap()
    x_t = x_in.rearrange("(t p) d -> t p d", p=P)
    out_t = x_out.rearrange("(t p) d -> t p d", p=P)
    xr_t = xr_dram.rearrange("(t p) d -> t p d", p=P)
    NE, NG = w_gate.shape[0], w_re.shape[0]
    EG = NE // NG
    NF = w_gate.shape[2]
    JF = NF // P

    s_zero, s_sc, s_idx, *rest = pool_dma
    s_xb, s_ga = rest[0:2], rest[2:6]
    with ExitStack() as ctx:
        def sb(name, shape, dt=F32):
            return ctx.enter_context(nc.sbuf_tensor(f"{tag}_{name}", shape, dt))

        def sem(name):
            return ctx.enter_context(nc.semaphore(f"{tag}_{name}"))

        X = sb("X", [P, T, D])
        ident = sb("ident", [P, P])
        gate1 = sb("gate1", [P, T])
        gate2 = sb("gate2", [P, T])
        pos1 = sb("pos1", [P, T], I32)
        pos2 = sb("pos2", [P, T], I32)
        ss = sb("ss", [P, T])
        rstd = sb("rstd", [P, T])
        junk = sb("junk", [P, D])

        with ExitStack() as c2:
            def sb2(name, shape, dt=F32):
                return c2.enter_context(nc.sbuf_tensor(f"{tag}_{name}", shape, dt))

            def ps2(name, shape, dt=F32):
                return c2.enter_context(nc.psum_tensor(f"{tag}_{name}", shape, dt))

            xs = sb2("xs", [P, T, D])
            xT = sb2("xT", [P, 2, J, P])
            wr = sb2("wr", [P, J, NG + NE])
            br = sb2("br", [P, NG + NE])
            nrow = sb2("nrow", [P, D])
            srow = sb2("srow", [P, D])
            shrow = sb2("shrow", [P, D])
            SU = sb2("SU", [P, P])
            ones = sb2("ones", [P, P])
            iota_e = sb2("iota_e", [P, NE])
            iota_b = sb2("iota_b", [1, NBLK])
            tokid = sb2("tokid", [P, T], I32)
            zero_i = sb2("zero_i", [P, NBLK + 2], I32)
            L = sb2("L", [P, T, 8 + NE])
            mg = sb2("mg", [P, T, 8])
            ig = sb2("ig", [P, T, 8], U32)
            igf = sb2("igf", [P, T, 8])
            pen = sb2("pen", [P, T, NG])
            LE = sb2("LE", [P, T, NE])
            me = sb2("me", [P, T, 8])
            ie = sb2("ie", [P, T, 8], U32)
            ief = sb2("ief", [P, T, 8])
            dg = sb2("dg", [P, T, NG])
            eg = sb2("eg", [P, T, NG])
            sg = sb2("sg", [P, T])
            de = sb2("de", [P, T])
            e2 = sb2("e2", [P, T])
            den = sb2("den", [P, T])
            M1 = sb2("M1", [P, T, NE])
            M2 = sb2("M2", [P, T, NE])
            M = sb2("M", [P, T, NE])
            Tc = sb2("Tc", [P, T, NE])
            cnt = sb2("cnt", [P, NE])
            nb = sb2("nb", [P, NE])
            onese = sb2("onese", [P, NE])
            bend = sb2("bend", [P, NE])
            bst = sb2("bst", [P, NE])
            slot = sb2("slot", [P, T, NE])
            pr = sb2("pr", [P, T, NE])
            posf = sb2("posf", [P, T])
            cb = sb2("cb", [1, NBLK, NE])
            bef = sb2("bef", [1, NBLK + 16])
            bei = sb2("bei", [1, NBLK + 16], I32)
            ps_t = ps2("ps_t", [P, 2, J, P])
            ps_l = ps2("ps_l", [P, T, 64])
            ps_r = ps2("ps_r", [P, T, NE])
            ps_c = ps2("ps_c", [P, T, NE])

            s_x = [sem(f"x{i}") for i in range(T)]
            s_par = sem("par")
            s_const = sem("const")
            s_sq = sem("sq")
            s_var = sem("var")
            s_rstd = sem("rstd")
            s_sqrt = sem("sqrt")
            s_xm = sem("xm")
            s_xs = sem("xs")
            s_tr = sem("tr")
            s_xT = sem("xT")
            s_log = sem("log")
            s_d = sem("dchain")
            s_dg = sem("dg")
            s_eg = sem("eg")
            s_M = sem("M")
            s_rank = sem("rank")
            s_pos = sem("pos")
            s_blk = sem("blk")
            s_st = sem("st")

            with nc.Block() as block:
                @block.sync
                def _(sp):
                    for t in range(T):
                        sp.dma_start(X[:, t, :], x_t[t]).then_inc(s_x[t], 16)
                        if t == 0:
                            sp.dma_start(nrow[:, :], norm_w.partition_broadcast(P)).then_inc(s_par, 16)
                            sp.dma_start(srow[:, :], mod[4 * D:5 * D].partition_broadcast(P)).then_inc(s_par, 16)
                            sp.dma_start(shrow[:, :], mod[3 * D:4 * D].partition_broadcast(P)).then_inc(s_par, 16)
                            sp.dma_start(wr[:, :, 0:NG], w_rg.rearrange("(p j) g -> p j g", j=J)).then_inc(s_par, 16)
                            for g in range(NG):
                                sp.dma_start(wr[:, :, NG + g * EG:NG + (g + 1) * EG],
                                             w_re[g].rearrange("(p j) e -> p j e", j=J)).then_inc(s_par, 16)
                            sp.dma_start(br[:, 0:NG], b_rg.partition_broadcast(P)).then_inc(s_par, 16)
                            sp.dma_start(br[:, NG:NG + NE], b_re.rearrange("g e -> (g e)").partition_broadcast(P)).then_inc(s_par, 16)
                    for t in range(T):
                        sp.wait_ge(s_xs, t + 1)
                        sp.dma_start(xr_t[t], xs[:, t, :]).then_inc(s_st, 16)
                    sp.wait_ge(s_blk, 1)
                    sp.dma_start(blk_dram, bei[:, :]).then_inc(s_st, 16)
                    sp.wait_ge(s_st, 16 * (T + 1))

                @block.gpsimd
                def _(pool):
                    nc.gpsimd.iota(iota_e[:, :], [[1, NE]], base=0, channel_multiplier=0,
                                   allow_small_or_imprecise_dtypes=True).then_inc(s_const, 1)
                    nc.gpsimd.iota(iota_b[:, :], [[1, NBLK]], base=0, channel_multiplier=0,
                                   allow_small_or_imprecise_dtypes=True).then_inc(s_const, 1)
                    nc.gpsimd.iota(tokid[:, :], [[P, T]], base=0, channel_multiplier=1).then_inc(s_const, 1)
                    nc.gpsimd.memset(zero_i[:, :], 0).then_inc(s_const, 1)
                    nc.gpsimd.memset(ones[:, :], 1.0).then_inc(s_const, 1)
                    pool.wait_ge(s_const, 5)
                    nc.gpsimd.affine_select(out=SU[:, :], in_=ones[:, :], compare_op=ALU.is_gt, fill=0.0, base=0,
                                            pattern=[[1, P]], channel_multiplier=-1).then_inc(s_const, 1)
                    nc.gpsimd.affine_select(out=ident[:, :], in_=ones[:, :], compare_op=ALU.is_equal, fill=0.0,
                                            base=0, pattern=[[1, P]], channel_multiplier=-1).then_inc(s_const, 1)
                    pool.dma_start(slot_tok.rearrange("(p b) o -> p (b o)", p=P), zero_i[:, :]).then_inc(s_zero, 16)
                    pool.wait_ge(s_zero, 16)
                    for k, pos in enumerate((pos1, pos2)):
                        pool.wait_ge(s_pos, k + 1)
                        for t in range(T):
                            pool.indirect_dma_start(slot_tok, bass.IndirectOffsetOnAxis(ap=pos[:, t:t + 1], axis=0),
                                                    tokid[:, t:t + 1], None).then_inc(s_sc, 16)
                    pool.wait_ge(s_sc, 16 * 2 * T)

                @block.scalar
                def _(act):
                    for t in range(T + 2):
                        if t < T:
                            act.wait_ge(s_x[t], 16)
                            if t > 0:
                                act.wait_ge(s_sq, t)
                            nc.scalar.activation(junk[:, :], X[:, t, :], ACT.Square,
                                                 accum_out=ss[:, t:t + 1]).then_inc(s_sq, 1)
                            act.wait_ge(s_var, t + 1)
                            nc.scalar.activation(rstd[:, t:t + 1], ss[:, t:t + 1], ACT.Sqrt).then_inc(s_sqrt, 1)
                        if t >= 2:
                            u = t - 2
                            act.wait_ge(s_tr, u + 1)
                            if u >= 2:
                                act.wait_ge(s_log, u - 1)
                            nc.scalar.activation(xT[:, u % 2, :, :], ps_t[:, u % 2, :, :], ACT.Copy).then_inc(s_xT, 1)
                    act.wait_ge(s_dg, 1)
                    nc.scalar.activation(eg[:, :, :], dg[:, :, :], ACT.Exp).then_inc(s_eg, 1)
                    nc.scalar.activation(e2[:, :], de[:, :], ACT.Exp).then_inc(s_eg, 1)

                @block.tensor
                def _(pe):
                    pe.wait_ge(s_const, 7)
                    pe.wait_ge(s_par, 16 * (6 + NG))
                    for t in range(T + 1):
                        if t < T:
                            pe.wait_ge(s_xs, t + 1)
                            if t >= 2:
                                pe.wait_ge(s_xT, t - 1)
                            for j in range(J):
                                last = nc.tensor.transpose(ps_t[:, t % 2, j, :], xs[:, t, j::J], ident[:, :])
                            last.then_inc(s_tr, 1)
                        if t >= 1:
                            pe.wait_ge(s_xT, t)
                            for j in range(J):
                                last = nc.tensor.matmul(ps_l[:, t - 1, 0:NG + NE], xT[:, (t - 1) % 2, j, :], wr[:, j, :],
                                                        start=(j == 0), stop=(j == J - 1))
                            last.then_inc(s_log, 1)
                    pe.wait_ge(s_M, 1)
                    nc.tensor.matmul(ps_r[:, :, :], SU[:, :], M[:, :, :], start=True, stop=True).then_inc(s_rank, 1)
                    nc.tensor.matmul(ps_c[:, :, :], ones[:, :], M[:, :, :], start=True, stop=True).then_inc(s_rank, 1)

                @block.vector
                def _(v):
                    n = [0]

                    def link(ins):
                        n[0] += 1
                        ins.then_inc(s_d, 1)
                        v.wait_ge(s_d, n[0])

                    v.wait_ge(s_par, 16 * (6 + NG))
                    link(nc.vector.scalar_tensor_tensor(out=srow[:, :], in0=srow[:, :], scalar=1.0, in1=nrow[:, :],
                                                        op0=ALU.add, op1=ALU.mult))
                    nc.vector.memset(L[:, :, NG:8], NEG)
                    link(nc.vector.memset(onese[:, :], 1.0))
                    for t in range(T):
                        v.wait_ge(s_sq, t + 1)
                        nc.vector.tensor_scalar(ss[:, t:t + 1], ss[:, t:t + 1], 1.0 / D, EPS, ALU.mult, ALU.add).then_inc(s_var, 1)
                        if t >= 1:
                            v.wait_ge(s_xm, t)
                            nc.vector.tensor_tensor(xs[:, t - 1, :], xs[:, t - 1, :], shrow[:, :], ALU.add).then_inc(s_xs, 1)
                        v.wait_ge(s_sqrt, t + 1)
                        nc.vector.reciprocal(rstd[:, t:t + 1], rstd[:, t:t + 1]).then_inc(s_rstd, 1)
                        v.wait_ge(s_rstd, t + 1)
                        nc.vector.scalar_tensor_tensor(out=xs[:, t, :], in0=X[:, t, :], scalar=rstd[:, t:t + 1],
                                                       in1=srow[:, :], op0=ALU.mult, op1=ALU.mult).then_inc(s_xm, 1)
                    v.wait_ge(s_xm, T)
                    nc.vector.tensor_tensor(xs[:, T - 1, :], xs[:, T - 1, :], shrow[:, :], ALU.add).then_inc(s_xs, 1)
                    v.wait_ge(s_log, T)
                    nc.vector.tensor_tensor(L[:, :, 0:NG], ps_l[:, :, 0:NG], bc(br[:, 0:NG], T, 1), ALU.add)
                    link(nc.vector.tensor_tensor(L[:, :, 8:8 + NE], ps_l[:, :, NG:NG + NE],
                                                 bc(br[:, NG:NG + NE], T, 1), ALU.add))
                    for t in range(T):
                        last = nc.vector.max(mg[:, t, :], L[:, t, 0:8])
                    link(last)
                    for t in range(T):
                        last = nc.vector.max_index(ig[:, t, :], mg[:, t, :], L[:, t, 0:8])
                    link(last)
                    link(nc.vector.tensor_copy(igf[:, :, :], ig[:, :, :]))
                    link(nc.vector.tensor_tensor(pen[:, :, :], bc(iota_e[:, 0:NG], T, 1), bc(igf[:, :, 0], NG, 2), ALU.is_equal))
                    link(nc.vector.tensor_scalar(pen[:, :, :], pen[:, :, :], -1.0, -NEG, ALU.add, ALU.mult))
                    link(nc.vector.tensor_tensor(LE[:, :, :].rearrange("p t (g e) -> p t g e", g=NG),
                                                 L[:, :, 8:8 + NE].rearrange("p t (g e) -> p t g e", g=NG),
                                                 bc(pen[:, :, :], EG, 3), ALU.add))
                    for t in range(T):
                        last = nc.vector.max(me[:, t, :], LE[:, t, :])
                    link(last)
                    for t in range(T):
                        last = nc.vector.max_index(ie[:, t, :], me[:, t, :], LE[:, t, :])
                    link(last)
                    link(nc.vector.tensor_copy(ief[:, :, :], ie[:, :, :]))
                    nc.vector.tensor_tensor(dg[:, :, :], L[:, :, 0:NG], bc(mg[:, :, 0], NG, 2), ALU.subtract)
                    nc.vector.tensor_tensor(de[:, :], me[:, :, 1], me[:, :, 0], ALU.subtract).then_inc(s_dg, 1)
                    nc.vector.tensor_tensor(M1[:, :, :], bc(iota_e[:, :], T, 1), bc(ief[:, :, 0], NE, 2), ALU.is_equal)
                    link(nc.vector.tensor_tensor(M2[:, :, :], bc(iota_e[:, :], T, 1), bc(ief[:, :, 1], NE, 2), ALU.is_equal))
                    nc.vector.tensor_tensor(M[:, :, :], M1[:, :, :], M2[:, :, :], ALU.add).then_inc(s_M, 1)
                    v.wait_ge(s_eg, 2)
                    link(nc.vector.tensor_reduce(sg[:, :], eg[:, :, :], AX.X, ALU.add))
                    link(nc.vector.scalar_tensor_tensor(out=den[:, :], in0=e2[:, :], scalar=1.0, in1=sg[:, :],
                                                        op0=ALU.add, op1=ALU.mult))
                    link(nc.vector.reciprocal(gate1[:, :], den[:, :]))
                    link(nc.vector.tensor_tensor(gate2[:, :], gate1[:, :], e2[:, :], ALU.mult))
                    v.wait_ge(s_rank, 2)
                    link(nc.vector.memset(Tc[:, 0, :], 0.0))
                    for t in range(1, T):
                        link(nc.vector.tensor_tensor(Tc[:, t, :], Tc[:, t - 1, :], ps_c[:, t - 1, :], ALU.add))
                    link(nc.vector.tensor_tensor(cnt[:, :], Tc[:, T - 1, :], ps_c[:, T - 1, :], ALU.add))
                    link(nc.vector.tensor_scalar(nb[:, :], cnt[:, :], 0.0, None, ALU.is_gt))
                    for k in range(1, SEQ // P):
                        link(nc.vector.scalar_tensor_tensor(out=nb[:, :], in0=cnt[:, :], scalar=float(P * k), in1=nb[:, :],
                                                            op0=ALU.is_gt, op1=ALU.add))
                    link(nc.vector.tensor_tensor_scan(bend[:, :], onese[:, :], nb[:, :], 0.0, ALU.mult, ALU.add))
                    link(nc.vector.tensor_tensor(bst[:, :], bend[:, :], nb[:, :], ALU.subtract))
                    link(nc.vector.scalar_tensor_tensor(out=slot[:, :, :], in0=bc(bst[:, :], T, 1), scalar=float(P),
                                                        in1=Tc[:, :, :], op0=ALU.mult, op1=ALU.add))
                    link(nc.vector.tensor_tensor(slot[:, :, :], ps_r[:, :, :], slot[:, :, :], ALU.add))
                    for Mk, pos in ((M1, pos1), (M2, pos2)):
                        link(nc.vector.tensor_tensor(pr[:, :, :], Mk[:, :, :], slot[:, :, :], ALU.mult))
                        link(nc.vector.tensor_reduce(posf[:, :], pr[:, :, :], AX.X, ALU.add))
                        ins = nc.vector.tensor_copy(pos[:, :], posf[:, :])
                        ins.then_inc(s_pos, 1)
                        v.wait_ge(s_pos, 1 if pos is pos1 else 2)
                    link(nc.vector.tensor_tensor(cb[:, :, :], bc(bend[0:1, :], NBLK, 1), bc(iota_b[:, :], NE, 2), ALU.is_le))
                    link(nc.vector.tensor_reduce(bef[:, 0:NBLK], cb[:, :, :], AX.X, ALU.add))
                    link(nc.vector.tensor_scalar(bef[:, 0:NBLK], bef[:, 0:NBLK], float(NE - 1), None, ALU.min))
                    link(nc.vector.tensor_scalar(cb[:, 0, 0:NBLK // 2], iota_b[:, 0:NBLK:2], bend[0:1, NE - 1:NE], None, ALU.is_lt))
                    link(nc.vector.memset(bef[:, NBLK:NBLK + 16], 0.0))
                    link(nc.vector.tensor_reduce(bef[:, NBLK:NBLK + 1], cb[:, 0, 0:NBLK // 2], AX.X, ALU.add))
                    nc.vector.tensor_copy(bei[:, :], bef[:, :]).then_inc(s_blk, 1)

        with ExitStack() as c2:
            def sb2(name, shape, dt=F32):
                return c2.enter_context(nc.sbuf_tensor(f"{tag}_{name}", shape, dt))

            def ps2(name, shape, dt=F32):
                return c2.enter_context(nc.psum_tensor(f"{tag}_{name}", shape, dt))

            WF = J * NF // 2
            assert 2 * WF == JF * D
            raw = [sb2(f"raw{p}", [P, WF]) for p in range(6)]
            wh = [sb2(f"wh{k}", [P, WF], F32R) for k in range(4)]
            wl = [sb2(f"wl{k}", [P, WF], F32R) for k in range(4)]
            idx = [sb2(f"idx{r}", [P, 1], I32) for r in range(2)]
            xb = [sb2(f"xb{r}", [P, D]) for r in range(2)]
            xh = [sb2(f"xh{r}", [P, J, P], F32R) for r in range(2)]
            xl = [sb2(f"xl{r}", [P, J, P], F32R) for r in range(2)]
            sil = sb2("sil", [P, NF])
            hid = sb2("hid", [P, NF])
            hh = sb2("hh", [P, JF, P], F32R)
            hl = sb2("hl", [P, JF, P], F32R)
            yb = [sb2(f"yb{r}", [P, D]) for r in range(2)]
            zrow = sb2("zrow", [P, D])
            ps_x = ps2("ps_x", [P, J, P])
            ps_g = ps2("ps_g", [P, NF])
            ps_u = ps2("ps_u", [P, NF])
            ps_h = ps2("ps_h", [P, JF, P])
            ps_y = ps2("ps_y", [P, D])

            s_raw = [sem(f"raw{p}") for p in range(6)]
            s_hi, s_lo, s_used = sem("hi"), sem("lo"), sem("used")
            s_xtr, s_xh, s_xl = sem("xtr"), sem("xh"), sem("xl")
            s_sil, s_hid = sem("sil"), sem("hid")
            s_htr, s_hh, s_hl = sem("htr"), sem("hh"), sem("hl")
            s_yb = sem("yb")
            s_ys = [sem(f"ys{r}") for r in range(2)]
            s_one = sem("one")
            s_zr, s_zs = sem("zr"), sem("zs")

            w_dram = (w_gate.rearrange("e (p j) f -> e p (j f)", j=J), w_up.rearrange("e (p j) f -> e p (j f)", j=J),
                      w_down.rearrange("e (p j) f -> e p (j f)", j=JF))
            tok_b = slot_tok.rearrange("(b p) o -> b p o", p=P)
            y_b = yrows.rearrange("(b p) d -> b p d", p=P)

            def pairs(eng):
                return eng.value_load(blk_dram[0:1, NBLK:NBLK + 1], min_val=1, max_val=NBLK // 2)

            with nc.Block() as block:
                @block.sync
                def _(sp):
                    n2 = pairs(sp)
                    sp.sem_inc(s_lo, 6)
                    with sp.Fori(0, n2) as i:
                        for r in range(2):
                            e = sp.value_load(blk_dram[0:1, bass.ds(2 * i + r, 1)], min_val=0, max_val=NE - 1)
                            for p in range(6):
                                sp.wait_ge(s_lo, 12 * i + 6 * r + p + 1)
                                sp.dma_start(raw[p][:, :], w_dram[p // 2][e][:, p % 2 * WF:(p % 2 + 1) * WF]).then_inc(s_raw[p], 16)
                        sp.sem_inc(s_zs, 32)
                    for p in range(4):
                        sp.wait_ge(s_lo, 12 * n2 + p + 1)
                        sp.sem_inc(s_raw[p], 16)
                    sp.wait_ge(s_zr, 1)
                    with sp.Fori(n2, NBLK // 2 + 1) as i:
                        for r in range(2):
                            sp.dma_start(y_b[2 * i + r], zrow[:, :]).then_inc(s_zs, 16)
                    sp.wait_ge(s_zs, 32 * (NBLK // 2 + 1))

                @block.gpsimd
                def _(pool):
                    n2 = pairs(pool)

                    def gather(b, r):
                        pool.wait_ge(s_xtr, b + 1)
                        pool.sem_inc(s_one, 1)
                        pool.dma_start(idx[r][:, :], tok_b[b]).then_inc(s_idx, 16)
                        pool.wait_ge(s_idx, 16 * b + 16)
                        pool.sem_inc(s_one, 1)
                        pool.indirect_dma_start(xb[r][:, :], None, xr_dram,
                                                bass.IndirectOffsetOnAxis(ap=idx[r][:, :], axis=0)).then_inc(s_xb[r], 16)

                    with pool.Fori(0, n2) as i:
                        for r in range(2):
                            gather(2 * i + r, r)
                    gather(pool.snap(2 * n2), 0)
                    pool.wait_ge(s_xb[0], 16 * n2 + 16)
                    pool.sem_inc(s_one, 1)

                @block.tensor
                def _(pe):
                    n2 = pairs(pe)
                    pe.sem_inc(s_xtr, 2)
                    pe.sem_inc(s_used, 4)
                    pe.sem_inc(s_htr, 1)

                    def rows_T(b, r, turn):
                        pe.wait_ge(s_xb[r], 16 * turn + 16)
                        pe.wait_ge(s_xl, b + 1)
                        for j in range(J):
                            last = nc.tensor.transpose(ps_x[:, j, :], xb[r][:, j::J], ident[:, :])
                        last.then_inc(s_xtr, 1)

                    def product(out, a_h, a_l, q, k, half, n_j, width):
                        w_h = wh[k][:, :].rearrange("p (j f) -> p j f", f=width)
                        w_l = wl[k][:, :].rearrange("p (j f) -> p j f", f=width)
                        pe.wait_ge(s_lo, q + 7)
                        for c in range(0, width, 512):
                            o = out[:, c:c + 512]
                            for i in range(n_j // 2):
                                j = half * n_j // 2 + i
                                nc.tensor.matmul(o, a_h[:, j, :], w_h[:, i, c:c + 512], start=(j == 0), stop=False)
                                nc.tensor.matmul(o, a_h[:, j, :], w_l[:, i, c:c + 512], start=False, stop=False)
                                last = nc.tensor.matmul(o, a_l[:, j, :], w_h[:, i, c:c + 512], start=False, stop=(j == n_j - 1))
                        last.then_inc(s_used, 1)

                    rows_T(0, 0, 0)
                    with pe.Fori(0, n2) as i:
                        for r in range(2):
                            b = 2 * i + r
                            q = 12 * i + 6 * r
                            pe.wait_ge(s_xl, b + 2)
                            pe.wait_ge(s_sil, b + 1)
                            for h in range(2):
                                product(ps_g, xh[r], xl[r], q + h, (2 * r + h) % 4, h, J, NF)
                            pe.wait_ge(s_hid, b + 1)
                            for h in range(2):
                                product(ps_u, xh[r], xl[r], q + 2 + h, (2 * r + 2 + h) % 4, h, J, NF)
                            rows_T(b + 1, 1 - r, i + r)
                            pe.wait_ge(s_hid, b + 2)
                            pe.wait_ge(s_hl, b + 1)
                            for j in range(JF):
                                last = nc.tensor.transpose(ps_h[:, j, :], hid[:, j::JF], ident[:, :])
                            last.then_inc(s_htr, 1)
                            pe.wait_ge(s_hl, b + 2)
                            pe.wait_ge(s_yb, b + 1)
                            for h in range(2):
                                product(ps_y, hh, hl, q + 4 + h, (2 * r + 4 + h) % 4, h, JF, D)

                @block.vector
                def _(v):
                    n2 = pairs(v)
                    for s in (s_xl, s_hid, s_hl):
                        v.sem_inc(s, 1)
                    nc.vector.memset(zrow[:, :], 0.0).then_inc(s_zr, 1)

                    def rows_low(b, r):
                        v.wait_ge(s_xh, b + 1)
                        nc.vector.tensor_tensor(xl[r][:, :, :], ps_x[:, :, :], xh[r][:, :, :].bitcast(F32),
                                                ALU.subtract).then_inc(s_xl, 1)

                    def low(q, p, k):
                        v.wait_ge(s_hi, q + 1)
                        nc.vector.tensor_tensor(wl[k][:, :], raw[p][:, :], wh[k][:, :].bitcast(F32), ALU.subtract).then_inc(s_lo, 1)

                    rows_low(0, 0)
                    for p in range(4):
                        low(p, p, p)
                    with v.Fori(0, n2) as i:
                        for r in range(2):
                            b = 2 * i + r
                            q = 12 * i + 6 * r
                            for p in (4, 5):
                                low(q + p, p, (2 * r + p) % 4)
                            v.wait_ge(s_sil, b + 2)
                            v.wait_ge(s_used, q + 8)
                            v.wait_ge(s_htr, b + 1)
                            nc.vector.tensor_tensor(hid[:, :], ps_u[:, :], sil[:, :], ALU.mult).then_inc(s_hid, 1)
                            rows_low(b + 1, 1 - r)
                            v.wait_ge(s_hh, b + 1)
                            nc.vector.tensor_tensor(hl[:, :, :], ps_h[:, :, :], hh[:, :, :].bitcast(F32), ALU.subtract).then_inc(s_hl, 1)
                            for p in range(4):
                                low(q + 6 + p, p, (2 * r + 6 + p) % 4)

                @block.scalar
                def _(act):
                    n2 = pairs(act)
                    for s in (s_sil, s_yb):
                        act.sem_inc(s, 1)
                    act.sem_inc(s_ys[0], 16)
                    act.sem_inc(s_ys[1], 16)

                    def high(q, p, k, turn):
                        act.wait_ge(s_raw[p], 16 * turn + 16)
                        act.wait_ge(s_used, q + 1)
                        nc.scalar.activation(wh[k][:, :], raw[p][:, :], ACT.Copy).then_inc(s_hi, 1)

                    def rows_high(b, r):
                        act.wait_ge(s_xtr, b + 3)
                        nc.scalar.activation(xh[r][:, :, :], ps_x[:, :, :], ACT.Copy).then_inc(s_xh, 1)

                    rows_high(0, 0)
                    for p in range(4):
                        high(p, p, p, 0)
                    with act.Fori(0, n2) as i:
                        for r in range(2):
                            b = 2 * i + r
                            q = 12 * i + 6 * r
                            high(q + 4, 4, (2 * r + 4) % 4, b)
                            act.wait_ge(s_used, q + 6)
                            act.wait_ge(s_hid, b + 1)
                            nc.scalar.activation(sil[:, :], ps_g[:, :], ACT.Silu).then_inc(s_sil, 1)
                            high(q + 5, 5, (2 * r + 5) % 4, b)
                            high(q + 6, 0, (2 * r + 6) % 4, b + 1)
                            rows_high(b + 1, 1 - r)
                            act.wait_ge(s_htr, b + 2)
                            nc.scalar.activation(hh[:, :, :], ps_h[:, :, :], ACT.Copy).then_inc(s_hh, 1)
                            for p in (1, 2, 3):
                                high(q + 6 + p, p, (2 * r + 6 + p) % 4, b + 1)
                            act.wait_ge(s_used, q + 10)
                            act.wait_ge(s_ys[r], 16 * i + 16)
                            nc.scalar.activation(yb[r][:, :], ps_y[:, :], ACT.Copy).then_inc(s_yb, 1)
                            act.wait_ge(s_yb, b + 2)
                            act.dma_start(y_b[b], yb[r][:, :]).then_inc(s_ys[r], 16)
                    act.wait_ge(s_ys[0], 16 * n2 + 16)
                    act.wait_ge(s_ys[1], 16 * n2 + 16)
                    act.sem_inc(s_one, 1)

        with ExitStack() as c2:
            def sb2(name, shape, dt=F32):
                return c2.enter_context(nc.sbuf_tensor(f"{tag}_{name}", shape, dt))

            GA = len(s_ga)
            ya = sb2("ya", [P, T, D])
            yc = sb2("yc", [P, T, D])
            g2row = sb2("g2row", [P, D])
            frow = sb2("frow", [P, D])
            s_row = sem("row")
            s_a = sem("a")
            s_sd = sem("sd")
            s_cm = sem("cm")
            s_q = sem("q")
            s_k = sem("k")
            s_f = sem("f")
            s_out = sem("out")
            s_v = sem("v2")
            with nc.Block() as block:
                @block.gpsimd
                def _(pool):
                    for t in range(T):
                        if t >= GA:
                            pool.wait_ge(s_cm, t - GA + 1)
                        pool.indirect_dma_start(ya[:, t, :], None, yrows,
                                                bass.IndirectOffsetOnAxis(ap=pos1[:, t:t + 1], axis=0)).then_inc(s_ga[t % GA], 16)
                        pool.indirect_dma_start(yc[:, t, :], None, yrows,
                                                bass.IndirectOffsetOnAxis(ap=pos2[:, t:t + 1], axis=0)).then_inc(s_ga[t % GA], 16)

                @block.vector
                def _(v):
                    n = [0]

                    def link(ins):
                        n[0] += 1
                        ins.then_inc(s_v, 1)
                        v.wait_ge(s_v, n[0])

                    v.wait_ge(s_row, 32)
                    for t in range(T + 1):
                        if t < T:
                            a = ya[:, t, :]
                            v.wait_ge(s_ga[t % GA], 32 * (t // GA + 1))
                            v.wait_ge(s_a, t + 1)
                            link(nc.vector.scalar_tensor_tensor(out=a, in0=yc[:, t, :], scalar=gate2[:, t:t + 1], in1=a,
                                                                op0=ALU.mult, op1=ALU.add))
                            link(nc.vector.tensor_tensor(a, a, g2row[:, :], ALU.mult))
                            nc.vector.tensor_tensor(X[:, t, :], X[:, t, :], a, ALU.add).then_inc(s_cm, 1)
                        if t >= 1:
                            u = t - 1
                            v.wait_ge(s_q, u + 1)
                            nc.vector.tensor_scalar(ss[:, u:t], ss[:, u:t], 1.0 / D, EPS, ALU.mult, ALU.add).then_inc(s_k, 1)
                            v.wait_ge(s_sd, u + 1)
                            link(nc.vector.reciprocal(rstd[:, u:t], rstd[:, u:t]))
                            nc.vector.scalar_tensor_tensor(out=X[:, u, :], in0=X[:, u, :], scalar=rstd[:, u:t],
                                                           in1=frow[:, :], op0=ALU.mult, op1=ALU.mult).then_inc(s_f, 1)

                @block.scalar
                def _(act):
                    for t in range(T + 1):
                        if t < T:
                            act.wait_ge(s_ga[t % GA], 32 * (t // GA + 1))
                            nc.scalar.activation(ya[:, t, :], ya[:, t, :], ACT.Copy, scale=gate1[:, t:t + 1]).then_inc(s_a, 1)
                        if t >= 1:
                            u = t - 1
                            act.wait_ge(s_cm, u + 1)
                            if u > 0:
                                act.wait_ge(s_q, u)
                            nc.scalar.activation(junk[:, :], X[:, u, :], ACT.Square, accum_out=ss[:, u:t]).then_inc(s_q, 1)
                            act.wait_ge(s_k, u + 1)
                            nc.scalar.activation(rstd[:, u:t], ss[:, u:t], ACT.Sqrt).then_inc(s_sd, 1)

                @block.sync
                def _(sp):
                    sp.dma_start(g2row[:, :], mod[5 * D:6 * D].partition_broadcast(P)).then_inc(s_row, 16)
                    sp.dma_start(frow[:, :], final_w.partition_broadcast(P)).then_inc(s_row, 16)
                    for t in range(T):
                        sp.wait_ge(s_f, t + 1)
                        sp.dma_start(out_t[t], X[:, t, :]).then_inc(s_out, 16)
                    sp.wait_ge(s_out, 16 * T)


class Chain:

    def __init__(self, engine, semaphore):
        self.engine, self.semaphore, self.n = engine, semaphore, 0

    def __call__(self, ins):
        self.n += 1
        ins.then_inc(self.semaphore, 1)
        self.engine.wait_ge(self.semaphore, self.n)


def mod_phase(nc, jobs):
    N = 6 * D // 512
    R = 4
    tiles = [(k, n) for k in range(len(jobs)) for n in range(N)]
    with ExitStack() as ctx:
        cs = [ctx.enter_context(nc.sbuf_tensor(f"mod_c{k}", [P, len(job[0]), J], F32)) for k, job in enumerate(jobs)]
        sg = [ctx.enter_context(nc.sbuf_tensor(f"mod_s{k}", [P, len(job[0]), J], F32)) for k, job in enumerate(jobs)]
        row = [ctx.enter_context(nc.sbuf_tensor(f"mod_r{k}", [len(job[0]), N, 512], F32)) for k, job in enumerate(jobs)]
        ring = ctx.enter_context(nc.sbuf_tensor("mod_ring", [P, R, J, 512], F32))
        acc = ctx.enter_context(nc.psum_tensor("mod_acc", [P, 4, 512], F32))
        s_w = [ctx.enter_context(nc.semaphore(f"mod_w{r}")) for r in range(R)]
        s_c = ctx.enter_context(nc.semaphore("mod_c"))
        s_b = ctx.enter_context(nc.semaphore("mod_b"))
        s_silu = ctx.enter_context(nc.semaphore("mod_silu"))
        s_mm = ctx.enter_context(nc.semaphore("mod_mm"))
        s_row = ctx.enter_context(nc.semaphore("mod_row"))
        s_out = ctx.enter_context(nc.semaphore("mod_out"))
        n_c = sum(len(job[0]) for job in jobs)
        with nc.Block() as block:
            @block.sync
            def _(sp):
                for i, (k, n) in enumerate(tiles):
                    if i >= R:
                        sp.wait_ge(s_mm, i - R + 1)
                    w = jobs[k][1]
                    sp.dma_start(ring[:, i % R, :, :], w[:, n * 512:(n + 1) * 512].rearrange("(p j) n -> p j n", j=J)
                                 ).then_inc(s_w[i % R], 16)

            @block.scalar
            def _(act):
                for k, (rows, w, b, out) in enumerate(jobs):
                    for r, src in enumerate(rows):
                        act.dma_start(cs[k][:, r, :], src.rearrange("(p j) -> p j", j=J)).then_inc(s_c, 16)
                for k, (rows, w, b, out) in enumerate(jobs):
                    act.dma_start(row[k][:, :, :].rearrange("r n c -> r (n c)"), b.partition_broadcast(len(rows))).then_inc(s_b, 16)
                act.wait_ge(s_c, 16 * n_c)
                for k in range(len(jobs)):
                    nc.scalar.activation(sg[k][:, :, :], cs[k][:, :, :], ACT.Silu).then_inc(s_silu, 1)
                for k, (rows, w, b, out) in enumerate(jobs):
                    act.wait_ge(s_row, N * (k + 1))
                    act.dma_start(out, row[k][:, :, :].rearrange("r n c -> r (n c)")).then_inc(s_out, 16)
                act.wait_ge(s_out, 16 * len(jobs))

            @block.tensor
            def _(pe):
                pe.wait_ge(s_silu, len(jobs))
                for i, (k, n) in enumerate(tiles):
                    pe.wait_ge(s_w[i % R], 16 * (i // R + 1))
                    if i >= 4:
                        pe.wait_ge(s_row, i - 3)
                    for j in range(J):
                        last = nc.tensor.matmul(acc[0:len(jobs[k][0]), i % 4, :], sg[k][:, :, j], ring[:, i % R, j, :],
                                                start=(j == 0), stop=(j == J - 1))
                    last.then_inc(s_mm, 1)

            @block.vector
            def _(v):
                v.wait_ge(s_b, 16 * len(jobs))
                for i, (k, n) in enumerate(tiles):
                    v.wait_ge(s_mm, i + 1)
                    nc.vector.tensor_tensor(row[k][:, n, :], acc[0:len(jobs[k][0]), i % 4, :], row[k][:, n, :],
                                            ALU.add).then_inc(s_row, 1)


def mod_beside(nc, ctx, c_row, w, b, out, ones, ring, acc):
    N = 6 * D // 512
    cs = ctx.enter_context(nc.sbuf_tensor("mb_c", [P, J], F32))
    row = ctx.enter_context(nc.sbuf_tensor("mb_row", [1, N, 512], F32))
    ps = ctx.enter_context(nc.psum_tensor("mb_ps", [1, 4, 512], F32))
    s_w = [ctx.enter_context(nc.semaphore(f"mb_w{r}")) for r in range(2)]
    s_c, s_b, s_silu, s_v, s_acc, s_mm, s_row, s_out = (
        ctx.enter_context(nc.semaphore(f"mb_{k}")) for k in ("c", "b", "silu", "v", "acc", "mm", "row", "out"))

    def load_w(sp):
        sp.dma_start(cs[:, :], c_row.rearrange("(p j) -> p j", j=J)).then_inc(s_c, 16)
        sp.dma_start(row[:, :, :].rearrange("r n c -> r (n c)"), b.partition_broadcast(1)).then_inc(s_b, 16)
        for n in range(N):
            if n >= 2:
                sp.wait_ge(s_acc, n - 1)
            sp.dma_start(ring[:, n % 2, :, :], w[:, n * 512:(n + 1) * 512].rearrange("(p j) n -> p j n", j=J)).then_inc(s_w[n % 2], 16)

    def silu(act):
        act.wait_ge(s_c, 16)
        nc.scalar.activation(cs[:, :], cs[:, :], ACT.Silu).then_inc(s_silu, 1)

    def products(v):
        link = Chain(v, s_v)
        v.wait_ge(s_silu, 1)
        for n in range(N):
            v.wait_ge(s_w[n % 2], 16 * (n // 2 + 1))
            for j in range(J):
                if j == 0:
                    ins = nc.vector.tensor_scalar(acc(n), ring[:, n % 2, j, :], cs[:, j:j + 1], None, ALU.mult)
                else:
                    ins = nc.vector.scalar_tensor_tensor(out=acc(n), in0=ring[:, n % 2, j, :], scalar=cs[:, j:j + 1],
                                                         in1=acc(n), op0=ALU.mult, op1=ALU.add)
                if j < J - 1:
                    link(ins)
                else:
                    ins.then_inc(s_acc, 1)
        v.wait_ge(s_b, 16)
        for n in range(N):
            v.wait_ge(s_mm, n + 1)
            nc.vector.tensor_tensor(row[:, n, :], ps[:, n % 4, :], row[:, n, :], ALU.add).then_inc(s_row, 1)

    def over_partitions(pe):
        for n in range(N):
            pe.wait_ge(s_acc, n + 1)
            if n >= 4:
                pe.wait_ge(s_row, n - 3)
            nc.tensor.matmul(ps[:, n % 4, :], ones[:, 0:1], acc(n), start=True, stop=True).then_inc(s_mm, 1)

    def store_row(sp):
        sp.wait_ge(s_row, N)
        sp.dma_start(out, row[:, :, :].rearrange("r n c -> r (n c)")).then_inc(s_out, 16)
        sp.wait_ge(s_out, 16)

    return {"sync": load_w, "scalar": silu, "vector": products}, {"sync": store_row, "tensor": over_partitions}


def norm_transpose(nc, tag, src, groups, ident, dst, dst_low=None):
    n = sum(g[0] for g in groups)
    of = [k for k, g in enumerate(groups) for _ in range(g[0])]
    with ExitStack() as ctx:
        def sb(name, shape):
            return ctx.enter_context(nc.sbuf_tensor(f"{tag}_{name}", shape, F32))

        def sem(name):
            return ctx.enter_context(nc.semaphore(f"{tag}_{name}"))

        NX = 4
        xin = sb("xin", [P, NX, D])
        xs = sb("xs", [P, 2, D])
        junk = sb("junk", [P, D])
        ss = sb("ss", [P, n])
        rstd = sb("rstd", [P, n])
        col = sb("col", [P, len(groups), 3, J])
        pt = ctx.enter_context(nc.psum_tensor(f"{tag}_pt", [P, 2, J, P], F32))
        s_x = [sem(f"x{r}") for r in range(NX)]
        s_par, s_col, s_sq, s_var, s_sd, s_rstd, s_xs, s_tr, s_ev = (
            sem(k) for k in ("par", "col", "sq", "var", "sd", "rstd", "xs", "tr", "ev"))
        if dst_low is not None:
            tv = sb("tv", [P, 2, J, P])
            s_th, s_tl = sem("th"), sem("tl")
        n_par = sum(1 + (g[2] is not None) + (g[3] is not None) for g in groups)
        with nc.Block() as block:
            @block.sync
            def _(sp):
                def params():
                    for k, (_, *cols) in enumerate(groups):
                        for c, v in enumerate(cols):
                            if v is not None:
                                sp.dma_start(col[:, k, c, :], v.rearrange("(p j) -> p j", j=J)).then_inc(s_par, 16)

                for t in range(n):
                    if t >= NX:
                        sp.wait_ge(s_xs, t - NX + 1)
                    sp.dma_start(xin[:, t % NX, :], src(t)).then_inc(s_x[t % NX], 16)
                    if t == 0:
                        params()

            def rows(t):
                return xin[:, t % NX, :]

            @block.scalar
            def _(act):
                for t in range(n + 2):
                    if t < n:
                        act.wait_ge(s_x[t % NX], 16 * (t // NX + 1))
                        if t > 0:
                            act.wait_ge(s_sq, t)
                        nc.scalar.activation(junk[:, :], rows(t), ACT.Square, accum_out=ss[:, t:t + 1]).then_inc(s_sq, 1)
                    if 0 < t <= n:
                        u = t - 1
                        act.wait_ge(s_rstd, u + 1)
                        if u >= 2:
                            act.wait_ge(s_tr, u - 1)
                        nc.scalar.activation(xs[:, u % 2, :], rows(u), ACT.Copy, scale=rstd[:, u:u + 1]).then_inc(s_xs, 1)
                    if t < n:
                        act.wait_ge(s_var, t + 1)
                        nc.scalar.activation(rstd[:, t:t + 1], ss[:, t:t + 1], ACT.Sqrt).then_inc(s_sd, 1)
                    if t > 1 and dst_low is not None:
                        act.wait_ge(s_ev, t - 1)
                        nc.scalar.activation(dst[:, :, (t - 2) * P:(t - 1) * P], tv[:, t % 2, :, :], ACT.Copy).then_inc(s_th, 1)

            @block.tensor
            def _(pe):
                for t in range(n):
                    pe.wait_ge(s_xs, t + 1)
                    if t >= 2:
                        pe.wait_ge(s_ev, t - 1)
                    for j in range(J):
                        last = nc.tensor.transpose(pt[:, t % 2, j, :], xs[:, t % 2, j::J], ident[:, :])
                    last.then_inc(s_tr, 1)

            @block.vector
            def _(v):
                link = Chain(v, s_col)
                v.wait_ge(s_par, 16 * n_par)
                for k, g in enumerate(groups):
                    if g[2] is not None:
                        link(nc.vector.scalar_tensor_tensor(out=col[:, k, 0, :], in0=col[:, k, 1, :], scalar=1.0,
                                                            in1=col[:, k, 0, :], op0=ALU.add, op1=ALU.mult))
                for t in range(n + 2):
                    if t < n:
                        v.wait_ge(s_sq, t + 1)
                        nc.vector.tensor_scalar(ss[:, t:t + 1], ss[:, t:t + 1], 1.0 / D, EPS, ALU.mult, ALU.add).then_inc(s_var, 1)
                        v.wait_ge(s_sd, t + 1)
                        nc.vector.reciprocal(rstd[:, t:t + 1], rstd[:, t:t + 1]).then_inc(s_rstd, 1)
                    if 0 < t <= n:
                        u = t - 1
                        k = of[u]
                        v.wait_ge(s_tr, u + 1)
                        for j in range(J):
                            o = dst[:, j, u * P:(u + 1) * P] if dst_low is None else tv[:, u % 2, j, :]
                            i = pt[:, u % 2, j, :]
                            if groups[k][3] is None:
                                last = nc.vector.tensor_scalar(o, i, col[:, k, 0, j:j + 1], None, ALU.mult)
                            else:
                                last = nc.vector.tensor_scalar(o, i, col[:, k, 0, j:j + 1], col[:, k, 2, j:j + 1],
                                                               ALU.mult, ALU.add)
                        last.then_inc(s_ev, 1)
                    if t > 1 and dst_low is not None:
                        u = t - 2
                        v.wait_ge(s_th, u + 1)
                        tok = slice(u * P, (u + 1) * P)
                        nc.vector.tensor_tensor(dst_low[:, :, tok], tv[:, u % 2, :, :], dst[:, :, tok].bitcast(F32),
                                                ALU.subtract).then_inc(s_tl, 1)
                        v.wait_ge(s_tl, u + 1)


def make_masks(nc, tag, masks):
    with ExitStack() as ctx:
        ones = ctx.enter_context(nc.sbuf_tensor(f"{tag}_one", [P, P], F32))
        s_one = ctx.enter_context(nc.semaphore(f"{tag}_s_one"))
        s_mask = ctx.enter_context(nc.semaphore(f"{tag}_s_mask"))
        with nc.Block() as block:
            @block.gpsimd
            def _(pool):
                nc.gpsimd.memset(ones[:, :], 1.0).then_inc(s_one, 1)
                pool.wait_ge(s_one, 1)
                for tile, op, sign in masks:
                    nc.gpsimd.affine_select(out=tile[:, :], in_=ones[:, :], compare_op=op, fill=0.0, base=0,
                                            pattern=[[sign, P]], channel_multiplier=-sign).then_inc(s_mask, 1)
                pool.wait_ge(s_mask, len(masks))


def run_part(programs, engine_name, engine):
    if engine_name in programs:
        programs[engine_name](engine)


def project_rows(nc, tag, xT, w_tiles, func, out, lhs=None, RP=4, first={}, then={}):
    lhs = lhs or (lambda j, t: xT[:, j, t * P:(t + 1) * P])
    R, RO = min(2, len(w_tiles)), 4
    with ExitStack() as ctx:
        ring = ctx.enter_context(nc.sbuf_tensor(f"{tag}_ring", [P, R, J, 512], F32))
        ob = ctx.enter_context(nc.sbuf_tensor(f"{tag}_ob", [P, RO, 512], F32))
        acc = ctx.enter_context(nc.psum_tensor(f"{tag}_acc", [P, RP, 512], F32))
        s_w = [ctx.enter_context(nc.semaphore(f"{tag}_w{r}")) for r in range(R)]
        s_o = [ctx.enter_context(nc.semaphore(f"{tag}_o{r}")) for r in range(RO)]
        s_mm = ctx.enter_context(nc.semaphore(f"{tag}_mm"))
        s_ev = ctx.enter_context(nc.semaphore(f"{tag}_ev"))
        steps = [(n, t) for n in range(len(w_tiles)) for t in range(T)]
        with nc.Block() as block:
            @block.vector
            def _(v):
                run_part(first, "vector", v)
                run_part(then, "vector", v)

            @block.sync
            def _(sp):
                for n, w in enumerate(w_tiles):
                    if n >= R:
                        sp.wait_ge(s_mm, T * (n - R + 1))
                    sp.dma_start(ring[:, n % R, :, :], w).then_inc(s_w[n % R], 16)
                run_part(first, "sync", sp)
                run_part(then, "sync", sp)

            @block.tensor
            def _(pe):
                run_part(first, "tensor", pe)
                for i, (n, t) in enumerate(steps):
                    if t == 0:
                        pe.wait_ge(s_w[n % R], 16 * (n // R + 1))
                    if i >= RP:
                        pe.wait_ge(s_ev, i - RP + 1)
                    for j in range(J):
                        last = nc.tensor.matmul(acc[:, i % RP, :], lhs(j, t), ring[:, n % R, j, :],
                                                start=(j == 0), stop=(j == J - 1))
                    last.then_inc(s_mm, 1)
                run_part(then, "tensor", pe)

            @block.scalar
            def _(act):
                run_part(first, "scalar", act)
                for i in range(len(steps)):
                    act.wait_ge(s_mm, i + 1)
                    if i >= RO:
                        act.wait_ge(s_o[i % RO], 16 * (i // RO))
                    nc.scalar.activation(ob[:, i % RO, :], acc[:, i % RP, :], func).then_inc(s_ev, 1)
                    act.wait_ge(s_ev, i + 1)
                    act.dma_start(out(*steps[i]), ob[:, i % RO, :]).then_inc(s_o[i % RO], 16)
                for r in range(RO):
                    act.wait_ge(s_o[r], 16 * len(steps[r::RO]))
                run_part(then, "scalar", act)


def project_channels(nc, tag, xT, n_j, w_tiles, func, bias, dst, first={}, then={}):
    FIRST = 2
    R, RP = min(2, len(w_tiles)), 4
    with ExitStack() as ctx:
        ring = ctx.enter_context(nc.sbuf_tensor(f"{tag}_ring", [P, R, n_j, 512], F32))
        acc = ctx.enter_context(nc.psum_tensor(f"{tag}_acc", [P, RP, 512], F32))
        s_w = [ctx.enter_context(nc.semaphore(f"{tag}_w{r}")) for r in range(R)]
        s_mm = ctx.enter_context(nc.semaphore(f"{tag}_mm"))
        s_ev = ctx.enter_context(nc.semaphore(f"{tag}_ev"))
        steps = [(n, c, h) for n in range(len(w_tiles)) for c in range(4) for h in range(2)]
        with nc.Block() as block:
            @block.vector
            def _(v):
                run_part(first, "vector", v)
                run_part(then, "vector", v)

            @block.sync
            def _(sp):
                for n, w in enumerate(w_tiles):
                    if n >= R:
                        sp.wait_ge(s_mm, 8 * (n - R + 1))
                    sp.dma_start(ring[:, n % R, :, :], w).then_inc(s_w[n % R], 16)
                run_part(first, "sync", sp)

            @block.tensor
            def _(pe):
                for i, (n, c, h) in enumerate(steps):
                    if i == FIRST:
                        run_part(first, "tensor", pe)
                    if c == 0 and h == 0:
                        pe.wait_ge(s_w[n % R], 16 * (n // R + 1))
                    if i >= RP:
                        pe.wait_ge(s_ev, i - RP + 1)
                    for j in range(n_j):
                        last = nc.tensor.matmul(acc[:, i % RP, :], ring[:, n % R, j, c * P:(c + 1) * P],
                                                xT[:, j, h * 512:(h + 1) * 512], start=(j == 0), stop=(j == n_j - 1))
                    last.then_inc(s_mm, 1)
                run_part(then, "tensor", pe)

            @block.scalar
            def _(act):
                for i, (n, c, h) in enumerate(steps):
                    if i == FIRST:
                        run_part(first, "scalar", act)
                    act.wait_ge(s_mm, i + 1)
                    m = 4 * n + c
                    if bias is None:
                        ins = nc.scalar.activation(dst(m, h), acc[:, i % RP, :], func)
                    else:
                        ins = nc.scalar.activation(dst(m, h), acc[:, i % RP, :], func, bias=bias[:, m:m + 1])
                    ins.then_inc(s_ev, 1)
                run_part(then, "scalar", act)


def transpose_rows(nc, tag, src, n_rows, ident, dst):
    with ExitStack() as ctx:
        rows = ctx.enter_context(nc.sbuf_tensor(f"{tag}_rows", [n_rows, P], F32))
        pt = ctx.enter_context(nc.psum_tensor(f"{tag}_pt", [P, n_rows], F32))
        s_in = ctx.enter_context(nc.semaphore(f"{tag}_in"))
        s_t = ctx.enter_context(nc.semaphore(f"{tag}_t"))
        s_e = ctx.enter_context(nc.semaphore(f"{tag}_e"))
        with nc.Block() as block:
            @block.sync
            def _(sp):
                at = 0
                for s in src:
                    sp.dma_start(rows[at:at + s.shape[0], :], s).then_inc(s_in, 16)
                    at += s.shape[0]

            @block.tensor
            def _(pe):
                pe.wait_ge(s_in, 16 * len(src))
                nc.tensor.transpose(pt[:, :], rows[:, :], ident[0:n_rows, 0:n_rows]).then_inc(s_t, 1)

            @block.vector
            def _(v):
                v.wait_ge(s_t, 1)
                nc.vector.tensor_copy(dst, pt[:, :]).then_inc(s_e, 1)


H, G, HD, NS, CW = 16, 4, 64, 128, 5
HG = H // G
NC = 256 // P
TT = T + NC
C0 = SEQ + 4
OUTW = C0 + NC * P
PADW = OUTW + CW - 1


def ssd_decays(nc, ctx, xnT, w_v, dt_bias, a_log, masks, dt, ecum, eend, etot, da):
    LE_, GT, GE, LT, ONE = masks

    def sb(name, shape, dt_=F32):
        return ctx.enter_context(nc.sbuf_tensor(f"sd_{name}", shape, dt_))

    def sem(name):
        return ctx.enter_context(nc.semaphore(f"sd_{name}"))

    wdt = sb("wdt", [P, J, 2 * H])
    bias = sb("bias", [P, 2 * H])
    alog = sb("alog", [P, 2 * H])
    raw, mag, u, w, c1, lg = (sb(n, [P, TT, 2 * H]) for n in ("raw", "mag", "u", "w", "c1", "lg"))
    pd = ctx.enter_context(nc.psum_tensor("sd_pd", [P, TT, 2 * H], F32))
    pc, pe_, po = (ctx.enter_context(nc.psum_tensor(f"sd_{n}", [P, 2, TT, H], F32)) for n in ("pc", "pe", "po"))
    s_in, s_mm, s_l, s_a, s_b, s_e = (sem(k) for k in ("in", "mm", "l", "a", "b", "e"))
    s_l2 = sem("l2")
    DT0 = D + D + 2 * G * NS

    def sync(sp):
        sp.dma_start(wdt[:, :, :], w_v[:, :, DT0:DT0 + 2 * H]).then_inc(s_in, 16)
        sp.dma_start(bias[:, :], dt_bias.rearrange("d h -> (d h)").partition_broadcast(P)).then_inc(s_in, 16)
        sp.dma_start(alog[:, :], a_log.rearrange("d h -> (d h)").partition_broadcast(P)).then_inc(s_in, 16)

    def tensor(pe):
        pe.wait_ge(s_in, 48)
        for t in range(TT):
            for j in range(J):
                last = nc.tensor.matmul(pd[:, t, :], xnT[:, j, t * P:(t + 1) * P], wdt[:, j, :],
                                        start=(j == 0), stop=(j == J - 1))
        last.then_inc(s_mm, 1)

    def sums(pe):
        pe.wait_ge(s_a, 1)
        for q, (mc, me) in enumerate(((LE_, GT), (GE, LT))):
            r = da[:, :, q * H:(q + 1) * H]
            nc.tensor.matmul(pc[:, q, :, :], mc[:, :], r, start=True, stop=True)
            nc.tensor.matmul(pe_[:, q, :, :], me[:, :], r, start=True, stop=True)
            nc.tensor.matmul(po[:, q, :, :], ONE[:, :], r, start=True, stop=True).then_inc(s_mm, 1)

    def vector(v):
        link = Chain(v, s_l)
        v.wait_ge(s_mm, 1)
        link(nc.vector.tensor_tensor(raw[:, :, :], pd[:, :, :], bc(bias[:, :], TT, 1), ALU.add))
        link(nc.vector.tensor_scalar(mag[:, :, :], raw[:, :, :], -1.0, None, ALU.mult))
        nc.vector.tensor_tensor(mag[:, :, :], mag[:, :, :], raw[:, :, :], ALU.min).then_inc(s_b, 1)
        v.wait_ge(s_e, 1)
        link(nc.vector.tensor_scalar(w[:, :, :], u[:, :, :], 1.0, None, ALU.add))
        nc.vector.tensor_scalar(c1[:, :, :], w[:, :, :], -1.0, None, ALU.add).then_inc(s_b, 1)
        v.wait_ge(s_b, 2)
        link(nc.vector.tensor_tensor(c1[:, :, :], u[:, :, :], c1[:, :, :], ALU.subtract))
        link(nc.vector.reciprocal(w[:, :, :], w[:, :, :]))
        link(nc.vector.tensor_tensor(c1[:, :, :], c1[:, :, :], w[:, :, :], ALU.mult))
        v.wait_ge(s_e, 3)
        link(nc.vector.tensor_tensor(lg[:, :, :], lg[:, :, :], c1[:, :, :], ALU.add))
        link(nc.vector.scalar_tensor_tensor(out=dt[:, :, :], in0=raw[:, :, :], scalar=0.0, in1=lg[:, :, :],
                                            op0=ALU.max, op1=ALU.add))
        nc.vector.scalar_tensor_tensor(out=da[:, :, :], in0=dt[:, :, :], scalar=-1.0, in1=bc(alog[:, :], TT, 1),
                                       op0=ALU.mult, op1=ALU.mult).then_inc(s_a, 1)

    def end_weights(v):
        link = Chain(v, s_l2)
        v.wait_ge(s_e, 6)
        for q in range(2):
            link(nc.vector.tensor_tensor(eend[:, :, q * H:(q + 1) * H], eend[:, :, q * H:(q + 1) * H],
                                         dt[:, :, q * H:(q + 1) * H], ALU.mult))

    def scalar(act):
        act.wait_ge(s_b, 1)
        nc.scalar.activation(u[:, :, :], mag[:, :, :], ACT.Exp).then_inc(s_e, 1)
        nc.scalar.activation(alog[:, :], alog[:, :], ACT.Exp).then_inc(s_e, 1)
        act.wait_ge(s_b, 2)
        nc.scalar.activation(lg[:, :, :], u[:, :, :], ACT.Ln, bias=1.0).then_inc(s_e, 1)

    def decay_values(act):
        act.wait_ge(s_mm, 3)
        for src, dst in ((pc, ecum), (pe_, eend), (po, etot)):
            nc.scalar.activation(dst[:, :, :].rearrange("p t (q h) -> p q t h", q=2), src[:, :, :, :],
                                 ACT.Exp).then_inc(s_e, 1)

    return ({"sync": sync, "tensor": tensor, "scalar": scalar, "vector": vector},
            {"tensor": sums, "scalar": decay_values, "vector": end_weights})


def ssd_inputs(nc, xnT, w_v, cwb, ident, xs_tok, b_tok, bT, cT):
    NM = (D + 2 * G * NS) // P
    with ExitStack() as ctx:
        def sb(name, shape, dt_=F32):
            return ctx.enter_context(nc.sbuf_tensor(f"si_{name}", shape, dt_))

        def ps(name, shape):
            return ctx.enter_context(nc.psum_tensor(f"si_{name}", shape, F32))

        def sem(name):
            return ctx.enter_context(nc.semaphore(f"si_{name}"))

        R = 2
        ring = sb("ring", [P, R, J, 512])
        xpad = sb("xpad", [P, 2, PADW])
        cacc = sb("cacc", [P, OUTW])
        xc = sb("xc", [P, 2, OUTW])
        acc = ps("acc", [P, 5, 512])
        pt = ps("pt", [P, 3, 4, P])
        s_w = [sem(f"w{r}") for r in range(R)]
        s_pad, s_mm, s_ev, s_cv, s_ch, s_xc, s_tr, s_te = (sem(k) for k in ("pad", "mm", "ev", "cv", "ch", "xc", "tr", "te"))
        halves = ((0, 512), (512, 512), (SEQ, NC * P))
        tgroups = ((0, 4), (4, 4), (8, NC))
        n_t = 12
        with nc.Block() as block:
            @block.sync
            def _(sp):
                for n in range(NM // 4):
                    if n >= R:
                        sp.wait_ge(s_mm, 3 * 4 * (n - R + 1))
                    sp.dma_start(ring[:, n % R, :, :], w_v[:, :, D + n * 512:D + (n + 1) * 512]).then_inc(s_w[n % R], 16)

            @block.tensor
            def _(pe):
                def turn(m):
                    for g, (t0, nt) in enumerate(tgroups):
                        i = 3 * m + g
                        pe.wait_ge(s_xc, m + 1)
                        if i >= 3:
                            pe.wait_ge(s_te, i - 2)
                        for k in range(nt):
                            at = (t0 + k) * P if t0 < T else C0 + k * P
                            last = nc.tensor.transpose(pt[:, i % 3, k, :], xc[:, m % 2, at:at + P], ident[:, :])
                        last.then_inc(s_tr, 1)

                for m in range(NM + 1):
                    if m < NM:
                        if m % 4 == 0:
                            pe.wait_ge(s_w[(m // 4) % R], 16 * (m // 4 // R + 1))
                        for g, (at, n) in enumerate(halves):
                            i = 3 * m + g
                            if i >= 5:
                                pe.wait_ge(s_ev, i - 4)
                            for j in range(J):
                                last = nc.tensor.matmul(acc[:, i % 5, 0:n], ring[:, (m // 4) % R, j, (m % 4) * P:(m % 4 + 1) * P],
                                                        xnT[:, j, at:at + n], start=(j == 0), stop=(j == J - 1))
                            last.then_inc(s_mm, 1)
                    if 1 <= m <= n_t:
                        turn(m - 1)

            @block.scalar
            def _(act):
                def fill(m):
                    if m >= 2:
                        act.wait_ge(s_cv, m - 1)
                    else:
                        act.wait_ge(s_pad, 1)
                    for g, (at, n) in enumerate(halves):
                        act.wait_ge(s_mm, 3 * m + g + 1)
                        o = 2 + at if at < SEQ else C0 + 2
                        nc.scalar.activation(xpad[:, m % 2, o:o + n], acc[:, (3 * m + g) % 5, 0:n], ACT.Copy).then_inc(s_ev, 1)

                for m in range(NM + 1):
                    if m < NM:
                        fill(m)
                    if m >= 1:
                        u = m - 1
                        act.wait_ge(s_cv, u + 1)
                        if 2 <= u < n_t:
                            act.wait_ge(s_tr, 3 * (u - 1))
                        bias = cwb[:, CW * NM + u:CW * NM + u + 1]
                        if u < n_t:
                            ins = nc.scalar.activation(xc[:, u % 2, :], cacc[:, :], ACT.Silu, bias=bias)
                            ins.then_inc(s_xc, 1)
                        if 8 <= u < 12:
                            nc.scalar.activation(bT[:, u - 8, :], cacc[:, 0:SEQ], ACT.Silu, bias=bias).then_inc(s_ch, 1)
                        if u >= 12:
                            nc.scalar.activation(cT[:, u - 12, :], cacc[:, 0:SEQ], ACT.Silu, bias=bias).then_inc(s_xc, 1)

            @block.vector
            def _(v):
                s_link = sem("link")
                link = Chain(v, s_link)
                link(nc.vector.memset(xpad[:, :, 0:2], 0.0))
                link(nc.vector.memset(xpad[:, :, SEQ + 2:C0 + 2], 0.0))
                nc.vector.memset(xpad[:, :, PADW - 2:PADW], 0.0).then_inc(s_pad, 1)

                def conv(m):
                    v.wait_ge(s_ev, 3 * m + 3)
                    if m >= 1:
                        v.wait_ge(s_xc, m)
                    if 9 <= m < 13:
                        v.wait_ge(s_ch, m - 8)
                    for k in range(CW):
                        w = cwb[:, k * NM + m:k * NM + m + 1]
                        x_k = xpad[:, m % 2, k:k + OUTW]
                        if k == 0:
                            ins = nc.vector.tensor_scalar(cacc[:, :], x_k, w, None, ALU.mult)
                        else:
                            ins = nc.vector.scalar_tensor_tensor(out=cacc[:, :], in0=x_k, scalar=w, in1=cacc[:, :],
                                                                 op0=ALU.mult, op1=ALU.add)
                        if k < CW - 1:
                            link(ins)
                        else:
                            ins.then_inc(s_cv, 1)

                def place(m):
                    for g, (t0, nt) in enumerate(tgroups):
                        v.wait_ge(s_tr, 3 * m + g + 1)
                        dst = xs_tok[:, t0:t0 + nt, m * P:(m + 1) * P] if m < 8 else b_tok[:, t0:t0 + nt, (m - 8) * P:(m - 7) * P]
                        nc.vector.tensor_copy(dst, pt[:, (3 * m + g) % 3, 0:nt, :]).then_inc(s_te, 1)

                for m in range(NM + 1):
                    if m < NM:
                        conv(m)
                    if 1 <= m <= n_t:
                        place(m - 1)


def ssd_scan(nc, masks, xs_tok, b_tok, bT, cT, dt, da, ecum, eend, etot, d_skip, y):
    LE_, GT, GE, LT, ONE = masks
    jobs = []
    for a, b in zip(list(range(T, TT)) + list(range(T)), list(reversed(range(T, TT))) + list(reversed(range(T)))):
        jobs += [(0, a), (1, b)]
    lat = [i for i, (q, c) in enumerate(jobs) if c < T]
    nth = {i: k for k, i in enumerate(lat)}
    with ExitStack() as ctx:
        def sb(name, shape, dt_=F32):
            return ctx.enter_context(nc.sbuf_tensor(f"ss_{name}", shape, dt_))

        def ps(name, shape):
            return ctx.enter_context(nc.psum_tensor(f"ss_{name}", shape, F32))

        def sem(name):
            return ctx.enter_context(nc.semaphore(f"ss_{name}"))

        hst = sb("hst", [P, 2, H, HD])
        tri = sb("tri", [P, 2, H, P])
        ex = sb("ex", [P, 2, HG, P])
        cbm = sb("cbm", [P, G, P])
        gm = sb("gm", [P, H, P])
        xd = sb("xd", [P, 2, H, HD])
        xe = sb("xe", [P, 2, H, HD])
        yo = sb("yo", [P, H, HD])
        dsk = sb("dsk", [P, H])
        p_seg = ps("seg", [P, 2, HG, P])
        p_cb = ps("cb", [P, G, P])
        p_d = ps("d", [P, H, HD])
        p_o = ps("o", [P, H, HD])
        s_in, s_tri, s_xd, s_seg, s_ex, s_cb, s_gm, s_d, s_o, s_st, s_v, s_yo, s_h, s_y = (
            sem(k) for k in ("in", "tri", "xd", "seg", "ex", "cb", "gm", "d", "o", "st", "v", "yo", "h", "y"))
        with nc.Block() as block:
            @block.sync
            def _(sp):
                sp.dma_start(dsk[:, :], d_skip.partition_broadcast(P)).then_inc(s_in, 16)

            @block.gpsimd
            def _(pool):
                for i, (q, c) in enumerate(jobs):
                    r = i % 2
                    if i >= 2:
                        pool.wait_ge(s_st, i - 1)
                    xv = xs_tok[:, c, :].rearrange("p (h d) -> p h d", h=H)
                    nc.gpsimd.tensor_tensor(xe[:, r, :, :], xv, bc(eend[:, c, q * H:(q + 1) * H], HD, 2), ALU.mult).then_inc(s_xd, 1)
                    if i in nth:
                        nc.gpsimd.tensor_tensor(xd[:, r, :, :], xv, bc(dt[:, c, q * H:(q + 1) * H], HD, 2), ALU.mult).then_inc(s_xd, 1)
                        m = LE_ if q == 0 else GE
                        nc.gpsimd.tensor_tensor(tri[:, r, :, :], bc(m[:, :], H, 1), bc(da[:, c, q * H:(q + 1) * H], P, 2),
                                                ALU.mult).then_inc(s_tri, 1)

            def xd_count(i):
                return sum(1 + (k in nth) for k in range(i + 1))

            @block.tensor
            def _(pe):
                for i, (q, c) in enumerate(jobs):
                    r = i % 2
                    tok = slice(c * P, (c + 1) * P)
                    if i in nth:
                        k = nth[i]
                        if k >= 1:
                            pe.wait_ge(s_gm, 4 * k)
                        for g in range(G):
                            last = nc.tensor.matmul(p_cb[:, g, :], bT[:, g, tok], cT[:, g, tok], start=True, stop=True)
                        last.then_inc(s_cb, 1)
                        pe.wait_ge(s_tri, k + 1)
                        for g in range(G):
                            n = 4 * k + g
                            if n >= 2:
                                pe.wait_ge(s_ex, n - 1)
                            nc.tensor.matmul(p_seg[:, n % 2, :, :], (GT if q == 0 else LT)[:, :], tri[:, r, 4 * g:4 * g + 4, :],
                                             start=True, stop=True).then_inc(s_seg, 1)
                        pe.wait_ge(s_h, 2 + i)
                        for g in range(G):
                            last = nc.tensor.matmul(p_o[:, 4 * g:4 * g + 4, :], cT[:, g, tok], hst[:, q, 4 * g:4 * g + 4, :],
                                                    start=True, stop=True)
                        last.then_inc(s_o, 1)
                        pe.wait_ge(s_xd, xd_count(i))
                        pe.wait_ge(s_gm, 4 * k + 4)
                        if k >= 1:
                            pe.wait_ge(s_y, k)
                        for h in range(H):
                            last = nc.tensor.matmul(p_d[:, h, :], gm[:, h, :], xd[:, r, h, :], start=True, stop=True)
                        last.then_inc(s_d, 1)
                        pe.wait_ge(s_yo, k + 1)
                    else:
                        pe.wait_ge(s_xd, xd_count(i))
                        pe.wait_ge(s_h, 2 + i)
                    for g in range(G):
                        last = nc.tensor.matmul(p_o[:, 4 * g:4 * g + 4, :], b_tok[:, c, g * NS:(g + 1) * NS],
                                                xe[:, r, 4 * g:4 * g + 4, :], start=True, stop=True)
                    last.then_inc(s_st, 1)

            @block.scalar
            def _(act):
                for k, i in enumerate(lat):
                    for g in range(G):
                        n = 4 * k + g
                        act.wait_ge(s_seg, n + 1)
                        if n >= 2:
                            act.wait_ge(s_gm, n - 1)
                        nc.scalar.activation(ex[:, n % 2, :, :], p_seg[:, n % 2, :, :], ACT.Exp).then_inc(s_ex, 1)

            @block.vector
            def _(v):
                link = Chain(v, s_v)
                nc.vector.memset(hst[:, 0, :, :], 0.0).then_inc(s_h, 1)
                nc.vector.memset(hst[:, 1, :, :], 0.0).then_inc(s_h, 1)
                v.wait_ge(s_in, 16)
                for c in range(T):
                    last = nc.vector.tensor_tensor(y[:, c, :].rearrange("p (h d) -> p h d", h=H),
                                                   xs_tok[:, c, :].rearrange("p (h d) -> p h d", h=H),
                                                   bc(dsk[:, :], HD, 2), ALU.mult)
                link(last)
                v.wait_ge(s_h, 2)
                for i, (q, c) in enumerate(jobs):
                    hs = slice(q * H, (q + 1) * H)
                    yc = y[:, c, :].rearrange("p (h d) -> p h d", h=H) if c < T else None
                    if i in nth:
                        k = nth[i]
                        v.wait_ge(s_cb, k + 1)
                        m = LE_ if q == 0 else GE
                        if k >= 1:
                            v.wait_ge(s_d, k)
                        link(nc.vector.tensor_tensor(cbm[:, :, :], p_cb[:, :, :], bc(m[:, :], G, 1), ALU.mult))
                        for g in range(G):
                            n = 4 * k + g
                            v.wait_ge(s_ex, n + 1)
                            nc.vector.tensor_tensor(gm[:, 4 * g:4 * g + 4, :], ex[:, n % 2, :, :], bc(cbm[:, g, :], HG, 1),
                                                    ALU.mult).then_inc(s_gm, 1)
                        v.wait_ge(s_o, k + 1)
                        nc.vector.tensor_tensor(yo[:, :, :], p_o[:, :, :], bc(ecum[:, c, hs], HD, 2), ALU.mult).then_inc(s_yo, 1)
                        v.wait_ge(s_yo, k + 1)
                        link(nc.vector.tensor_tensor(yc, yc, yo[:, :, :], ALU.add))
                        v.wait_ge(s_d, k + 1)
                        nc.vector.tensor_tensor(yc, p_d[:, :, :], yc, ALU.add).then_inc(s_y, 1)
                    link(nc.vector.tensor_tensor(hst[:, q, :, :], hst[:, q, :, :], bc(etot[:, c, hs], HD, 2), ALU.mult))
                    v.wait_ge(s_st, i + 1)
                    nc.vector.tensor_tensor(hst[:, q, :, :], p_o[:, :, :], hst[:, q, :, :], ALU.add).then_inc(s_h, 1)
                    v.wait_ge(s_h, 3 + i)


def gate_rows(nc, tag, y, z_rows, out_rows):
    with ExitStack() as ctx:
        zb = ctx.enter_context(nc.sbuf_tensor(f"{tag}_zb", [P, 4, D], F32))
        s_z = [ctx.enter_context(nc.semaphore(f"{tag}_z{r}")) for r in range(4)]
        s_m = ctx.enter_context(nc.semaphore(f"{tag}_m"))
        s_o = ctx.enter_context(nc.semaphore(f"{tag}_o"))
        with nc.Block() as block:
            @block.sync
            def _(sp):
                for t in range(T):
                    if t >= 4:
                        sp.wait_ge(s_m, t - 3)
                    sp.dma_start(zb[:, t % 4, :], z_rows(t)).then_inc(s_z[t % 4], 16)

            @block.vector
            def _(v):
                for t in range(T):
                    v.wait_ge(s_z[t % 4], 16 * (t // 4 + 1))
                    nc.vector.tensor_tensor(y[:, t, :], y[:, t, :], zb[:, t % 4, :], ALU.mult).then_inc(s_m, 1)

            @block.scalar
            def _(act):
                for t in range(T):
                    act.wait_ge(s_m, t + 1)
                    act.dma_start(out_rows(t), y[:, t, :]).then_inc(s_o, 16)
                act.wait_ge(s_o, 16 * T)


def fourier(nc, f_dram, fh, fl, w_four, dft, rot):
    C = 512
    with ExitStack() as ctx:
        def sb(name, shape):
            return ctx.enter_context(nc.sbuf_tensor(f"fo_{name}", shape, F32))

        def ps(name, shape):
            return ctx.enter_context(nc.psum_tensor(f"fo_{name}", shape, F32))

        def sem(name):
            return ctx.enter_context(nc.semaphore(f"fo_{name}"))

        fT = sb("fT", [P, G, SEQ])
        tab = sb("tab", [P, 2, P])
        rt = sb("rt", [P, 2, T, P])
        wf = sb("wf", [P, G, P])
        cw = sb("cw", [P, G, 2, P])
        ab = sb("ab", [P, 2, T, C])
        bb = sb("bb", [P, 2, T, C])
        p_w = ps("w", [P, G, 2, P])
        p_u = ps("u", [P, 2, G, 2, P])
        p_f = ps("f", [P, 2, G, P])
        s_in, s_f, s_w, s_cw, s_u, s_ev, s_v, s_g, s_o, s_oe = (sem(k) for k in ("in", "f", "w", "cw", "u", "ev", "v", "g", "o", "oe"))
        s_ol = sem("ol")
        with nc.Block() as block:
            @block.sync
            def _(sp):
                sp.dma_start(tab[:, :, :], dft).then_inc(s_in, 16)
                sp.dma_start(wf[:, :, :], w_four.rearrange("g c d -> c g d")).then_inc(s_in, 16)
                sp.dma_start(rt[:, :, :, :], rot).then_inc(s_in, 16)
                sp.dma_start(fT[:, :, :], f_dram).then_inc(s_f, 16)

            @block.tensor
            def _(pe):
                pe.wait_ge(s_in, 48)
                for g in range(G):
                    for a in range(2):
                        last = nc.tensor.matmul(p_w[:, g, a, :], tab[:, a, :], wf[:, g, :], start=True, stop=True)
                last.then_inc(s_w, 1)
                pe.wait_ge(s_cw, 1)
                pe.wait_ge(s_f, 16)
                for t in range(T):
                    if t >= 2:
                        pe.wait_ge(s_ev, 2 * (t - 1))
                    for g in range(G):
                        last = nc.tensor.matmul(p_u[:, t % 2, g, :, :], fT[:, g, t * P:(t + 1) * P], cw[:, g, :, :],
                                                start=True, stop=True)
                    last.then_inc(s_u, 1)
                pe.wait_ge(s_g, 1)
                for k2 in range(T):
                    if k2 >= 2:
                        pe.wait_ge(s_ol, k2 - 1)
                    for g in range(G):
                        for a in range(2):
                            last = nc.tensor.matmul(p_f[:, k2 % 2, g, :], ab[:, a, k2, g * P:(g + 1) * P], rt[:, a, k2, :],
                                                    start=(a == 0), stop=(a == 1))
                    last.then_inc(s_o, 1)

            @block.scalar
            def _(act):
                for t in range(T):
                    act.wait_ge(s_u, t + 1)
                    nc.scalar.activation(ab[:, 0, t, :].rearrange("p (g c) -> p g c", g=G), p_u[:, t % 2, :, 0, :], ACT.Copy).then_inc(s_ev, 1)
                    nc.scalar.activation(ab[:, 1, t, :].rearrange("p (g c) -> p g c", g=G), p_u[:, t % 2, :, 1, :], ACT.Copy,
                                         scale=-1.0).then_inc(s_ev, 1)
                for k2 in range(T):
                    act.wait_ge(s_o, k2 + 1)
                    nc.scalar.activation(fh[:, :, k2::T], p_f[:, k2 % 2, :, :], ACT.Copy).then_inc(s_oe, 1)

            @block.vector
            def _(v):
                link = Chain(v, s_v)
                v.wait_ge(s_w, 1)
                nc.vector.tensor_copy(cw[:, :, :, :], p_w[:, :, :, :]).then_inc(s_cw, 1)
                v.wait_ge(s_ev, 2 * T)
                re, im = 0, 1
                RT = 0.5 ** 0.5

                def tt(o, a, b, op):
                    return nc.vector.tensor_tensor(o, a, b, op)

                for c in (re, im):
                    tt(bb[:, c, 0:4, :], ab[:, c, 0:4, :], ab[:, c, 4:8, :], ALU.add)
                    last = tt(bb[:, c, 4:8, :], ab[:, c, 0:4, :], ab[:, c, 4:8, :], ALU.subtract)
                link(last)
                for t in (5, 7):
                    tt(ab[:, re, t, :], bb[:, re, t, :], bb[:, im, t, :], ALU.add)
                    last = tt(ab[:, im, t, :], bb[:, im, t, :], bb[:, re, t, :], ALU.subtract)
                link(last)
                nc.vector.tensor_scalar(bb[:, re, 5, :], ab[:, re, 5, :], RT, None, ALU.mult)
                nc.vector.tensor_scalar(bb[:, im, 5, :], ab[:, im, 5, :], RT, None, ALU.mult)
                nc.vector.tensor_scalar(bb[:, re, 7, :], ab[:, im, 7, :], RT, None, ALU.mult)
                link(nc.vector.tensor_scalar(bb[:, im, 7, :], ab[:, re, 7, :], -RT, None, ALU.mult))
                nc.vector.tensor_copy(ab[:, re, 6, :], bb[:, im, 6, :])
                link(nc.vector.tensor_scalar(ab[:, im, 6, :], bb[:, re, 6, :], -1.0, None, ALU.mult))
                nc.vector.tensor_copy(bb[:, re, 6, :], ab[:, re, 6, :])
                link(nc.vector.tensor_copy(bb[:, im, 6, :], ab[:, im, 6, :]))
                s = bb[:, :, :, :].rearrange("p c (a b) n -> p c a b n", a=2)
                d = ab[:, :, :, :].rearrange("p c (a b) n -> p c a b n", a=2)
                for c in (re, im):
                    for a in range(2):
                        tt(d[:, c, a, 0:2, :], s[:, c, a, 0:2, :], s[:, c, a, 2:4, :], ALU.add)
                        last = tt(d[:, c, a, 2:4, :], s[:, c, a, 0:2, :], s[:, c, a, 2:4, :], ALU.subtract)
                link(last)
                for a in range(2):
                    for c, o, op in ((re, im, (ALU.add, ALU.subtract)), (im, re, (ALU.subtract, ALU.add))):
                        tt(bb[:, c, a, :], d[:, c, a, 0, :], d[:, c, a, 1, :], ALU.add)
                        tt(bb[:, c, 4 + a, :], d[:, c, a, 0, :], d[:, c, a, 1, :], ALU.subtract)
                        tt(bb[:, c, 2 + a, :], d[:, c, a, 2, :], d[:, o, a, 3, :], op[0])
                        last = tt(bb[:, c, 6 + a, :], d[:, c, a, 2, :], d[:, o, a, 3, :], op[1])
                link(last)
                nc.vector.tensor_copy(ab[:, re, :, :], bb[:, re, :, :])
                nc.vector.tensor_scalar(ab[:, im, :, :], bb[:, im, :, :], -1.0, None, ALU.mult).then_inc(s_g, 1)
                for k2 in range(T):
                    v.wait_ge(s_oe, k2 + 1)
                    nc.vector.tensor_tensor(fl[:, :, k2::T], p_f[:, k2 % 2, :, :], fh[:, :, k2::T].bitcast(F32),
                                            ALU.subtract).then_inc(s_ol, 1)


def split_stream(nc, ctx, tag, units, width, R):
    raw = [ctx.enter_context(nc.sbuf_tensor(f"{tag}_raw{r}", [P, width], F32)) for r in range(R)]
    s_raw = [ctx.enter_context(nc.semaphore(f"{tag}_raw{r}")) for r in range(R)]
    s_hi, s_lo = (ctx.enter_context(nc.semaphore(f"{tag}_{k}")) for k in ("hi", "lo"))

    def value(u):
        v, shape = raw[u % R][:, :], units[u][1].shape
        return v if len(shape) == 2 else v.rearrange("p (a b) -> p a b", b=shape[2])

    def sync(sp):
        for u, (src, _, _) in enumerate(units):
            if u >= R:
                sp.wait_ge(s_lo, u - R + 1)
            sp.dma_start(value(u), src).then_inc(s_raw[u % R], 16)

    def scalar(act):
        for u, (_, high, _) in enumerate(units):
            act.wait_ge(s_raw[u % R], 16 * (u // R + 1))
            nc.scalar.activation(high, value(u), ACT.Copy).then_inc(s_hi, 1)

    def vector(v):
        for u, (_, high, low) in enumerate(units):
            v.wait_ge(s_hi, u + 1)
            nc.vector.tensor_tensor(low, value(u), high.bitcast(F32), ALU.subtract).then_inc(s_lo, 1)

    return sync, scalar, vector, s_lo, raw


def mix_out(nc, tag, ph, pl, part, w_parts, x_rows, gate, out_rows, R=2):
    K = ph.shape[1]
    with ExitStack() as ctx:
        wh = ctx.enter_context(nc.sbuf_tensor(f"{tag}_wh", [P, K, D], F32R))
        wl = ctx.enter_context(nc.sbuf_tensor(f"{tag}_wl", [P, K, D], F32R))
        grow = ctx.enter_context(nc.sbuf_tensor(f"{tag}_grow", [P, D], F32))
        acc = ctx.enter_context(nc.psum_tensor(f"{tag}_acc", [P, 4, D], F32))
        s_g = ctx.enter_context(nc.semaphore(f"{tag}_sg"))
        s_x = [ctx.enter_context(nc.semaphore(f"{tag}_sx{r}")) for r in range(2)]
        s_mm, s_t, s_y = (ctx.enter_context(nc.semaphore(f"{tag}_{k}")) for k in ("mm", "st", "sy"))
        s_o = [ctx.enter_context(nc.semaphore(f"{tag}_so{r}")) for r in range(2)]
        units = []
        for k, w in enumerate([w[:, k, :] for w in w_parts for k in range(w.shape[1])]):
            if part is not None:
                units.append((part[:, k, :], ph[:, k, :], pl[:, k, :]))
            units.append((w, wh[:, k, :], wl[:, k, :]))
        split_sync, split_scalar, split_vector, s_lo, xb = split_stream(nc, ctx, f"{tag}s", units, D, R)
        with nc.Block() as block:
            @block.sync
            def _(sp):
                split_sync(sp)
                sp.dma_start(grow[:, :], gate.partition_broadcast(P)).then_inc(s_g, 16)
                sp.wait_ge(s_lo, len(units))
                for t in range(T):
                    if t >= 2:
                        sp.wait_ge(s_o[t % 2], 16 * (t // 2))
                    sp.dma_start(xb[t % 2][:, :], x_rows(t)).then_inc(s_x[t % 2], 16)

            @block.tensor
            def _(pe):
                for tp in range(T // 2):
                    if tp >= 2:
                        pe.wait_ge(s_y, 2 * (tp - 1))
                    for k in range(K):
                        if tp == 0:
                            pe.wait_ge(s_lo, len(units) // K * (k + 1))
                        for t in (2 * tp, 2 * tp + 1):
                            x_h, x_l = ph[:, k, t * P:(t + 1) * P], pl[:, k, t * P:(t + 1) * P]
                            for c in range(2):
                                o, cs = acc[:, t % 4, c * 512:(c + 1) * 512], slice(c * 512, (c + 1) * 512)
                                nc.tensor.matmul(o, x_h, wh[:, k, cs], start=(k == 0), stop=False)
                                nc.tensor.matmul(o, x_h, wl[:, k, cs], start=False, stop=False)
                                last = nc.tensor.matmul(o, x_l, wh[:, k, cs], start=False, stop=(k == K - 1))
                    last.then_inc(s_mm, 1)

            @block.vector
            def _(v):
                split_vector(v)
                v.wait_ge(s_g, 16)
                for t in range(T):
                    v.wait_ge(s_mm, t // 2 + 1)
                    nc.vector.tensor_tensor(acc[:, t % 4, :], acc[:, t % 4, :], grow[:, :], ALU.mult).then_inc(s_t, 1)
                    v.wait_ge(s_t, t + 1)
                    v.wait_ge(s_x[t % 2], 16 * (t // 2 + 1))
                    nc.vector.tensor_tensor(xb[t % 2][:, :], acc[:, t % 4, :], xb[t % 2][:, :], ALU.add).then_inc(s_y, 1)

            @block.scalar
            def _(act):
                split_scalar(act)
                for t in range(T):
                    act.wait_ge(s_y, t + 1)
                    act.dma_start(out_rows(t), xb[t % 2][:, :]).then_inc(s_o[t % 2], 16)
                for r in range(2):
                    act.wait_ge(s_o[r], 16 * len(range(r, T, 2)))


def mixer1_phase(nc, x, ctx_in, mod, norm1, w_in, conv_w, conv_b, dt_bias, a_log, d_skip, ssd_norm, w_four, w_out,
                 dft, rot, second_mod, x1_out):
    x_t, c_t, out_t = (a.rearrange("(t p) d -> t p d", p=P) for a in (x, ctx_in, x1_out))
    w_v = w_in.rearrange("(p j) n -> p j n", j=J)
    F0 = D + D + 2 * G * NS + 2 * H
    z_dram = nc.dram_tensor("x1_zd", (SEQ, D), F32, kind="Internal").ap().rearrange("(t p) d -> t p d", p=P)
    y_dram = nc.dram_tensor("x1_yd", (SEQ, D), F32, kind="Internal").ap().rearrange("(t p) d -> t p d", p=P)
    f_dram = nc.dram_tensor("x1_fd", (P, G, SEQ), F32, kind="Internal").ap()

    with ExitStack() as top:
        ident = top.enter_context(nc.sbuf_tensor("x1_ident", [P, P], F32))
        with ExitStack() as mid:
            def sb(name, shape):
                return mid.enter_context(nc.sbuf_tensor(f"x1_{name}", shape, F32))

            masks = tuple(sb(n, [P, P]) for n in ("mLE", "mGT", "mGE", "mLT", "mONE"))
            make_masks(nc, "x1m", [(ident, ALU.is_equal, 1), (masks[0], ALU.is_ge, 1), (masks[1], ALU.is_gt, -1),
                                   (masks[2], ALU.is_ge, -1), (masks[3], ALU.is_gt, 1), (masks[4], ALU.is_ge, 0)])
            xs_tok, b_tok = sb("xs_tok", [P, TT, D]), sb("b_tok", [P, TT, G * NS])
            bT, cT = sb("bT", [P, G, SEQ]), sb("cT", [P, G, SEQ])
            dt, da, ecum, eend, etot = (sb(n, [P, TT, 2 * H]) for n in ("dt", "da", "ecum", "eend", "etot"))
            cwb = sb("cwb", [P, (CW + 1) * 16])
            with ExitStack() as c2:
                xnT = c2.enter_context(nc.sbuf_tensor("x1_xnT", [P, J, TT * P], F32))
                norm_transpose(nc, "x1n", lambda t: x_t[t] if t < T else c_t[t - T],
                               [(T, norm1, mod[0, D:2 * D], mod[0, 0:D]), (NC, norm1, mod[1, D:2 * D], mod[1, 0:D])],
                               ident, xnT)
                transpose_rows(nc, "x1c", [conv_w.rearrange("k (m p) -> (k m) p", p=P), conv_b.rearrange("(m p) -> m p", p=P)],
                               (CW + 1) * 16, ident, cwb[:, :])
                with ExitStack() as c3:
                    ring = xs_tok[:, 0:8, :].rearrange("p (r a) (b c) -> p r (a b) c", r=2, c=512)
                    before, after = mod_beside(nc, c3, *second_mod, masks[4], ring,
                                               lambda n: (bT if n < 8 else cT)[:, n % 8 // 2, n % 2 * 512:(n % 2 + 1) * 512])
                    project_rows(nc, "x1z", xnT, [w_v[:, :, 0:512], w_v[:, :, 512:1024]], ACT.Silu,
                                 lambda n, t: z_dram[t][:, n * 512:(n + 1) * 512], first=before, then=after)
                with ExitStack() as c3:
                    fb = c3.enter_context(nc.sbuf_tensor("x1_fb", [P, G, SEQ], F32))
                    before, after = ssd_decays(nc, c3, xnT, w_v, dt_bias, a_log, masks, dt, ecum, eend, etot, da)
                    project_channels(nc, "x1f", xnT, J, [w_v[:, :, F0:F0 + 512]], ACT.Copy, None,
                                     lambda m, h: fb[:, m, h * 512:(h + 1) * 512], first=before, then=after)
                    store(nc, "x1fs", fb[:, :, :], f_dram)
                ssd_inputs(nc, xnT, w_v, cwb, ident, xs_tok, b_tok, bT, cT)
            y = sb("y", [P, T, D])
            ssd_scan(nc, masks, xs_tok, b_tok, bT, cT, dt, da, ecum, eend, etot, d_skip, y)
            gate_rows(nc, "x1g", y, lambda t: z_dram[t], lambda t: y_dram[t])
        ph, pl = (top.enter_context(nc.sbuf_tensor(f"x1_{n}", [P, J + G, SEQ], F32R)) for n in ("ph", "pl"))
        norm_transpose(nc, "x1y", lambda t: y_dram[t], [(T, ssd_norm, None, None)], ident, ph[:, 0:J, :], pl[:, 0:J, :])
        fourier(nc, f_dram, ph[:, J:, :], pl[:, J:, :], w_four, dft, rot)
        mix_out(nc, "x1o", ph, pl, None, [w_out[0:D, :].rearrange("(p j) n -> p j n", j=J),
                                          w_out[D:D + G * P, :].rearrange("(g p) n -> p g n", p=P)],
                lambda t: x_t[t], mod[0, 2 * D:3 * D], lambda t: out_t[t])


def store(nc, tag, src, dst):
    with nc.semaphore(f"{tag}_s") as s_st:
        with nc.Block() as block:
            @block.sync
            def _(sp):
                sp.dma_start(dst, src).then_inc(s_st, 16)
                sp.wait_ge(s_st, 16)


def dft_tables():
    import numpy as np
    c = np.arange(P)
    a = 2 * np.pi * np.outer(c, c) / P
    scale = 1.0 / np.sqrt(SEQ * P)
    dft = np.stack([np.cos(a), np.sin(a)], 1) * scale
    k = (np.arange(T)[:, None] + T * np.arange(P)[None, :])
    b = 2 * np.pi * np.mod(c[:, None, None] * k, SEQ) / SEQ
    rot = np.stack([np.cos(b), -np.sin(b)], 1)
    return dft.astype(np.float32), rot.astype(np.float32)


SG, SN, SC = 32, 64, 16
NQ = SG // 2
TC = P // SC
W2 = SG * SC
M2 = W2 // P
SH, SHD = 8, 64
LN_EPS = 1e-5
TWO_PI = 6.283185307179586
CW1 = 6.28125
CW2 = 0.0019350051879882812
CW3 = TWO_PI - CW1 - CW2
ROUND = 1.5 * 2.0 ** 23
PI_IN = 3.1415925


def s5_coefficients(nc, ctx, a_re, a_im, b_re, b_im, c_re, c_im, log_step, ident, pw, phase8, rho8, wre, wim, cre, cim,
                    spare, spare_q):
    def sb(name, shape):
        return ctx.enter_context(nc.sbuf_tensor(f"sc_{name}", shape, F32))

    def sem(name):
        return ctx.enter_context(nc.semaphore(f"sc_{name}"))

    rows = sb("rows", [NQ, 3, P])
    ls = sb("ls", [NQ, 2])
    w1, w2 = (spare[:, 2 * k:2 * k + 2, :].rearrange("p a (b c d) -> p (a b) c d", c=TC, d=SC) for k in range(2))
    crow = spare[0:SC, 4:8, :].rearrange("p (k a) (b c) -> p k (a b) c", k=2, c=P)
    bb, fb = (spare_q[:, 4 * k:4 * k + 4, :].rearrange("p (a b) (c h) -> p a (b c) h", a=2, h=SC) for k in range(2))
    par = sb("par", [P, 3, NQ])
    names = ("lr", "dtv", "m", "th", "k", "r", "ra", "sn", "cs", "den", "nr", "t1", "t2", "fr", "fi")
    v_ = {n: sb(n, [P, NQ]) for n in names}
    rev = spare_q[:, 8:10, :].rearrange("p a (d q) -> p a d q", q=NQ)
    p_p = ctx.enter_context(nc.psum_tensor("sc_p", [P, 3, NQ], F32))
    p_c = [ctx.enter_context(nc.psum_tensor(f"sc_c{k}", [P, NQ, SC], F32)) for k in range(2)]
    s_in, s_c, s_b, s_ls, s_t, s_v, s_a, s_x = (sem(k) for k in ("in", "c", "b", "ls", "t", "v", "a", "x"))
    def sync(sp):
        sp.dma_start(ls[:, :], log_step.rearrange("(q r) -> q r", r=2)).then_inc(s_in, 16)
        sp.dma_start(rows[:, 0, :], a_re.rearrange("(q r) n -> q (r n)", r=2)).then_inc(s_in, 16)
        sp.dma_start(rows[:, 1, :], a_im.rearrange("(q r) n -> q (r n)", r=2)).then_inc(s_in, 16)
        for k, b in enumerate((b_re, b_im)):
            for r in range(2):
                sp.dma_start(bb[r * SN:(r + 1) * SN, k, :, :], b.rearrange("(q r) n h -> r n q h", r=2)[r]).then_inc(s_b, 16)

        for k, c in enumerate((c_re, c_im)):
            for r in range(2):
                sp.dma_start(crow[:, k, :, r * SN:(r + 1) * SN], c.rearrange("(q r) h n -> r h q n", r=2)[r]).then_inc(s_c, 16)

    def tensor(pe):
        pe.wait_ge(s_ls, 1)
        for k in range(3):
            last = nc.tensor.transpose(p_p[:, k, :], rows[:, k, :], ident[0:NQ, 0:NQ])
        last.then_inc(s_t, 1)

    def c_transposes(pe):
        pe.wait_ge(s_c, 64)
        for k in range(2):
            for q in range(NQ):
                last = nc.tensor.transpose(p_c[k][:, q, :], crow[:, k, q, :], ident[0:SC, 0:SC])
        last.then_inc(s_t, 1)

    def scalar(act):
        act.wait_ge(s_x, 1)
        nc.scalar.activation(v_["dtv"][:, :], par[:, 2, :], ACT.Exp).then_inc(s_a, 1)
        act.wait_ge(s_x, 2)
        nc.scalar.activation(v_["m"][:, :], v_["m"][:, :], ACT.Exp).then_inc(s_a, 1)
        act.wait_ge(s_x, 3)
        nc.scalar.activation(v_["sn"][:, :], v_["r"][:, :], ACT.Sin).then_inc(s_a, 1)
        nc.scalar.activation(v_["cs"][:, :], v_["ra"][:, :], ACT.Sin).then_inc(s_a, 1)

    def vector(v):
        link = Chain(v, s_v)

        def tt(o, a, b, op):
            link(nc.vector.tensor_tensor(o, a, b, op))

        def ts(o, a, c1, op1, c2=None, op2=None):
            link(nc.vector.tensor_scalar(o, a, c1, c2, op1, op2) if op2 else nc.vector.tensor_scalar(o, a, c1, None, op1))

        def stt(o, a, c, b, op0, op1):
            link(nc.vector.scalar_tensor_tensor(out=o, in0=a, scalar=c, in1=b, op0=op0, op1=op1))

        def g(n):
            return v_[n][:, :]

        v.wait_ge(s_in, 48)
        nc.vector.tensor_copy(rows[:, 2, :].rearrange("q (r n) -> q r n", r=2), bc(ls[:, :], SN, 2)).then_inc(s_ls, 1)
        for t_ in (wre, wim):
            link(nc.vector.memset(t_[:, :, TC:, :], 0.0))
        for t_ in (cre, cim):
            link(nc.vector.memset(t_[:, :, :, :], 0.0))
        v.wait_ge(s_t, 1)
        nc.vector.tensor_copy(par[:, :, :], p_p[:, :, :]).then_inc(s_x, 1)
        v.wait_ge(s_x, 1)
        ts(g("lr"), par[:, 0, :], -1e-4, ALU.min)
        li = par[:, 1, :]
        v.wait_ge(s_a, 1)
        nc.vector.tensor_tensor(g("m"), g("lr"), g("dtv"), ALU.mult).then_inc(s_x, 1)
        tt(g("th"), li, g("dtv"), ALU.mult)
        ts(g("k"), g("th"), 1.0 / TWO_PI, ALU.mult)
        ts(g("k"), g("k"), ROUND, ALU.add)
        ts(g("k"), g("k"), -ROUND, ALU.add)
        stt(g("r"), g("k"), -CW1, g("th"), ALU.mult, ALU.add)
        stt(g("r"), g("k"), -CW2, g("r"), ALU.mult, ALU.add)
        stt(g("r"), g("k"), -CW3, g("r"), ALU.mult, ALU.add)
        ts(g("r"), g("r"), PI_IN, ALU.min, -PI_IN, ALU.max)
        stt(g("ra"), g("r"), -1.0, g("r"), ALU.mult, ALU.max)
        nc.vector.tensor_scalar(g("ra"), g("ra"), -1.0, 0.5 * 3.141592653589793, ALU.mult, ALU.add).then_inc(s_x, 1)
        v.wait_ge(s_a, 4)
        P_re, P_im = pw[0], pw[1]
        link(nc.vector.memset(P_re[:, 0, :], 1.0))
        link(nc.vector.memset(P_im[:, 0, :], 0.0))
        tt(P_re[:, 1, :], g("m"), g("cs"), ALU.mult)
        tt(P_im[:, 1, :], g("m"), g("sn"), ALU.mult)

        def cmul(o_re, o_im, ar, ai, br, bi, t1, t2, t3):
            tt(t1, ar, br, ALU.mult)
            tt(t2, ai, bi, ALU.mult)
            tt(t3, ar, bi, ALU.mult)
            tt(t1, t1, t2, ALU.subtract)
            tt(t2, ai, br, ALU.mult)
            link(nc.vector.tensor_copy(o_re, t1))
            tt(o_im, t3, t2, ALU.add)

        for d in range(2, TC + 1):
            cmul(P_re[:, d, :], P_im[:, d, :], P_re[:, d - 1, :], P_im[:, d - 1, :], P_re[:, 1, :], P_im[:, 1, :],
                 g("t1"), g("t2"), g("k"))
        link(nc.vector.tensor_copy(phase8[0], g("cs")))
        link(nc.vector.tensor_copy(phase8[1], g("sn")))
        link(nc.vector.tensor_copy(rho8, g("m")))
        for _ in range(3):
            cmul(phase8[0], phase8[1], phase8[0], phase8[1], phase8[0], phase8[1], g("t1"), g("t2"), g("k"))
            tt(rho8, rho8, rho8, ALU.mult)
        tt(g("den"), g("lr"), g("lr"), ALU.mult)
        tt(g("t1"), li, li, ALU.mult)
        tt(g("den"), g("den"), g("t1"), ALU.add)
        link(nc.vector.reciprocal(g("den"), g("den")))
        ts(g("nr"), P_re[:, 1, :], -1.0, ALU.add)
        tt(g("t1"), g("nr"), g("lr"), ALU.mult)
        tt(g("t2"), P_im[:, 1, :], li, ALU.mult)
        tt(g("fr"), g("t1"), g("t2"), ALU.add)
        tt(g("fr"), g("fr"), g("den"), ALU.mult)
        tt(g("t1"), P_im[:, 1, :], g("lr"), ALU.mult)
        tt(g("t2"), g("nr"), li, ALU.mult)
        tt(g("fi"), g("t1"), g("t2"), ALU.subtract)
        tt(g("fi"), g("fi"), g("den"), ALU.mult)
        v.wait_ge(s_b, 64)
        fr, fi = bc(g("fr"), SC, 2), bc(g("fi"), SC, 2)
        cmul(fb[:, 0, :, :], fb[:, 1, :, :], fr, fi, bb[:, 0, :, :], bb[:, 1, :, :],
             w1[:, :, 0, :], w2[:, :, 0, :], w1[:, :, 1, :])
        for j in range(TC):
            for k in range(2):
                link(nc.vector.tensor_copy(rev[:, k, j, :], pw[k][:, TC - 1 - j, :]))
        ar, ai = (bc(rev[:, k, :, :].rearrange("p d q -> p q d"), SC, 3) for k in range(2))
        br, bi = (bc(fb[:, k, :, :], TC, 2) for k in range(2))
        tt(w1[:, :, :, :], ar, br, ALU.mult)
        tt(w2[:, :, :, :], ai, bi, ALU.mult)
        tt(wre[:, :, 0:TC, :], w1[:, :, :, :], w2[:, :, :, :], ALU.subtract)
        tt(w1[:, :, :, :], ar, bi, ALU.mult)
        tt(w2[:, :, :, :], ai, br, ALU.mult)
        tt(wim[:, :, 0:TC, :], w1[:, :, :, :], w2[:, :, :, :], ALU.add)
        v.wait_ge(s_t, 2)
        for r in range(2):
            h = slice(r * SN, (r + 1) * SN)
            link(nc.vector.tensor_copy(cre[h, :, r, :], p_c[0][h, :, :]))
            link(nc.vector.tensor_scalar(cim[h, :, r, :], p_c[1][h, :, :], -1.0, None, ALU.mult))

    return {"sync": sync, "tensor": tensor, "scalar": scalar, "vector": vector}, {"tensor": c_transposes}


def gate_projection(nc, ctx, tag, xnT, w_gate, b_gate, gates):
    R = 3
    ring = ctx.enter_context(nc.sbuf_tensor(f"{tag}_ring", [P, R, J, P], F32))
    ob = ctx.enter_context(nc.sbuf_tensor(f"{tag}_ob", [P, 2, 512], F32))
    acc = ctx.enter_context(nc.psum_tensor(f"{tag}_acc", [P, 2, 512], F32))
    s_w = [ctx.enter_context(nc.semaphore(f"{tag}_w{r}")) for r in range(R)]
    s_o = [ctx.enter_context(nc.semaphore(f"{tag}_o{r}")) for r in range(2)]
    s_mm, s_ev = (ctx.enter_context(nc.semaphore(f"{tag}_{k}")) for k in ("mm", "ev"))
    NM = D // P

    def sync(sp):
        for m in range(NM):
            if m >= R:
                sp.wait_ge(s_mm, 2 * (m - R + 1))
            sp.dma_start(ring[:, m % R, :, :], w_gate[:, m * P:(m + 1) * P].rearrange("(p j) n -> p j n", j=J)).then_inc(s_w[m % R], 16)

    def tensor(pe, i):
        m, h = i // 2, i % 2
        if h == 0:
            pe.wait_ge(s_w[m % R], 16 * (m // R + 1))
        if i >= 2:
            pe.wait_ge(s_ev, i - 1)
        for j in range(J):
            last = nc.tensor.matmul(acc[:, h, :], ring[:, m % R, j, :], xnT[:, j, h * 512:(h + 1) * 512],
                                    start=(j == 0), stop=(j == J - 1))
        last.then_inc(s_mm, 1)

    def scalar(act, i):
        m, h = i // 2, i % 2
        act.wait_ge(s_mm, i + 1)
        if i >= 2:
            act.wait_ge(s_o[h], 16 * m)
        nc.scalar.activation(ob[:, h, :], acc[:, h, :], ACT.Sigmoid, bias=b_gate[:, m:m + 1]).then_inc(s_ev, 1)
        act.wait_ge(s_ev, i + 1)
        act.dma_start(gates[m][:, h * 512:(h + 1) * 512], ob[:, h, :]).then_inc(s_o[h], 16)
        if i >= 2 * NM - 2:
            act.wait_ge(s_o[h], 16 * NM)

    return sync, tensor, scalar


def s5_states(nc, gate, za, ident, pw, phase8, rho8, wre, wim, cre, cim, uT, mT, hre, him, z_re, z_im, t1, t2, t3):
    with ExitStack() as ctx:
        bt = ctx.enter_context(nc.sbuf_tensor("sx_bt", [P, 2, 2, P], F32))
        ub = ctx.enter_context(nc.sbuf_tensor("sx_ub", [P, 2, 4, TC, SC], F32))
        gate_sync, gate_tensor, gate_scalar = gate_projection(nc, ctx, "fg", *gate)
        p_m = ctx.enter_context(nc.psum_tensor("sx_m", [P, 2, 512], F32))
        p_u = p_m[:, :, :].rearrange("p a (k n) -> p a k n", k=4)
        p_b = ctx.enter_context(nc.psum_tensor("sx_b", [P, 2, 512], F32))
        p_z = ctx.enter_context(nc.psum_tensor("sx_z", [P, 2, 512], F32))
        s_u, s_ue, s_m, s_me, s_b, s_be, s_z, s_ze, s_v = (
            ctx.enter_context(nc.semaphore(f"sx_{k}")) for k in ("u", "ue", "m", "me", "b", "be", "z", "ze", "v"))
        s_ub = ctx.enter_context(nc.semaphore("sx_ub"))
        C = P
        assert NQ == 2 * D // P
        with nc.Block() as block:
            @block.sync
            def _(sp):
                gate_sync(sp)

            @block.gpsimd
            def _(pool):
                for i in range(SG // 4):
                    if i >= 2:
                        pool.wait_ge(s_u, i - 1)
                    nc.gpsimd.tensor_copy(ub[:, i % 2, :, :, :], za[:, :, 4 * i * SC:4 * (i + 1) * SC].rearrange(
                        "p t (g h) -> p g t h", g=4)).then_inc(s_ub, 1)

            @block.tensor
            def _(pe):
                for i in range(SG // 4):
                    if i >= 2:
                        pe.wait_ge(s_ue, i - 1)
                    for k in range(4):
                        if k == 0:
                            pe.wait_ge(s_ub, i + 1)
                        last = nc.tensor.transpose(p_u[:, i % 2, k, :], ub[:, i % 2, k, :, :], ident[:, :])
                    last.then_inc(s_u, 1)
                for q in range(NQ + 1):
                    if q < NQ:
                        if q >= 2:
                            pe.wait_ge(s_be, q - 1)
                        nc.tensor.transpose(p_b[:, q % 2, 0:P], wre[:, q, 0:TC, :], ident[:, :])
                        nc.tensor.transpose(p_b[:, q % 2, P:2 * P], wim[:, q, 0:TC, :], ident[:, :]).then_inc(s_b, 1)
                    if q >= 1:
                        u = q - 1
                        pe.wait_ge(s_be, u + 1)
                        pe.wait_ge(s_ue, u // 2 + 1)
                        if u >= 2:
                            pe.wait_ge(s_ze, u - 1)
                        for k in range(2):
                            for r in range(2):
                                last = nc.tensor.matmul(p_z[r * SN:(r + 1) * SN, u % 2, k * C:(k + 1) * C],
                                                        bt[:, u % 2, k, r * SN:(r + 1) * SN], uT[:, 2 * u + r, :],
                                                        start=True, stop=True)
                        last.then_inc(s_z, 1)
                pe.wait_ge(s_ue, SG // 4)
                for q in range(NQ):
                    if q >= 2:
                        pe.wait_ge(s_me, q - 1)
                    for t in range(TC):
                        o = p_m[:, q % 2, t * 2 * SC:(t + 1) * 2 * SC]
                        nc.tensor.matmul(o, wre[:, q, TC - 1 - t:2 * TC - 1 - t, :], cre[:, q, :, :], start=True, stop=False)
                        last = nc.tensor.matmul(o, wim[:, q, TC - 1 - t:2 * TC - 1 - t, :], cim[:, q, :, :], start=False, stop=True)
                    last.then_inc(s_m, 1)
                    gate_tensor(pe, q)

            @block.scalar
            def _(act):
                for i in range(SG // 4):
                    act.wait_ge(s_u, i + 1)
                    nc.scalar.activation(uT[:, 4 * i:4 * i + 4, :], p_u[:, i % 2, :, :], ACT.Copy).then_inc(s_ue, 1)
                for q in range(NQ + 1):
                    if q < NQ:
                        act.wait_ge(s_b, q + 1)
                        if q >= 2:
                            act.wait_ge(s_z, q - 1)
                        nc.scalar.activation(bt[:, q % 2, :, :].rearrange("p k n -> p (k n)"), p_b[:, q % 2, 0:2 * P], ACT.Copy).then_inc(s_be, 1)
                    if q >= 1:
                        u = q - 1
                        act.wait_ge(s_z, u + 1)
                        nc.scalar.activation(z_re[:, u, :], p_z[:, u % 2, 0:C], ACT.Copy)
                        nc.scalar.activation(z_im[:, u, :], p_z[:, u % 2, C:2 * C], ACT.Copy).then_inc(s_ze, 1)
                for q in range(NQ):
                    act.wait_ge(s_m, q + 1)
                    nc.scalar.activation(mT[:, 2 * q:2 * q + 2, :, :].rearrange("p r t h -> p t r h"),
                                         p_m[:, q % 2, 0:2 * P].rearrange("p (t r h) -> p t r h", t=TC, r=2),
                                         ACT.Copy).then_inc(s_me, 1)
                    gate_scalar(act, q)

            @block.vector
            def _(v):
                link = Chain(v, s_v)

                def tt(o, a, b, op):
                    link(nc.vector.tensor_tensor(o, a, b, op))

                cs, sn = hre, him
                link(nc.vector.memset(cs[:, :, 0:1], 1.0))
                link(nc.vector.memset(sn[:, :, 0:1], 0.0))
                link(nc.vector.tensor_copy(cs[:, :, 1], phase8[0]))
                link(nc.vector.tensor_copy(sn[:, :, 1], phase8[1]))
                n = 1
                while n < C // 2:
                    c_, s_ = cs[:, :, n], sn[:, :, n]
                    tt(t1[:, :, 0], c_, c_, ALU.mult)
                    tt(t2[:, :, 0], s_, s_, ALU.mult)
                    tt(t3[:, :, 0], c_, s_, ALU.mult)
                    tt(cs[:, :, 2 * n], t1[:, :, 0], t2[:, :, 0], ALU.subtract)
                    link(nc.vector.tensor_scalar(sn[:, :, 2 * n], t3[:, :, 0], 2.0, None, ALU.mult))
                    m = 2 * n
                    a_c, a_s = bc(cs[:, :, m], m - 1, 2), bc(sn[:, :, m], m - 1, 2)
                    b_c, b_s = cs[:, :, 1:m], sn[:, :, 1:m]
                    tt(t1[:, :, 1:m], a_c, b_c, ALU.mult)
                    tt(t2[:, :, 1:m], a_s, b_s, ALU.mult)
                    tt(cs[:, :, m + 1:2 * m], t1[:, :, 1:m], t2[:, :, 1:m], ALU.subtract)
                    tt(t1[:, :, 1:m], a_c, b_s, ALU.mult)
                    tt(t2[:, :, 1:m], a_s, b_c, ALU.mult)
                    tt(sn[:, :, m + 1:2 * m], t1[:, :, 1:m], t2[:, :, 1:m], ALU.add)
                    n = m
                v.wait_ge(s_ze, NQ)
                tt(t1, z_re, cs, ALU.mult)
                tt(t2, z_im, sn, ALU.mult)
                tt(t1, t1, t2, ALU.add)
                tt(t2, z_im, cs, ALU.mult)
                tt(t3, z_re, sn, ALU.mult)
                tt(t2, t2, t3, ALU.subtract)
                link(nc.vector.tensor_copy(t3, bc(rho8, C, 2)))
                link(nc.vector.memset(t3[:, :, 0:1], 0.0))

                def flat(a):
                    return a.rearrange("p q c -> p (q c)")

                link(nc.vector.tensor_tensor_scan(flat(z_re), flat(t3), flat(t1), 0.0, ALU.mult, ALU.add))
                link(nc.vector.tensor_tensor_scan(flat(z_im), flat(t3), flat(t2), 0.0, ALU.mult, ALU.add))
                tt(t1, z_re, cs, ALU.mult)
                tt(t2, z_im, sn, ALU.mult)
                tt(t3, z_re, sn, ALU.mult)
                tt(z_im, z_im, cs, ALU.mult)
                link(nc.vector.memset(hre[:, :, 0:1], 0.0))
                link(nc.vector.memset(him[:, :, 0:1], 0.0))
                tt(hre[:, :, 1:], t1[:, :, 0:C - 1], t2[:, :, 0:C - 1], ALU.subtract)
                tt(him[:, :, 1:], t3[:, :, 0:C - 1], z_im[:, :, 0:C - 1], ALU.add)


def s5_outputs(nc, gate, za, ident, d_skip, pw, cre, cim, uT, mT, hre, him, yT):
    with ExitStack() as ctx:
        gate_sync, gate_tensor, gate_scalar = gate_projection(nc, ctx, "lg", *gate)
        dsk = ctx.enter_context(nc.sbuf_tensor("so_dsk", [P, W2], F32))
        ot = ctx.enter_context(nc.sbuf_tensor("so_ot", [P, 2, 2, 2, TC, SC], F32))
        t1 = ctx.enter_context(nc.sbuf_tensor("so_t1", [P, 2, TC, SC], F32))
        t2 = ctx.enter_context(nc.sbuf_tensor("so_t2", [P, 2, TC, SC], F32))
        p_y = ctx.enter_context(nc.psum_tensor("so_y", [P, 2, 512], F32))
        p_t = ctx.enter_context(nc.psum_tensor("so_t", [P, 2, M2, P], F32))
        s_in, s_v, s_ot, s_y, s_ye, s_g, s_t, s_te = (
            ctx.enter_context(nc.semaphore(f"so_{k}")) for k in ("in", "v", "ot", "y", "ye", "g", "t", "te"))
        with nc.Block() as block:
            @block.sync
            def _(sp):
                sp.dma_start(dsk[:, :], d_skip.rearrange("g h -> (g h)").partition_broadcast(P)).then_inc(s_in, 16)
                gate_sync(sp)

            @block.tensor
            def _(pe):
                for q in range(NQ):
                    pe.wait_ge(s_ot, q + 1)
                    if q >= 2:
                        pe.wait_ge(s_ye, q - 1)
                    o = p_y[:, q % 2, 0:2 * P]
                    nc.tensor.matmul(o, hre[:, q, :], ot[:, q % 2, 0, :, :, :], start=True, stop=False, skip_group_check=True)
                    nc.tensor.matmul(o, him[:, q, :], ot[:, q % 2, 1, :, :, :], start=False, stop=False, skip_group_check=True)
                    for r in range(2):
                        last = nc.tensor.matmul(p_y[:, q % 2, r * P:(r + 1) * P], uT[:, 2 * q + r, :], mT[:, 2 * q + r, :, :],
                                                start=False, stop=(r == 1), skip_group_check=True)
                    last.then_inc(s_y, 1)
                    gate_tensor(pe, q)
                for t in range(TC):
                    pe.wait_ge(s_g, t + 1)
                    if t >= 2:
                        pe.wait_ge(s_te, t - 1)
                    for m in range(M2):
                        last = nc.tensor.transpose(p_t[:, t % 2, m, :], za[:, t, m * P:(m + 1) * P], ident[:, :])
                    last.then_inc(s_t, 1)

            @block.vector
            def _(v):
                link = Chain(v, s_v)
                v.wait_ge(s_in, 16)
                link(nc.vector.tensor_tensor(za[:, :, :], za[:, :, :], bc(dsk[:, :], TC, 1), ALU.mult))

                def coefficients(q):
                    if q >= 2:
                        v.wait_ge(s_y, q - 1)
                    ar, ai = (bc(bc(pw[k][:, 1:, q], 2, 1), SC, 3) for k in range(2))
                    cr, ci = (bc(c[:, q, :, :], TC, 2) for c in (cre, cim))
                    o = ot[:, q % 2]
                    link(nc.vector.tensor_tensor(t1[:, :, :, :], ar, cr, ALU.mult))
                    link(nc.vector.tensor_tensor(t2[:, :, :, :], ai, ci, ALU.mult))
                    link(nc.vector.tensor_tensor(o[:, 0], t1[:, :, :, :], t2[:, :, :, :], ALU.add))
                    link(nc.vector.tensor_tensor(t1[:, :, :, :], ar, ci, ALU.mult))
                    link(nc.vector.tensor_tensor(t2[:, :, :, :], ai, cr, ALU.mult))
                    nc.vector.tensor_tensor(o[:, 1], t1[:, :, :, :], t2[:, :, :, :], ALU.subtract).then_inc(s_ot, 1)
                    v.wait_ge(s_ot, q + 1)

                for q in range(NQ + 1):
                    if q < NQ:
                        coefficients(q)
                    if q >= 1:
                        u = q - 1
                        v.wait_ge(s_y, u + 1)
                        z = za[:, :, u * 2 * SC:(u + 1) * 2 * SC].rearrange("p t (r h) -> p r t h", r=2)
                        nc.vector.tensor_tensor(z, p_y[:, u % 2, 0:2 * P].rearrange("p (r t h) -> p r t h", r=2, t=TC), z,
                                                ALU.add).then_inc(s_ye, 1)
                for t in range(TC):
                    v.wait_ge(s_t, t + 1)
                    nc.vector.tensor_copy(yT[:, :, t * P:(t + 1) * P], p_t[:, t % 2, :, :]).then_inc(s_te, 1)

            @block.scalar
            def _(act):
                for q in range(NQ):
                    gate_scalar(act, q)
                act.wait_ge(s_ye, NQ)
                for t in range(TC):
                    nc.scalar.activation(za[:, t, :], za[:, t, :], ACT.Gelu_apprx_tanh).then_inc(s_g, 1)


def glu_close(nc, yT, sg, yaT, ya_dram):
    with nc.semaphore("gc_s") as s_m, nc.semaphore("gc_o") as s_o:
        with nc.Block() as block:
            @block.vector
            def _(v):
                for m in range(M2):
                    nc.vector.tensor_tensor(yaT[:, m, :].rearrange("p (c t) -> p t c", t=TC),
                                            yT[:, m, :].rearrange("p (t c) -> p t c", t=TC),
                                            sg[:, m, :].rearrange("p (t c) -> p t c", t=TC), ALU.mult).then_inc(s_m, 1)

            @block.sync
            def _(sp):
                for m in range(M2):
                    sp.wait_ge(s_m, m + 1)
                    sp.dma_start(ya_dram[:, m, :], yaT[:, m, :]).then_inc(s_o, 16)
                sp.wait_ge(s_o, 16 * M2)


def spatial_gating(nc, ctx, u_rows, v_rows, ln_g, ln_b, w_s, b_s, ident, tril, yb_dram, spare, ybT, spare_w):
    def sb(name, shape):
        return ctx.enter_context(nc.sbuf_tensor(f"sg_{name}", shape, F32))

    def sem(name):
        return ctx.enter_context(nc.semaphore(f"sg_{name}"))

    u, vv = spare[:, 0:M2, :].rearrange("p a (b c) -> p (a b) c", c=W2), spare[:, M2:2 * M2, :].rearrange("p a (b c) -> p (a b) c", c=W2)
    lg, lb = sb("lg", [P, W2]), sb("lb", [P, W2])
    ws, wsT = spare_w[:, 0], spare_w[:, 1]
    br, bs = sb("br", [SH, P]), sb("bs", [P, SH])
    st, ag = sb("st", [P, T, 6]), sb("ag", [P, T, 2])
    sd = sb("sd", [P, T])
    p_w = ctx.enter_context(nc.psum_tensor("sg_w", [P, SH, P], F32))
    p_x = ctx.enter_context(nc.psum_tensor("sg_x", [P, 2, T, SHD], F32))
    p_t = ctx.enter_context(nc.psum_tensor("sg_t", [P, 2, M2, P], F32))
    p_b = p_t[:, 0, 0, :]
    s_u, s_w, s_b, s_l = sem("iu"), sem("iw"), sem("ib"), sem("il")
    s_st = sem("st")
    s_vt = [sem(f"v{t}") for t in range(T)]
    s_v, s_wm, s_wt, s_ag, s_sd, s_ln, s_x, s_y, s_t, s_te, s_wc = (
        sem(k) for k in ("v", "wm", "wt", "ag", "sd", "ln", "x", "y", "t", "te", "wc"))
    def sync(sp):
        sp.dma_start(ws[:, :, :], w_s.rearrange("h t s -> t h s")).then_inc(s_w, 16)
        sp.dma_start(br[:, :], b_s).then_inc(s_b, 16)
        sp.dma_start(lg[:, :], ln_g.partition_broadcast(P)).then_inc(s_l, 16)
        sp.dma_start(lb[:, :], ln_b.partition_broadcast(P)).then_inc(s_l, 16)
        for t in range(T):
            sp.dma_start(vv[:, t, :], v_rows(t)).then_inc(s_vt[t], 16)
        for t in range(T):
            sp.dma_start(u[:, t, :], u_rows(t)).then_inc(s_u, 16)

    def tensor(pe):
        pe.wait_ge(s_b, 16)
        nc.tensor.transpose(p_b[:, 0:SH], br[:, :], ident[0:SH, 0:SH]).then_inc(s_wt, 1)
        pe.wait_ge(s_wm, 1)
        for h in range(SH):
            last = nc.tensor.transpose(p_w[:, h, :], ws[:, h, :], ident[:, :])
        last.then_inc(s_wt, 1)
        pe.wait_ge(s_wc, 2)
        pe.wait_ge(s_ln, T)
        for h in range(SH):
            if h >= 2:
                pe.wait_ge(s_y, h - 1)
            nc.tensor.matmul(p_x[:, h % 2, :, :], wsT[:, h, :], vv[:, :, h * SHD:(h + 1) * SHD],
                             start=True, stop=True).then_inc(s_x, 1)
        pe.wait_ge(s_y, SH)
        for t in range(T):
            if t >= 2:
                pe.wait_ge(s_te, t - 1)
            for m in range(M2):
                last = nc.tensor.transpose(p_t[:, t % 2, m, :], u[:, t, m * P:(m + 1) * P], ident[:, :])
            last.then_inc(s_t, 1)

    def deviation(act):
        act.wait_ge(s_ag, 1)
        nc.scalar.activation(sd[:, :], sd[:, :], ACT.Sqrt).then_inc(s_sd, 1)

    def transposed(act):
        for t in range(T):
            tok = slice(t * P, (t + 1) * P)
            act.wait_ge(s_t, t + 1)
            nc.scalar.activation(ybT[:, :, tok], p_t[:, t % 2, :, :], ACT.Copy).then_inc(s_te, 1)
            act.wait_ge(s_te, t + 1)
            act.dma_start(yb_dram[:, :, tok], ybT[:, :, tok]).then_inc(s_st, 16)
        act.wait_ge(s_st, 16 * T)

    def vector(v):
        link = Chain(v, s_v)
        v.wait_ge(s_w, 16)
        nc.vector.tensor_tensor(ws[:, :, :], ws[:, :, :], bc(tril[:, :], SH, 1), ALU.mult).then_inc(s_wm, 1)
        for t in range(T):
            v.wait_ge(s_vt[t], 16)
            link(nc.vector.bn_stats(st[:, t, :], vv[:, t, :]))
            last = nc.vector.bn_aggr(ag[:, t, :], st[:, t, :])
        link(last)
        nc.vector.tensor_scalar(sd[:, :], ag[:, :, 1], LN_EPS, None, ALU.add).then_inc(s_ag, 1)
        v.wait_ge(s_wt, 2)
        nc.vector.tensor_copy(bs[:, :], p_b[:, 0:SH]).then_inc(s_wc, 1)
        nc.vector.tensor_copy(wsT[:, :, :], p_w[:, :, :]).then_inc(s_wc, 1)
        v.wait_ge(s_sd, 1)
        link(nc.vector.reciprocal(sd[:, :], sd[:, :]))
        v.wait_ge(s_l, 32)
        for t in range(T):
            link(nc.vector.tensor_scalar(vv[:, t, :], vv[:, t, :], ag[:, t, 0:1], sd[:, t:t + 1], ALU.subtract, ALU.mult))
            link(nc.vector.tensor_tensor(vv[:, t, :], vv[:, t, :], lg[:, :], ALU.mult))
            nc.vector.tensor_tensor(vv[:, t, :], vv[:, t, :], lb[:, :], ALU.add).then_inc(s_ln, 1)
        v.wait_ge(s_u, 16 * T)
        v.wait_ge(s_wc, 2)
        for h in range(SH):
            v.wait_ge(s_x, h + 1)
            z = u[:, :, h * SHD:(h + 1) * SHD]
            nc.vector.scalar_tensor_tensor(out=z, in0=p_x[:, h % 2, :, :], scalar=bs[:, h:h + 1], in1=z,
                                           op0=ALU.add, op1=ALU.mult).then_inc(s_y, 1)

    return ({"sync": sync, "scalar": deviation},
            {"tensor": tensor, "scalar": transposed, "vector": vector})


def merge(nc, ya_dram, yb_dram, gates, w_a, w_b, m_dram):
    with ExitStack() as ctx:
        wh, wl = (ctx.enter_context(nc.sbuf_tensor(f"mg_w{n}", [P, 2, 2, M2, 512], F32R)) for n in "hl")
        yh, yl = (ctx.enter_context(nc.sbuf_tensor(f"mg_y{n}", [P, 2, M2, SEQ], F32R)) for n in "hl")
        gs = ctx.enter_context(nc.sbuf_tensor("mg_gs", [P, 4, 2, 512], F32))
        acc = ctx.enter_context(nc.psum_tensor("mg_acc", [P, 4, 2, 512], F32))
        s_g = [ctx.enter_context(nc.semaphore(f"mg_g{r}")) for r in range(4)]
        s_o = [ctx.enter_context(nc.semaphore(f"mg_o{r}")) for r in range(4)]
        s_mm, s_v, s_m = (ctx.enter_context(nc.semaphore(f"mg_{k}")) for k in ("mm", "v", "m"))
        steps = [(m, h) for m in range(D // P) for h in range(2)]
        w_v = [w.rearrange("(m p) n -> p m n", p=P) for w in (w_a, w_b)]
        y_v = (ya_dram, yb_dram)

        def w_unit(n, k):
            return w_v[k][:, :, n * 512:(n + 1) * 512], wh[:, n, k, :, :], wl[:, n, k, :, :]

        def y_unit(k, h):
            tok = slice(h * 512, (h + 1) * 512)
            return y_v[k][:, :, tok], yh[:, k, :, tok], yl[:, k, :, tok]

        units = [w_unit(0, 0), y_unit(0, 0), w_unit(0, 1), y_unit(1, 0), y_unit(0, 1), y_unit(1, 1), w_unit(1, 0), w_unit(1, 1)]
        needed = {(0, 0): 2, (0, 1): 4, (1, 0): 5, (1, 1): 6, (8, 0): 7, (8, 1): 8}
        split_sync, split_scalar, split_vector, s_lo, _ = split_stream(nc, ctx, "mgs", units, M2 * 512, 3)
        with nc.Block() as block:
            @block.sync
            def _(sp):
                split_sync(sp)
                for i, (m, h) in enumerate(steps):
                    if i >= 4:
                        sp.wait_ge(s_o[i % 4], 16 * (i // 4))
                    for k in range(2):
                        sp.dma_start(gs[:, i % 4, k, :], gates[k][m][:, h * 512:(h + 1) * 512]).then_inc(s_g[i % 4], 16)

            @block.tensor
            def _(pe):
                for i, (m, h) in enumerate(steps):
                    n, c, tok = m // 4, slice((m % 4) * P, (m % 4 + 1) * P), slice(h * 512, (h + 1) * 512)
                    if i >= 4:
                        pe.wait_ge(s_m, i - 3)
                    for k in range(2):
                        if (i, k) in needed:
                            pe.wait_ge(s_lo, needed[i, k])
                        o = acc[:, i % 4, k, :]
                        for j in range(M2):
                            nc.tensor.matmul(o, wh[:, n, k, j, c], yh[:, k, j, tok], start=(j == 0), stop=False)
                            nc.tensor.matmul(o, wh[:, n, k, j, c], yl[:, k, j, tok], start=False, stop=False)
                            last = nc.tensor.matmul(o, wl[:, n, k, j, c], yh[:, k, j, tok], start=False, stop=(j == M2 - 1))
                    last.then_inc(s_mm, 1)

            @block.vector
            def _(v):
                split_vector(v)
                link = Chain(v, s_v)
                for i, (m, h) in enumerate(steps):
                    v.wait_ge(s_mm, i + 1)
                    v.wait_ge(s_g[i % 4], 32 * (i // 4 + 1))
                    link(nc.vector.tensor_tensor(gs[:, i % 4, :, :], acc[:, i % 4, :, :], gs[:, i % 4, :, :], ALU.mult))
                    nc.vector.tensor_tensor(gs[:, i % 4, 0, :], gs[:, i % 4, 0, :], gs[:, i % 4, 1, :], ALU.add).then_inc(s_m, 1)

            @block.scalar
            def _(act):
                split_scalar(act)
                for i, (m, h) in enumerate(steps):
                    act.wait_ge(s_m, i + 1)
                    act.dma_start(m_dram[:, m, h * 512:(h + 1) * 512], gs[:, i % 4, 0, :]).then_inc(s_o[i % 4], 16)
                for r in range(4):
                    act.wait_ge(s_o[r], 16 * len(range(r, len(steps), 4)))


def load(nc, tag, dst, src):
    with nc.semaphore(f"{tag}_s") as s_ld:
        with nc.Block() as block:
            @block.sync
            def _(sp):
                sp.dma_start(dst, src).then_inc(s_ld, 16)
                sp.wait_ge(s_ld, 16)


def mixer2_phase(nc, h_in, mod, norm1, w_in, w_gate, b_gate, a_re, a_im, b_re, b_im, c_re, c_im, s_d, log_step,
                 w_glu, b_glu, ln_g, ln_b, sgu_w, sgu_b, w_a, w_b, w_out, h_out):
    h_t, out_t = (a.rearrange("(t p) d -> t p d", p=P) for a in (h_in, h_out))
    w_v = w_in.rearrange("(p j) n -> p j n", j=J)
    u_dram = nc.dram_tensor("x2_u", (SEQ, W2), F32, kind="Internal").ap().rearrange("(t p) d -> t p d", p=P)
    v_dram = nc.dram_tensor("x2_v", (SEQ, W2), F32, kind="Internal").ap().rearrange("(t p) d -> t p d", p=P)
    yb_dram = nc.dram_tensor("x2_yb", (P, M2, SEQ), F32, kind="Internal").ap()
    ya_dram = nc.dram_tensor("x2_ya", (P, M2, SEQ), F32, kind="Internal").ap()
    m_dram = nc.dram_tensor("x2_m", (P, D // P, SEQ), F32, kind="Internal").ap()
    gates = nc.dram_tensor("x2_gates", (2, D // P, P, SEQ), F32, kind="Internal").ap()
    za_dram = nc.dram_tensor("x2_za", (P, TC, W2), F32, kind="Internal").ap()

    with ExitStack() as top:
        def sb(name, shape, to=top):
            return to.enter_context(nc.sbuf_tensor(f"x2_{name}", shape, F32))

        ident, tril = sb("ident", [P, P]), sb("tril", [P, P])
        make_masks(nc, "x2m", [(ident, ALU.is_equal, 1), (tril, ALU.is_ge, -1)])
        bcol = sb("bcol", [P, 2 * D // P + M2])
        transpose_rows(nc, "x2c", [b_gate.rearrange("(m p) -> m p", p=P), b_glu.rearrange("(m p) -> m p", p=P)],
                       2 * D // P + M2, ident, bcol[:, :])
        with ExitStack() as mid:
            mT = sb("mT", [P, D // P, SEQ], mid)
            xnT = sb("xnT", [P, J, SEQ], mid)
            norm_transpose(nc, "x2n", lambda t: h_t[t], [(T, norm1, mod[D:2 * D], mod[0:D])], ident, xnT)
            yaT = sb("yaT", [P, M2, SEQ], mid)
            with ExitStack() as s5:
                pw = [sb(f"pw{k}", [P, TC + 1, NQ], s5) for k in range(2)]
                ph = sb("ph", [P, 3, NQ], s5)
                phase8, rho8 = (ph[:, 0, :], ph[:, 1, :]), ph[:, 2, :]
                cre, cim = (sb(f"c{k}", [P, NQ, 2, SC], s5) for k in ("re", "im"))
                uT, msT = sb("uT", [P, SG, P], s5), sb("msT", [P, SG, TC, SC], s5)
                hre, him = (sb(f"h{k}", [P, NQ, P], s5) for k in ("re", "im"))
                response = s5.enter_context(ExitStack())
                wre, wim = (sb(f"w{k}", [P, NQ, 2 * TC - 1, SC], response) for k in ("re", "im"))
                with ExitStack() as st:
                    before, after = s5_coefficients(nc, st, a_re, a_im, b_re, b_im, c_re, c_im, log_step, ident, pw, phase8,
                                                   rho8, wre, wim, cre, cim, mT, hre)
                    project_rows(nc, "x2v", xnT, [w_v[:, :, W2:2 * W2], w_v[:, :, 2 * W2:3 * W2]], ACT.Gelu_apprx_tanh,
                                 lambda n, t: (u_dram, v_dram)[n][t], first=before, then=after)
                with ExitStack() as st:
                    before, after = spatial_gating(nc, st, lambda t: u_dram[t], lambda t: v_dram[t], ln_g, ln_b, sgu_w, sgu_b,
                                                   ident, tril, yb_dram, mT, uT[:, :, :].rearrange("p (m a) c -> p m (a c)", m=M2),
                                                   msT[:, 0:SG // 2, :, :].rearrange("p (k h a) t s -> p k h (a t s)", k=2, h=SH))
                    project_rows(nc, "x2a", None, [w_v[:, :, 0:W2]], ACT.Copy, lambda n, t: za_dram[:, t, :],
                                 lhs=lambda j, t: xnT[:, j, t::TC], RP=2, first=before, then=after)
                with ExitStack() as st:
                    bufs = [mT[:, 2 * k:2 * k + 2, :].rearrange("p a (b c) -> p (a b) c", c=P) for k in range(3)]
                    z_re = mT[:, 6:8, :].rearrange("p a (b c) -> p (a b) c", c=P)
                    z_im = yaT[:, 0:2, :].rearrange("p a (b c) -> p (a b) c", c=P)
                    za1 = sb("za1", [P, TC, W2], st)
                    load(nc, "x2l1", za1[:, :, :], za_dram)
                    s5_states(nc, (xnT, w_gate[:, 0:D], bcol[:, 0:D // P], gates[0]), za1, ident, pw, phase8, rho8, wre, wim, cre, cim, uT, msT,
                              hre[:, :, :], him[:, :, :], z_re, z_im, *bufs)
                response.close()
                with ExitStack() as st:
                    za2, yT = sb("za2", [P, TC, W2], st), sb("yT", [P, M2, SEQ], st)
                    load(nc, "x2l2", za2[:, :, :], za_dram)
                    s5_outputs(nc, (xnT, w_gate[:, D:2 * D], bcol[:, D // P:2 * D // P], gates[1]),
                               za2, ident, s_d, pw, cre, cim, uT, msT, hre, him, yT)
                    sg = mT[:, 0:M2, :]
                    project_channels(nc, "x2g", yT, M2, [w_glu.rearrange("(m p) n -> p m n", p=P)], ACT.Sigmoid,
                                     bcol[:, 2 * D // P:], lambda m, h: sg[:, m, h * 512:(h + 1) * 512])
                    glu_close(nc, yT, sg, yaT, ya_dram)
        merge(nc, ya_dram, yb_dram, gates, w_a, w_b, m_dram)
        ph, pl = (top.enter_context(nc.sbuf_tensor(f"x2_m{n}", [P, D // P, SEQ], F32R)) for n in ("h", "l"))
        mix_out(nc, "x2o", ph, pl, m_dram, [w_out.rearrange("(m p) n -> p m n", p=P)], lambda t: h_t[t], mod[2 * D:3 * D],
                lambda t: out_t[t], R=4)


def free_semaphores(nc):
    used = list(nc.released_uncleared_semaphores)
    with nc.Block() as block:
        @block.gpsimd
        def _(pool):
            pool.sem_clear(range(min(used), max(used) + 1))


def two_blocks(nc, i, out):
    with ExitStack() as ctx:
        pool_dma = [ctx.enter_context(nc.semaphore(f"pool_dma{k}")) for k in range(2 * POOL_DMA_SEMAPHORES)]
        run_blocks(nc, i, out, pool_dma)


def run_blocks(nc, i, out, pool_dma):
    mod1 = nc.dram_tensor("mod1", (2, 6 * D), F32, kind="Internal").ap()
    mod2 = nc.dram_tensor("mod2", (1, 6 * D), F32, kind="Internal").ap()
    stage = [nc.dram_tensor(f"stage{k}", (SEQ, D), F32, kind="Internal").ap() for k in range(3)]
    mod_phase(nc, [([i["c"][0], i["c_ctx"]], i["w_mod"][0], i["b_mod"][0], mod1)])
    mixer1_phase(nc, i["x"][0], i["ctx"][0], mod1, *(i[n][0] for n in (
        "norm1", "w_in", "conv_w", "conv_b", "dt_bias", "a_log", "d_skip", "ssd_norm", "w_four", "w_out")),
        i["dft"], i["rot"], (i["c_2"][0], i["w_ada_2"][0], i["b_ada_2"][0], mod2), stage[0])
    free_semaphores(nc)
    moe_phase(nc, "m1", stage[0], mod1[0], *(i[n][0] for n in (
        "norm2", "w_rg", "b_rg", "w_re", "b_re", "w_eg", "w_eu", "w_ed")), i["final_norm"], stage[1], pool_dma[:POOL_DMA_SEMAPHORES])
    free_semaphores(nc)
    mixer2_phase(nc, stage[1], mod2[0], *(i[n + "_2"][0] for n in (
        "norm1_g", "w_in", "w_gate", "b_gate", "ssm_a_re", "ssm_a_im", "ssm_b_re", "ssm_b_im", "ssm_c_re", "ssm_c_im",
        "ssm_d", "ssm_log_step", "w_glu", "b_glu", "sgu_ln_g", "sgu_ln_b", "sgu_w", "sgu_b", "w_branch_a", "w_branch_b",
        "w_out")), stage[2])
    free_semaphores(nc)
    moe_phase(nc, "m2", stage[2], mod2[0], *(i[n + "_2"][0] for n in (
        "norm2_g", "w_router_group", "b_router_group", "w_router_expert", "b_router_expert", "w1", "w3", "w2")),
        i["norm_f_g_2"], out[0], pool_dma[POOL_DMA_SEMAPHORES:])


def kernel(**inputs):
    import numpy as _np
    import concourse.bacc as _bacc
    from concourse import mybir as _mybir
    from concourse.bass_utils import run_bass_kernel_spmd as _run

    nc = _bacc.Bacc("TRN2", target_bir_lowering=False, num_devices=1)
    arrays, args = {}, {}
    dft, rot = dft_tables()
    for name, a in list(inputs.items()) + [("dft", dft), ("rot", rot)]:
        a = _np.ascontiguousarray(a)
        arrays[f"in_{name}_dram"] = a
        args[name] = nc.dram_tensor(f"in_{name}_dram", a.shape, _mybir.dt.from_np(a.dtype), kind="ExternalInput").ap()
    out = nc.dram_tensor("out_0_dram", (1, SEQ, D), F32, kind="ExternalOutput").ap()
    two_blocks(nc, args, out)
    r = _run(nc, [arrays], core_ids=[0])
    return r.results[0]["out_0_dram"]
```
